# Optimizing a Trainium2 kernel written in Bass

```python
import jax, jax.numpy as jnp
from jax import lax
import numpy as np
import math

D_MODEL = 1024
BATCH = 1
SEQ = 256
DEPTH = 2

HEAD_DIM = 64
ROPE_THETA = 10000.0

RET_HEADS = 4
RET_DK = 64
RET_DV = 64
RET_CHUNK = 128

SWA_Q_HEADS = 6
SWA_KV_HEADS = 2
SWA_WINDOW = 128
SWA_BLOCK = 128

MLA_HEADS = 6
MLA_Q_RANK = 384
MLA_KV_RANK = 256
MLA_NOPE = 64
MLA_ROPE = 32
MLA_V = 64
MLA_BLOCK = 128

RET_W = RET_HEADS * RET_DV
SWA_W = SWA_Q_HEADS * HEAD_DIM
MLA_W = MLA_HEADS * MLA_V
D_MIX = RET_W + SWA_W + MLA_W

IN_SIZES = (
    RET_HEADS * RET_DK,
    RET_HEADS * RET_DK,
    RET_W,
    RET_W,
    SWA_Q_HEADS * HEAD_DIM,
    SWA_KV_HEADS * HEAD_DIM,
    SWA_KV_HEADS * HEAD_DIM,
    MLA_Q_RANK,
    MLA_KV_RANK,
    MLA_ROPE,
)
IN_COLS = sum(IN_SIZES)

N_EXPERTS = 16
N_GROUPS = 4
EXPERTS_PER_GROUP = N_EXPERTS // N_GROUPS
TOP_K = 2
D_EXPERT = 256

DEEPNORM_ALPHA = (2 * DEPTH) ** 0.25
DEEPNORM_BETA = (8 * DEPTH) ** -0.25
LN_EPS = 1e-5
RMS_EPS = 1e-6
NEG_INF = -1e30


def _split_points():
    return [int(s) for s in np.cumsum(np.array(IN_SIZES))[:-1]]

def layer_norm(x, g, b):
    xf = x.astype(jnp.float32)
    mu = jnp.mean(xf, -1, keepdims=True)
    var = jnp.mean(jnp.square(xf - mu), -1, keepdims=True)
    return ((xf - mu) * lax.rsqrt(var + LN_EPS) * g + b).astype(x.dtype)

def rms_norm(x, g):
    xf = x.astype(jnp.float32)
    return (xf * lax.rsqrt(jnp.mean(xf * xf, -1, keepdims=True) + RMS_EPS) * g).astype(x.dtype)

def rope(x, pos):
    d = x.shape[-1]
    inv = ROPE_THETA ** (-jnp.arange(0, d, 2, dtype=jnp.float32) / d)
    ang = pos.astype(jnp.float32)[:, None] * inv[None, :]
    cos = jnp.cos(ang)[:, None, :]
    sin = jnp.sin(ang)[:, None, :]
    x1, x2 = x[..., : d // 2], x[..., d // 2:]
    return jnp.concatenate([x1 * cos - x2 * sin, x1 * sin + x2 * cos], -1).astype(x.dtype)

def retention(q, k, v, g, gn_w):
    B, S, H, dk = q.shape
    dv = RET_DV
    C = RET_CHUNK
    NC = S // C
    gamma = 1.0 - 2.0 ** (-5.0 - jnp.arange(H, dtype=jnp.float32))
    log_g = jnp.log(gamma)
    idx = jnp.arange(C, dtype=jnp.float32)
    rel = idx[:, None] - idx[None, :]
    decay_in = jnp.where(rel[None] >= 0,
                         jnp.exp(jnp.maximum(rel, 0.0)[None] * log_g[:, None, None]), 0.0)
    xi = jnp.exp((idx[None, :] + 1.0) * log_g[:, None]).T
    zeta = jnp.exp((C - 1.0 - idx[None, :]) * log_g[:, None]).T
    chunk_decay = jnp.exp(C * log_g)

    qc = q.reshape(B, NC, C, H, dk).astype(jnp.float32)
    kc = (k * (dk ** -0.5)).reshape(B, NC, C, H, dk).astype(jnp.float32)
    vc = v.reshape(B, NC, C, H, dv).astype(jnp.float32)

    scores = jnp.einsum('bnihd,bnjhd->bnhij', qc, kc) * decay_in[None, None]
    inner = jnp.einsum('bnhij,bnjhe->bnihe', scores, vc)

    upd = jnp.einsum('bnjhd,bnjhe->bnhde', kc * zeta[None, None, :, :, None], vc)

    def step(state, u):
        return chunk_decay[None, :, None, None] * state + u, state

    init = jnp.zeros((B, H, dk, dv), jnp.float32)
    _, prev_states = lax.scan(step, init, jnp.moveaxis(upd, 1, 0))
    prev_states = jnp.moveaxis(prev_states, 0, 1)
    cross = jnp.einsum('bnihd,bnhde->bnihe', qc * xi[None, None, :, :, None], prev_states)

    o = (inner + cross).reshape(B, S, H, dv)
    mu = jnp.mean(o, -1, keepdims=True)
    var = jnp.mean(jnp.square(o - mu), -1, keepdims=True)
    o = (o - mu) * lax.rsqrt(var + LN_EPS) * gn_w.astype(jnp.float32).reshape(H, dv)
    o = o.reshape(B, S, H * dv) * jax.nn.silu(g.astype(jnp.float32))
    return o.astype(q.dtype)

def sliding_window_sink_attention(q, k, v, sinks):
    B, S, Hq, d = q.shape
    Hkv = k.shape[2]
    G = Hq // Hkv
    L = SWA_BLOCK
    NB = S // L
    qb = q.reshape(B, NB, L, Hkv, G, d)
    kb = k.reshape(B, NB, L, Hkv, d)
    vb = v.reshape(B, NB, L, Hkv, d)
    pad = ((0, 0), (1, 0), (0, 0), (0, 0), (0, 0))
    kwin = jnp.concatenate([jnp.pad(kb, pad)[:, :NB], kb], axis=2)
    vwin = jnp.concatenate([jnp.pad(vb, pad)[:, :NB], vb], axis=2)

    s = jnp.einsum('bnihgd,bnjhd->bnhgij', qb, kwin).astype(jnp.float32) * (d ** -0.5)
    i = jnp.arange(L)[:, None]
    j = jnp.arange(2 * L)[None, :]
    band = (j <= i + L) & (j > i + L - SWA_WINDOW)
    blk = jnp.arange(NB)[:, None]
    valid = (blk > 0) | (jnp.arange(2 * L)[None, :] >= L)
    mask = band[None] & valid[:, None, :]
    s = jnp.where(mask[None, :, None, None], s, NEG_INF)

    sink = sinks.astype(jnp.float32).reshape(1, 1, Hkv, G, 1, 1)
    m = jnp.maximum(jnp.max(s, -1, keepdims=True), sink)
    p = jnp.exp(s - m)
    denom = jnp.sum(p, -1, keepdims=True) + jnp.exp(sink - m)
    o = jnp.einsum('bnhgij,bnjhd->bnihgd', (p / denom).astype(v.dtype), vwin)
    return o.reshape(B, S, Hq * d)

def latent_attention(c_q, c_kv, k_rope, q_norm_w, kv_norm_w, w_uq, w_ukv, pos):
    B, S, _ = c_q.shape
    H = MLA_HEADS
    dq = MLA_NOPE + MLA_ROPE
    q = (rms_norm(c_q, q_norm_w) @ w_uq).reshape(B, S, H, dq)
    q = jnp.concatenate([q[..., :MLA_NOPE], rope(q[..., MLA_NOPE:], pos)], -1)
    kv = (rms_norm(c_kv, kv_norm_w) @ w_ukv).reshape(B, S, H, MLA_NOPE + MLA_V)
    k_nope, v = kv[..., :MLA_NOPE], kv[..., MLA_NOPE:]
    k_pe = rope(k_rope[:, :, None, :], pos)
    k = jnp.concatenate([k_nope, jnp.broadcast_to(k_pe, (B, S, H, MLA_ROPE))], -1)
    scale = dq ** -0.5
    L = MLA_BLOCK
    NB = S // L
    qb = jnp.moveaxis(q.reshape(B, NB, L, H, dq), 1, 0)
    kpos = jnp.arange(S)

    def block(args):
        q_blk, n = args
        s = jnp.einsum('bihd,bjhd->bhij', q_blk, k).astype(jnp.float32) * scale
        qpos = n * L + jnp.arange(L)
        s = jnp.where(kpos[None, :] <= qpos[:, None], s, NEG_INF)
        p = jax.nn.softmax(s, axis=-1)
        return jnp.einsum('bhij,bjhe->bihe', p.astype(v.dtype), v)

    o = lax.map(block, (qb, jnp.arange(NB)))
    return jnp.moveaxis(o, 0, 1).reshape(B, S, H * MLA_V)

def grouped_moe(x, router_w, router_bias, w_gate_up, w_down):
    B, S, D = x.shape
    t = x.reshape(-1, D)
    T = t.shape[0]
    scores = jax.nn.sigmoid((t @ router_w).astype(jnp.float32))
    biased = scores + router_bias.astype(jnp.float32)
    grp = biased.reshape(T, N_GROUPS, EXPERTS_PER_GROUP)
    grp_score = jnp.sum(lax.top_k(grp, TOP_K)[0], -1)
    sel_group = jnp.argmax(grp_score, -1)
    in_group = jnp.repeat(jax.nn.one_hot(sel_group, N_GROUPS) > 0, EXPERTS_PER_GROUP, axis=-1)
    _, top_idx = lax.top_k(jnp.where(in_group, biased, -jnp.inf), TOP_K)
    sel = jnp.take_along_axis(scores, top_idx, -1)
    weights = sel / jnp.sum(sel, -1, keepdims=True)
    gates = jnp.sum(jax.nn.one_hot(top_idx, N_EXPERTS, dtype=jnp.float32) * weights[..., None], 1)
    h = jnp.einsum('td,edf->tef', t, w_gate_up)
    a = jax.nn.silu(h[..., :D_EXPERT]) * h[..., D_EXPERT:] * gates[..., None].astype(h.dtype)
    y = jnp.einsum('tef,efd->td', a, w_down)
    return y.reshape(B, S, D)

def first_inputs(seed: int = 0) -> dict:
    key = jax.random.key(seed)
    ks = jax.random.split(key, 20)
    f32 = jnp.float32
    nrm = lambda k, shape, s: jax.random.normal(k, shape, f32) * s
    return {
        "x": nrm(ks[0], (BATCH, SEQ, D_MODEL), 1.0),
        "w_in": nrm(ks[1], (DEPTH, D_MODEL, IN_COLS), D_MODEL ** -0.5),
        "ret_gn_w": 1.0 + nrm(ks[2], (DEPTH, RET_W), 0.02),
        "swa_sinks": nrm(ks[3], (DEPTH, SWA_Q_HEADS), 0.5),
        "mla_q_norm_w": 1.0 + nrm(ks[4], (DEPTH, MLA_Q_RANK), 0.02),
        "mla_kv_norm_w": 1.0 + nrm(ks[5], (DEPTH, MLA_KV_RANK), 0.02),
        "mla_w_uq": nrm(ks[6], (DEPTH, MLA_Q_RANK, MLA_HEADS * (MLA_NOPE + MLA_ROPE)), MLA_Q_RANK ** -0.5),
        "mla_w_ukv": nrm(ks[7], (DEPTH, MLA_KV_RANK, MLA_HEADS * (MLA_NOPE + MLA_V)), MLA_KV_RANK ** -0.5),
        "w_out": nrm(ks[8], (DEPTH, D_MIX, D_MODEL), DEEPNORM_BETA * D_MIX ** -0.5),
        "ln1_g": 1.0 + nrm(ks[9], (DEPTH, D_MODEL), 0.02),
        "ln1_b": nrm(ks[10], (DEPTH, D_MODEL), 0.02),
        "router_w": nrm(ks[11], (D_MODEL, N_EXPERTS), D_MODEL ** -0.5),
        "router_bias": nrm(ks[12], (N_EXPERTS,), 0.01),
        "exp_w_gate_up": nrm(ks[13], (DEPTH, N_EXPERTS, D_MODEL, 2 * D_EXPERT), D_MODEL ** -0.5),
        "exp_w_down": nrm(ks[14], (DEPTH, N_EXPERTS, D_EXPERT, D_MODEL), DEEPNORM_BETA * D_EXPERT ** -0.5),
        "ln2_g": 1.0 + nrm(ks[15], (DEPTH, D_MODEL), 0.02),
        "ln2_b": nrm(ks[16], (DEPTH, D_MODEL), 0.02),
    }

def first_block(x, w_in, ret_gn_w, swa_sinks, mla_q_norm_w, mla_kv_norm_w, mla_w_uq, mla_w_ukv,
              w_out, ln1_g, ln1_b, router_w, router_bias, exp_w_gate_up, exp_w_down, ln2_g, ln2_b):
    B, S, _ = x.shape
    pos = jnp.arange(S)
    splits = _split_points()
    for l in range(DEPTH):
        (r_q, r_k, r_v, r_g, s_q, s_k, s_v, c_q, c_kv, k_rope) = jnp.split(x @ w_in[l], splits, axis=-1)
        rq = rope(r_q.reshape(B, S, RET_HEADS, RET_DK), pos)
        rk = rope(r_k.reshape(B, S, RET_HEADS, RET_DK), pos)
        ret_o = retention(rq, rk, r_v, r_g, ret_gn_w[l])
        swa_o = sliding_window_sink_attention(
            s_q.reshape(B, S, SWA_Q_HEADS, HEAD_DIM),
            s_k.reshape(B, S, SWA_KV_HEADS, HEAD_DIM),
            s_v.reshape(B, S, SWA_KV_HEADS, HEAD_DIM),
            swa_sinks[l])
        mla_o = latent_attention(c_q, c_kv, k_rope, mla_q_norm_w[l], mla_kv_norm_w[l],
                                 mla_w_uq[l], mla_w_ukv[l], pos)
        mix = jnp.concatenate([ret_o, swa_o, mla_o], axis=-1) @ w_out[l]
        x = layer_norm(DEEPNORM_ALPHA * x + mix, ln1_g[l], ln1_b[l])
        ffn = grouped_moe(x, router_w, router_bias, exp_w_gate_up[l], exp_w_down[l])
        x = layer_norm(DEEPNORM_ALPHA * x + ffn, ln2_g[l], ln2_b[l])
    return x


DEPTH_2 = 1

N_ATTN_HEADS = 8
ATTN_WIDTH = N_ATTN_HEADS * HEAD_DIM
LRU_WIDTH = D_MODEL - ATTN_WIDTH
N_LRU_BLOCKS = 8
LRU_BLOCK = LRU_WIDTH // N_LRU_BLOCKS
MIX_WIDTH = ATTN_WIDTH + LRU_WIDTH
IN_WIDTH = 3 * ATTN_WIDTH + 2 * LRU_WIDTH
CONV_WIDTH = 4
LRU_C = 8.0
D_FF = 4 * D_MODEL
BLOCK_Q = 128
EPS = 1e-6


def rms_norm_2(x, g):
    xf = x.astype(jnp.float32)
    y = xf * lax.rsqrt(jnp.mean(xf * xf, axis=-1, keepdims=True) + EPS)
    return (y * g.astype(jnp.float32)).astype(x.dtype)

def causal_depthwise_conv(u, w, b):
    S = u.shape[1]
    up = jnp.pad(u, ((0, 0), (CONV_WIDTH - 1, 0), (0, 0)))
    out = b
    for k in range(CONV_WIDTH):
        out = out + up[:, k:k + S] * w[k]
    return out

def _linear_rec_combine(left, right):
    a1, b1 = left
    a2, b2 = right
    return a1 * a2, a2 * b1 + b2

def rg_lru(u, w_rg, b_rg, w_ig, b_ig, lam):
    B, S, _ = u.shape
    ub = u.reshape(B, S, N_LRU_BLOCKS, LRU_BLOCK)
    r = jax.nn.sigmoid(jnp.einsum('bsnc,ncd->bsnd', ub, w_rg) + b_rg.reshape(N_LRU_BLOCKS, LRU_BLOCK))
    i = jax.nn.sigmoid(jnp.einsum('bsnc,ncd->bsnd', ub, w_ig) + b_ig.reshape(N_LRU_BLOCKS, LRU_BLOCK))
    r = r.reshape(B, S, LRU_WIDTH).astype(jnp.float32)
    i = i.reshape(B, S, LRU_WIDTH).astype(jnp.float32)
    log_a = -LRU_C * r * jax.nn.softplus(-lam.astype(jnp.float32))
    a = jnp.exp(log_a)
    mult = jnp.sqrt(-jnp.expm1(2.0 * log_a))
    bterm = mult * (i * u.astype(jnp.float32))
    _, h = lax.associative_scan(_linear_rec_combine, (a, bterm), axis=1)
    return h.astype(u.dtype)

def stick_breaking_attention(q, k, v):
    S = q.shape[1]
    scale = 1.0 / math.sqrt(HEAD_DIM)
    qf = q.astype(jnp.float32)
    kf = k.astype(jnp.float32)
    vf = v.astype(jnp.float32)
    outs = []
    for blk in range(S // BLOCK_Q):
        q0 = blk * BLOCK_Q
        end = q0 + BLOCK_Q
        z = jnp.einsum('bqhd,bkhd->bhqk', qf[:, q0:end], kf[:, :end]) * scale
        qpos = q0 + jnp.arange(BLOCK_Q)[:, None]
        kpos = jnp.arange(end)[None, :]
        mask = kpos < qpos
        log_one_minus = jnp.where(mask, jax.nn.log_sigmoid(-z), 0.0)
        suffix = lax.cumsum(log_one_minus, axis=3, reverse=True) - log_one_minus
        log_w = jax.nn.log_sigmoid(z) + suffix
        w = jnp.where(mask, jnp.exp(log_w), 0.0)
        outs.append(jnp.einsum('bhqk,bkhd->bqhd', w, vf[:, :end]))
    return jnp.concatenate(outs, axis=1).astype(v.dtype)

def hybrid_mixer(h, w_in, conv_w, conv_b, w_rg, b_rg, w_ig, b_ig, lam, q_norm_g, k_norm_g, w_out):
    B, S, _ = h.shape
    proj = h @ w_in
    q, k, v, xl, gl = jnp.split(proj, [ATTN_WIDTH, 2 * ATTN_WIDTH, 3 * ATTN_WIDTH, 3 * ATTN_WIDTH + LRU_WIDTH], axis=-1)
    q = rms_norm_2(q.reshape(B, S, N_ATTN_HEADS, HEAD_DIM), q_norm_g)
    k = rms_norm_2(k.reshape(B, S, N_ATTN_HEADS, HEAD_DIM), k_norm_g)
    v = v.reshape(B, S, N_ATTN_HEADS, HEAD_DIM)
    attn = stick_breaking_attention(q, k, v).reshape(B, S, ATTN_WIDTH)
    xl = causal_depthwise_conv(xl, conv_w, conv_b)
    lru = rg_lru(xl, w_rg, b_rg, w_ig, b_ig, lam) * jax.nn.gelu(gl)
    return jnp.concatenate([attn, lru], axis=-1) @ w_out

def sq_relu_mlp(h, w_up, w_down):
    return jnp.square(jax.nn.relu(h @ w_up)) @ w_down

def second_inputs(seed: int = 0) -> dict:
    key = jax.random.key(seed)
    ks = jax.random.split(key, 17)
    f32 = jnp.float32
    nrm = lambda kk, shape, s: jax.random.normal(kk, shape, f32) * s
    a0 = jax.random.uniform(ks[10], (DEPTH_2, LRU_WIDTH), f32, minval=0.9, maxval=0.999)
    return {
        'x': jax.random.normal(ks[0], (BATCH, SEQ, D_MODEL), f32),
        'norm1_g': 1.0 + nrm(ks[1], (DEPTH_2, D_MODEL), 0.02),
        'w_in': nrm(ks[2], (DEPTH_2, D_MODEL, IN_WIDTH), D_MODEL ** -0.5),
        'conv_w': nrm(ks[3], (DEPTH_2, CONV_WIDTH, LRU_WIDTH), CONV_WIDTH ** -0.5),
        'conv_b': nrm(ks[4], (DEPTH_2, LRU_WIDTH), 0.01),
        'w_rg': nrm(ks[5], (DEPTH_2, N_LRU_BLOCKS, LRU_BLOCK, LRU_BLOCK), LRU_BLOCK ** -0.5),
        'b_rg': nrm(ks[6], (DEPTH_2, LRU_WIDTH), 0.01),
        'w_ig': nrm(ks[7], (DEPTH_2, N_LRU_BLOCKS, LRU_BLOCK, LRU_BLOCK), LRU_BLOCK ** -0.5),
        'b_ig': nrm(ks[8], (DEPTH_2, LRU_WIDTH), 0.01),
        'lru_lambda': jnp.log(a0) - jnp.log1p(-a0),
        'q_norm_g': 1.0 + nrm(ks[11], (DEPTH_2, HEAD_DIM), 0.02),
        'k_norm_g': 1.0 + nrm(ks[12], (DEPTH_2, HEAD_DIM), 0.02),
        'w_out': nrm(ks[13], (DEPTH_2, MIX_WIDTH, D_MODEL), MIX_WIDTH ** -0.5),
        'norm2_g': 1.0 + nrm(ks[14], (DEPTH_2, D_MODEL), 0.02),
        'w_up': nrm(ks[15], (DEPTH_2, D_MODEL, D_FF), D_MODEL ** -0.5),
        'w_down': nrm(ks[16], (DEPTH_2, D_FF, D_MODEL), D_FF ** -0.5),
    }

def second_block(x, norm1_g, w_in, conv_w, conv_b, w_rg, b_rg, w_ig, b_ig, lru_lambda, q_norm_g, k_norm_g, w_out, norm2_g, w_up, w_down):
    for l in range(DEPTH_2):
        h = rms_norm_2(x, norm1_g[l])
        x = x + hybrid_mixer(h, w_in[l], conv_w[l], conv_b[l], w_rg[l], b_rg[l], w_ig[l], b_ig[l],
                             lru_lambda[l], q_norm_g[l], k_norm_g[l], w_out[l])
        h = rms_norm_2(x, norm2_g[l])
        x = x + sq_relu_mlp(h, w_up[l], w_down[l])
    return x


def setup_inputs(seed=0):
    out = dict(first_inputs(seed))
    for name, value in second_inputs(seed + 1).items():
        if name != "x":
            out[name + "_2"] = value
    return out


def reference(
    x, w_in, ret_gn_w, swa_sinks, mla_q_norm_w, mla_kv_norm_w, mla_w_uq, mla_w_ukv, w_out,
    ln1_g, ln1_b, router_w, router_bias, exp_w_gate_up, exp_w_down, ln2_g, ln2_b, norm1_g_2,
    w_in_2, conv_w_2, conv_b_2, w_rg_2, b_rg_2, w_ig_2, b_ig_2, lru_lambda_2, q_norm_g_2,
    k_norm_g_2, w_out_2, norm2_g_2, w_up_2, w_down_2,
):
    x = first_block(
        x, w_in, ret_gn_w, swa_sinks, mla_q_norm_w, mla_kv_norm_w, mla_w_uq, mla_w_ukv, w_out,
        ln1_g, ln1_b, router_w, router_bias, exp_w_gate_up, exp_w_down, ln2_g, ln2_b,
    )
    return second_block(
        x, norm1_g_2, w_in_2, conv_w_2, conv_b_2, w_rg_2, b_rg_2, w_ig_2, b_ig_2, lru_lambda_2,
        q_norm_g_2, k_norm_g_2, w_out_2, norm2_g_2, w_up_2, w_down_2,
    )


_drawn_inputs = setup_inputs


def setup_inputs(seed=0):
    import zlib

    import numpy as np

    out = dict(_drawn_inputs(seed))
    spreads = {}
    factors = {'ret_gn_w': 8.0,
     'swa_sinks': 8.0,
     'mla_q_norm_w': 5.343,
     'mla_kv_norm_w': 5.265,
     'norm1_g_2': 4.31,
     'conv_b_2': 6.33,
     'b_rg_2': 38.221,
     'b_ig_2': 32.626,
     'q_norm_g_2': 8.0,
     'k_norm_g_2': 8.0,
     'norm2_g_2': 9.439}
    for name, (base, spread) in spreads.items():
        noise = np.random.default_rng([zlib.crc32(name.encode()), seed]).standard_normal(out[name].shape)
        drawn = base * np.exp(spread * noise) if base else spread * noise
        out[name] = __import__('jax').numpy.asarray(drawn.astype(out[name].dtype))
    for name, factor in factors.items():
        out[name] = (out[name] * factor).astype(out[name].dtype)
    return out
```

```python
from contextlib import ExitStack

import numpy as np

import concourse.bass as bass
from concourse import mybir

P = 128
SEQ, D, NL = 256, 1024, 2
T = SEQ // P
KD = D // P
HD = 64
RET_H, SWA_H, SWA_KV, MLA_H = 4, 6, 2, 6
Q_RANK, KV_RANK, NOPE, ROPE_D, MLA_VD = 384, 256, 64, 32, 64
DQ = NOPE + ROPE_D
N_EXP, N_GRP, D_EXP = 16, 4, 256
PER_GRP = N_EXP // N_GRP
ST_H, CONV, D_FF, LRU_W = 8, 4, 4096, 512
FF_CHUNK = 256
N_CHUNK = D_FF // FF_CHUNK
ALPHA = float((2 * NL) ** 0.25)
LN_EPS, RMS_EPS = 1e-5, 1e-6
NEG = -1e30
LRU_C = 8.0

C_RQ, C_RV, C_SQ, C_SK, C_SV, C_CQ, C_KR = 0, 512, 1024, 1408, 1536, 1664, 2304
N_LAT = Q_RANK + KV_RANK + ROPE_D
N_SWA = C_CQ - C_SQ

F32 = mybir.dt.float32
ALU = mybir.AluOpType
ACT = mybir.ActivationFunctionType
AX = mybir.AxisListType

LAYER_JOBS = [
    ("xT0", 0), ("xT1", 1), ("xT2", 2), ("xT3", 3),
    ("lat0", 4), ("lat1", 5), ("lat2", 6),
    ("ret_q", 7), ("ret_k", 0), ("lat_ssq", 1),
    ("swa_q01", 2), ("swa_q2k", 3), ("ret_vg0", 7), ("ret_vg1", 0), ("swa_v", 2),
    ("ret_q_swap", 1), ("ret_k_swap", 3),
    ("mla_q0", 4), ("mla_q1", 5), ("mla_q2", 6),
    ("mla_k0", 2), ("mla_k1", 7), ("mla_k2", 0), ("mla_v0", 1), ("mla_v1", 3),
    ("mla_q_swap0", 4), ("mla_q_swap1", 5), ("mla_q_swap2", 6), ("mla_kr_swap", 2),
    ("ret_s0", 7), ("ret_s1", 0), ("ret_s2", 1), ("ret_s3", 3),
    ("swa_s1_0", 2), ("swa_s1_1", 4), ("swa_s1_2", 5), ("swa_s0_0", 6), ("swa_s0_1", 7),
    ("ret_o", 0),
    ("mla_s1_0", 1), ("mla_s1_1", 3), ("mla_s1_2", 2), ("mla_s0_0", 4), ("mla_s0_1", 5),
    ("swa_pT0", 6), ("swa_pT1", 7), ("swa_pT2", 6), ("swa_pT3", 7), ("swa_pT4", 6), ("swa_pT5", 7),
    ("ret_oT", 0), ("swa_o0", 4), ("swa_o1", 5),
    ("mla_pT0", 1), ("mla_pT1", 3), ("mla_pT2", 2), ("mla_pT3", 1), ("mla_pT4", 3), ("mla_pT5", 2),
    ("mla_o0", 6), ("mla_o1", 7),
    ("mix0", 0), ("mix1", 4), ("mix2", 5), ("mix3", 1),
    ("x1T0", 2), ("x1T1", 3), ("x1T2", 6), ("x1T3", 7),
    ("router", 0), ("gatesT", 1),
    ("y0", 0), ("y1", 1), ("y2", 2), ("y3", 3),
    ("gate0", 4), ("up0", 5), ("gate1", 6), ("up1", 7),
]
FINAL_JOBS = [
    ("n1T0", 0), ("n1T1", 1), ("n1T2", 2), ("n1T3", 3),
    ("q0", 4), ("q1", 5), ("k0", 6), ("k1", 7),
    ("ssq0", 0), ("ssq1", 1), ("v0", 2), ("ssq2", 3), ("v1", 0), ("ssq3", 1),
    ("xl0", 2), ("xl1", 3), ("gl0", 4), ("gl1", 5),
    ("z0", 6), ("z1", 7), ("rg0", 2), ("rg1", 3), ("ig0", 4), ("ig1", 5),
    ("sfx0", 0), ("z2", 6), ("sfx1", 1), ("z3", 7), ("sfx2", 0), ("z4", 6), ("sfx3", 1), ("z5", 7),
    ("sfx4", 0), ("z6", 6), ("sfx5", 1), ("z7", 7), ("sfx6", 0), ("sfx7", 1),
    ("att0", 2), ("att1", 3),
    ("out0", 4), ("out1", 5), ("out2", 6), ("out3", 7),
    ("n2T0", 0), ("n2T1", 1), ("n2T2", 2), ("n2T3", 3),
    ("m0", 0), ("m1", 1), ("m2", 2), ("m3", 3),
    ("ff0", 4), ("ff1", 5),
]
REPEATED = {"gate0": N_EXP // 2, "up0": N_EXP // 2, "gate1": N_EXP // 2, "up1": N_EXP // 2,
            "ff0": N_CHUNK // 2, "ff1": N_CHUNK // 2}


def place_jobs(jobs):
    count, where = [0] * 8, {}
    for name, bank in jobs:
        where[name] = (bank, count[bank])
        count[bank] += REPEATED.get(name, 1)
    return where, count


def tables():
    pos = np.arange(SEQ, dtype=np.float32)
    row = np.arange(P)

    def rope_table(dim, first_row):
        half = dim // 2
        inv = (10000.0 ** (-np.arange(0, dim, 2, dtype=np.float32) / np.float32(dim))).astype(np.float32)
        ang = (pos[None, :] * inv[(row - first_row) % half][:, None]).astype(np.float32)
        sign = np.where((row - first_row) % dim < half, -1.0, 1.0)[:, None]
        return np.cos(ang.astype(np.float64)), np.sin(ang.astype(np.float64)) * sign

    def swap_table(dim):
        swap = np.zeros((P, P))
        swap[row, np.where(row % dim < dim // 2, row + dim // 2, row - dim // 2)] = 1.0
        return swap

    cos_r, sin_r = rope_table(HD, 0)
    cos_m, sin_m = rope_table(ROPE_D, NOPE)
    i, j = row[:, None], row[None, :]
    decay = np.zeros((P, RET_H, 3 * P))
    for h in range(RET_H):
        log_g = np.log(1.0 - 2.0 ** (-5.0 - h))
        for block, shift in ((0, 0), (1, P), (2, 0)):
            rel = (j + shift) - i
            decay[:, h, block * P:(block + 1) * P] = np.where(rel >= 0, np.exp(rel * log_g), 0.0) * HD ** -0.5
    low = (i // HD == j // HD).astype(np.float64)
    tie = np.zeros((PER_GRP, PER_GRP))
    for e in range(PER_GRP):
        tie[e, :e] = 1.0
    return {
        "ident": np.eye(P), "ones": np.ones((P, P)), "half_ones": low,
        "swap_r": swap_table(HD), "swap_m": swap_table(ROPE_D),
        "cos_r": cos_r, "sin_r": sin_r, "cos_m": cos_m, "sin_m": sin_m,
        "decay": decay.reshape(P, -1),
        "mask_swa": np.concatenate([np.where(j > i, 0.0, NEG), np.where(j <= i, 0.0, NEG)], 1),
        "mask_mla": np.concatenate([np.zeros((P, P)), np.where(j <= i, 0.0, NEG)], 1),
        "later": (i > j).astype(np.float64),
        "before": (i < j).astype(np.float64),
        "tie": np.broadcast_to(tie.reshape(1, -1), (P, PER_GRP * PER_GRP)),
        "ln_eps": np.full((P, 1), LN_EPS), "rms_eps": np.full((P, 1), RMS_EPS), "one": np.ones((P, 1)),
    }


TABLE_AT, TABLE_W = {}, 0
for _name, _t in tables().items():
    TABLE_AT[_name] = (TABLE_W, _t.shape[1])
    TABLE_W += _t.shape[1]


class Link:

    def __init__(self, eng, sem, start=0):
        self.eng, self.sem, self.start, self.n = eng, sem, start, 0

    def __call__(self, ins):
        ins.then_inc(self.sem, 1)
        self.n += 1
        self.eng.wait_ge(self.sem, self.start + self.n)


def build(nc, a, out):
    ctx = ExitStack()
    with ctx:
        def sb(name, shape):
            return ctx.enter_context(nc.sbuf_tensor(name, shape, F32))

        def sem(name):
            return ctx.enter_context(nc.semaphore(name))

        tab = sb("tab", [P, TABLE_W])
        X = sb("X", [P, T, D])
        XT = sb("XT", [P, KD, SEQ])
        LNB = sb("LNB", [P, 2, D])
        WA = sb("WA", [P, 9472])
        WE = sb("WE", [P, 12480])
        WB = sb("WB", [P, KD * D])
        AC = sb("AC", [P, 9984])
        small = sb("small", [P, 1400])

        def tb(name):
            o, w = TABLE_AT[name]
            return tab[:, o:o + w]

        class Arena:
            def __init__(self, tensor, at=0):
                self.t, self.at, self.size = tensor, at, tensor[:, :].shape[1]

            def take(self, *shape):
                w = int(np.prod(shape))
                v = self.t[:, self.at:self.at + w]
                self.at += w
                assert self.at <= self.size, (self.at, self.size)
                if len(shape) == 2:
                    v = v.rearrange("p (a b) -> p a b", b=shape[1])
                elif len(shape) == 3:
                    v = v.rearrange("p (a b c) -> p a b c", b=shape[1], c=shape[2])
                return v

        ar = Arena(WA)
        w_lat, w_rqk = ar.take(KD, N_LAT), ar.take(KD, C_RV)
        ar = Arena(WE)
        w_rvg, w_swa = ar.take(KD, 512), ar.take(KD, N_SWA)
        w_uq, w_ukv = ar.take(Q_RANK // P, MLA_H * DQ), ar.take(KV_RANK // P, MLA_H * (NOPE + MLA_VD))
        w_gu, w_dn = [], []
        for s in range(2):
            ar = Arena(WE, s * 6240)
            w_gu.append(ar.take(KD, 2 * D_EXP))
            w_dn.append(ar.take(D_EXP // P, D))
        w_out = Arena(WB).take(KD, D)
        ar = Arena(WA)
        mla_p1, mla_p0, mla_pT = ar.take(MLA_H, SEQ), ar.take(MLA_H, P), ar.take(MLA_H, 3 * P)
        swa_p1, swa_p0, swa_pT = ar.take(SWA_H, SEQ), ar.take(SWA_H, P), ar.take(SWA_H, 3 * P)
        ar = Arena(WB)
        lat_sq, lat_n, lat_rstd = ar.take(5, SEQ), ar.take(5, SEQ), ar.take(2, SEQ)
        rope_m, rope_r, kr_cos = ar.take(MLA_H, SEQ), ar.take(4, SEQ), ar.take(SEQ)
        kr_sin = ar.take(SEQ)
        ar = Arena(WB)
        gates_b = ar.take(N_EXP, SEQ)
        sig = [ar.take(512) for _ in range(2)]
        gat = [ar.take(512) for _ in range(2)]
        hid = [ar.take(2, SEQ) for _ in range(2)]
        gatesT = ar.take(SEQ)
        ar = Arena(AC)
        ret_qT, ret_kT = ar.take(2, SEQ), ar.take(2, SEQ)
        swa_qT, swa_kT = ar.take(3, SEQ), ar.take(SEQ)
        ret_v, ret_g, swa_v = ar.take(T, 256), ar.take(T, 256), ar.take(T, P)
        mla_qT, mla_kT, mla_v = ar.take(MLA_H, SEQ), ar.take(MLA_H, SEQ), ar.take(T, MLA_H * MLA_VD)
        krT, ret_pT = ar.take(SEQ), ar.take(RET_H, 3 * P)
        ret_c, ret_sq = ar.take(T * RET_H, HD), ar.take(T * RET_H, HD)
        ar = Arena(AC)
        st_qT, st_kT, st_v = ar.take(4, SEQ), ar.take(4, SEQ), ar.take(T, 512)
        xl_pad = ar.take(4, SEQ + CONV - 1)
        conv_u, glT, rgT, igT, lruA = (ar.take(4, SEQ) for _ in range(5))
        lruT = Arena(AC, 3 * 1024).take(4, SEQ)
        xn = LNB[:, :, :]
        gel, lruH = LNB[:, 0, :].rearrange("p (a b) -> p a b", b=SEQ), LNB[:, 1, :].rearrange("p (a b) -> p a b", b=SEQ)
        ar = Arena(WB)
        qk_sq, qk_rstd = ar.take(4, 512), ar.take(4, 512)
        ar = Arena(WA)
        w_qk2 = ar.take(KD, 1024)
        ar = Arena(WA)
        stS, stL, stW = ar.take(ST_H, 3 * P), ar.take(ST_H, 3 * P), ar.take(ST_H, 3 * P)
        ar = Arena(WE)
        w_vx2, w_gl2 = ar.take(KD, 1024), ar.take(KD, 512)
        w_bd = sb("w_bd", [P, 2, 4, P])
        ar = Arena(small)
        qn_g, kvn_g, gn_b, sink_b = ar.take(3), ar.take(2), ar.take(256), ar.take(SWA_H)
        router, rbias = ar.take(KD, N_EXP), ar.take(N_EXP)
        mx = {"swa": ar.take(T, 6), "mla": ar.take(T, 6)}
        nmx = {"swa": ar.take(T, 6), "mla": ar.take(T, 6)}
        psm = {"swa": ar.take(T, 6), "mla": ar.take(T, 6)}
        rin = {"swa": ar.take(T, 6), "mla": ar.take(T, 6)}
        sk_e = ar.take(T, 6)
        gmu, gvar, grs = ar.take(8), ar.take(8), ar.take(8)
        st6, mv2, lrs = ar.take(T, 2 * 6), ar.take(T, 2), ar.take(T, 1)
        sc, bi, pr, gs = ar.take(32), ar.take(8, 4), ar.take(8, 6), ar.take(8)
        c1, c2 = ar.take(8, 4, 4), ar.take(8, 4, 4)
        g1, g2 = ar.take(2, 4, 4), ar.take(2, 4, 4)
        gsel, esel, gden, gates = ar.take(8), ar.take(8, 4), ar.take(2), ar.take(2, N_EXP)
        n1g, n2g = ar.take(KD), ar.take(KD)
        qg2, kg2 = ar.take(1), ar.take(1)
        cw, cb = ar.take(CONV, 4), ar.take(4)
        brg, big, lam = ar.take(4), ar.take(4), ar.take(4)
        sp_e, sp_s, sp_s2, sp_p = ar.take(4), ar.take(4), ar.take(4), ar.take(4)
        rss, marks = ar.take(T), ar.take(8 + T + 1)
        ident, ones = tb("ident"), tb("ones")
        decay = tb("decay").rearrange("p (h c) -> p h c", h=RET_H)
        tie = tb("tie").rearrange("p (a b) -> p a b", b=PER_GRP)
        psum = [ctx.enter_context(nc.psum_tensor(f"bank{b}", [P, 512], F32)) for b in range(8)]
        gates_dram = nc.dram_tensor("gates_scratch", [NL, N_EXP, SEQ], F32, kind="Internal").ap()

        psum_full = [sem(f"psum_full{b}") for b in range(8)]
        psum_read = [sem(f"psum_read{b}") for b in range(8)]
        in_layer, per_layer = place_jobs(LAYER_JOBS)
        in_final, _ = place_jobs(FINAL_JOBS)

        def count_of(name, l):
            bank, n = (in_layer if name in in_layer else in_final)[name]
            return bank, l * per_layer[bank] + n

        def free(name, l, m=0):
            bank, n = count_of(name, l)
            return psum_read[bank], n + m + 1

        def full(name, l, m=0):
            bank, n = count_of(name, l)
            return psum_full[bank], n + m + 1

        def read(name, l, m=0):
            bank, n = count_of(name, l)
            return psum_read[bank], n + m + 2

        def bank(name):
            return psum[(in_layer if name in in_layer else in_final)[name][0]]

        def made(name):
            return psum_full[(in_layer if name in in_layer else in_final)[name][0]], 1

        def took(name):
            return psum_read[(in_layer if name in in_layer else in_final)[name][0]], 1

        tab_in, x_in, router_in, final_in, bd_in = (sem(n) for n in ("tab_in", "x_in", "router_in", "final_in", "bd_in"))
        wlat_in, wrqk_in, wrvg_in, wswa_in, wup_in, wout_in = (
            sem(n) for n in ("wlat_in", "wrqk_in", "wrvg_in", "wswa_in", "wup_in", "wout_in"))
        norms_in, ln1_in, ln2_in, gates_in, gates_out = (sem(n) for n in ("norms_in", "ln1_in", "ln2_in", "gates_in", "gates_out"))
        gu_in, dn_in = [sem(f"gu_in{s}") for s in range(2)], [sem(f"dn_in{s}") for s in range(2)]
        x_ready = sem("x_ready")
        lat_squared, kr_copied = sem("lat_squared"), sem("kr_copied")
        rows_turned = sem("rows_turned")
        rstd_ready = sem("rstd_ready")
        ret_cos, ret_roped = sem("ret_cos"), sem("ret_roped")
        ret_gate_w, q_roped, k_roped = sem("ret_gate_w"), sem("q_roped"), sem("k_roped")
        maxed = {n: sem(f"{n}_maxed") for n in ("swa", "mla")}
        expd = {n: sem(f"{n}_expd") for n in ("swa", "mla")}
        normed = {n: sem(f"{n}_normed") for n in ("swa", "mla")}
        gn_squared, gn_var, gn_rstd, ret_out = (sem(n) for n in ("gn_squared", "gn_var", "gn_rstd", "ret_out"))
        ln_var, ln_rstd, x1_ready = sem("ln_var"), sem("ln_rstd"), sem("x1_ready")
        gates_ready, expert_used = sem("gates_ready"), sem("expert_used")
        dve_link, act_link, pool_link = sem("dve_link"), sem("act_link"), sem("pool_link")
        dve_moe, dve_fin, act_fin = sem("dve_moe"), sem("dve_fin"), sem("act_fin")
        wqk_in, wvx_in, wgl_in = sem("wqk_in"), sem("wvx_in"), sem("wgl_in")
        rms_rstd, rms_rows = sem("rms_rstd"), sem("rms_rows")
        qk_squared, qk_rstd_ok = sem("qk_squared"), sem("qk_rstd_ok")
        bd_zero, pad_zero, conv_done = sem("bd_zero"), sem("pad_zero"), sem("conv_done")
        consts2 = sem("consts2")
        log1pd, soft, masked_sp = sem("log1pd"), sem("soft"), sem("masked_sp")
        wexp, w_masked = sem("wexp"), sem("w_masked")
        lru_la, lru_at, lru_m2, lru_sq, gel_in, gel_t, lru_mix, sp_lam = (
            sem(n) for n in ("lru_la", "lru_at", "lru_m2", "lru_sq", "gel_in", "gel_t", "lru_mix", "sp_lam"))
        up_in, down_in = [sem(f"up_in{s}") for s in range(2)], [sem(f"down_in{s}") for s in range(2)]
        ff_used, relu_done, stored = sem("ff_used"), sem("relu_done"), sem("stored")

        def token(t):
            return slice(t * P, (t + 1) * P)

        def spread(ap, axis, shape):
            return ap.unsqueeze(axis).to_broadcast(shape)

        DVE_LINKS, ACT_LINKS, POOL_LINKS, MOE_LINKS = 40, 3, 2, 1

        block = ctx.enter_context(nc.Block())

        @block.sync
        def _(sp):
            sp.dma_start(X[:, :, :], a["x"].rearrange("o (t p) d -> p (o t) d", p=P)).then_inc(x_in, 16)
            with sp.Fori(0, NL) as l:
                w = a["w_in"][bass.ds(l, 1)].rearrange("o (p k) n -> p (o k) n", k=KD)
                sp.dma_start(w_lat, w[:, :, C_CQ:C_CQ + N_LAT]).then_inc(wlat_in, 16)
                sp.dma_start(w_rqk, w[:, :, C_RQ:C_RV]).then_inc(wrqk_in, 16)
                sp.wait_ge(psum_read[3], l * per_layer[3] + 1)
                for m in range(3):
                    for g in range(2):
                        sp.dma_start(w_swa[:, :, m * P + g * HD:m * P + (g + 1) * HD],
                                     w[:, :, C_SQ + (3 * g + m) * HD:C_SQ + (3 * g + m + 1) * HD]).then_inc(wswa_in, 16)
                sp.dma_start(w_swa[:, :, C_SK - C_SQ:N_SWA], w[:, :, C_SK:C_CQ]).then_inc(wswa_in, 16)
                sp.dma_start(w_rvg, w[:, :, C_RV:C_SQ]).then_inc(wrvg_in, 16)
                sp.dma_start(w_uq, a["mla_w_uq"][bass.ds(l, 1)].rearrange("o (c p) n -> p (o c) n", p=P)).then_inc(wup_in, 16)
                sp.dma_start(w_ukv, a["mla_w_ukv"][bass.ds(l, 1)].rearrange("o (c p) n -> p (o c) n", p=P)).then_inc(wup_in, 16)
                sp.wait_ge(k_roped, l + 2)
                sp.dma_start(w_out, a["w_out"][bass.ds(l, 1)].rearrange("o (c p) n -> p (o c) n", p=P)).then_inc(wout_in, 16)

                def load_gate_up(e, s):
                    sp.dma_start(w_gu[s], a["exp_w_gate_up"][bass.ds(l, 1), bass.ds(e, 1)].rearrange(
                        "o e (p k) n -> p (o e k) n", k=KD)).then_inc(gu_in[s], 16)

                def load_down(e, s):
                    sp.dma_start(w_dn[s], a["exp_w_down"][bass.ds(l, 1), bass.ds(e, 1)].rearrange(
                        "o e (c p) n -> p (o e c) n", p=P)).then_inc(dn_in[s], 16)

                for s in range(2):
                    load_gate_up(s, s)
                    load_down(s, s)
                sp.wait_ge(x1_ready, (l + 1) * T)
                sp.dma_start(LNB[:, 0, :], a["ln2_g"][bass.ds(l, 1)].rearrange("o n -> (o n)").partition_broadcast(P)).then_inc(ln2_in, 16)
                sp.dma_start(LNB[:, 1, :], a["ln2_b"][bass.ds(l, 1)].rearrange("o n -> (o n)").partition_broadcast(P)).then_inc(ln2_in, 16)
                with sp.Fori(1, N_EXP // 2) as m:
                    for s in range(2):
                        sp.wait_ge(*full(f"up{s}", l, m - 1))
                        load_gate_up(2 * m + s, s)
                        sp.wait_ge(expert_used, l * (N_EXP - 1) + 2 * m + (s - 1))
                        load_down(2 * m + s, s)
            w2 = a["w_in_2"][0].rearrange("(p k) n -> p k n", k=KD)
            sp.dma_start(w_qk2, w2[:, :, 0:1024]).then_inc(wqk_in, 16)
            sp.wait_ge(psum_read[3], NL * per_layer[3] + 1)
            sp.dma_start(w_vx2, w2[:, :, 1024:2048]).then_inc(wvx_in, 16)
            sp.dma_start(w_gl2, w2[:, :, 2048:2560]).then_inc(wgl_in, 16)
            for n in ("q0", "q1", "k0", "k1"):
                sp.wait_ge(*read(n, NL))
            sp.dma_start(w_out, a["w_out_2"][0].rearrange("(c p) n -> p c n", p=P)).then_inc(wout_in, 16)
            sp.wait_ge(*full("gl1", NL))

            def load_up(c, s):
                sp.dma_start(w_gu[s][:, :, 0:FF_CHUNK], a["w_up_2"][0].rearrange("(p k) n -> p k n", k=KD)[
                    :, :, bass.ds(c * FF_CHUNK, FF_CHUNK)]).then_inc(up_in[s], 16)

            def load_ff_down(c, s):
                sp.dma_start(w_dn[s], a["w_down_2"][0].rearrange("(g c p) n -> g p c n", c=2, p=P)[
                    bass.ds(c, 1)].rearrange("g p c n -> p (g c) n")).then_inc(down_in[s], 16)

            for s in range(2):
                load_up(s, s)
                load_ff_down(s, s)
            with sp.Fori(1, N_CHUNK // 2) as m:
                for s in range(2):
                    sp.wait_ge(*full(f"ff{s}", NL, m - 1))
                    load_up(2 * m + s, s)
                    sp.wait_ge(ff_used, 2 * m + (s - 1))
                    load_ff_down(2 * m + s, s)
            o = out.rearrange("o (t p) d -> p (o t) d", p=P)
            for t in range(T):
                sp.wait_ge(*read(f"m{2 * t}", NL))
                sp.wait_ge(*read(f"m{2 * t + 1}", NL))
                sp.dma_start(o[:, t, :], X[:, t, :]).then_inc(stored, 16)
            sp.wait_ge(stored, 16 * T)

        @block.gpsimd
        def _(pool):
            pool.dma_start(tab[:, :], a["tables"]).then_inc(tab_in, 16)
            with nc.allow_non_contiguous_dma(reason="small vectors"):
                pool.dma_start(router, a["router_w"].rearrange("(p k) e -> p k e", k=KD)).then_inc(router_in, 16)
                pool.dma_start(rbias, a["router_bias"].partition_broadcast(P)).then_inc(router_in, 16)
            pool.wait_ge(tab_in, 16)
            nc.gpsimd.memset(marks[:, 8 + T:9 + T], 0.0).then_inc(k_roped, 1)
            with pool.Fori(0, NL) as l:
                link = Link(pool, pool_link, l * POOL_LINKS)
                with nc.allow_non_contiguous_dma(reason="small vectors"):
                    pool.wait_ge(x_ready, (l + 1) * T)
                    pool.dma_start(qn_g, a["mla_q_norm_w"][bass.ds(l, 1)].rearrange("o (c p) -> p (o c)", p=P)).then_inc(norms_in, 16)
                    pool.dma_start(kvn_g, a["mla_kv_norm_w"][bass.ds(l, 1)].rearrange("o (c p) -> p (o c)", p=P)).then_inc(norms_in, 16)
                    pool.dma_start(gn_b, a["ret_gn_w"][bass.ds(l, 1)].rearrange("o n -> (o n)").partition_broadcast(P)).then_inc(norms_in, 16)
                    pool.dma_start(sink_b, a["swa_sinks"][bass.ds(l, 1)].rearrange("o n -> (o n)").partition_broadcast(P)).then_inc(norms_in, 16)
                pool.dma_start(LNB[:, 0, :], a["ln1_g"][bass.ds(l, 1)].rearrange("o n -> (o n)").partition_broadcast(P)).then_inc(ln1_in, 16)
                pool.dma_start(LNB[:, 1, :], a["ln1_b"][bass.ds(l, 1)].rearrange("o n -> (o n)").partition_broadcast(P)).then_inc(ln1_in, 16)
                pool.wait_ge(k_roped, l + 1)
                for n, (src, name) in enumerate(((ret_qT, "ret_q"), (ret_kT, "ret_k"))):
                    pool.wait_ge(*read(name, l))
                    nc.gpsimd.tensor_tensor(rope_r[:, 2 * n:2 * n + 2, :], src, spread(tb("cos_r"), 1, [P, 2, SEQ]),
                                            ALU.mult).then_inc(ret_cos, 1)
                pool.wait_ge(norms_in, (l + 1) * 64)
                for t in range(T):
                    pool.wait_ge(*read(f"ret_vg{t}", l))
                nc.gpsimd.tensor_tensor(ret_g, ret_g, spread(gn_b, 1, [P, T, 256]), ALU.mult).then_inc(ret_gate_w, 1)
                rows = slice(NOPE, DQ)
                cos, shape = tb("cos_m")[rows], [ROPE_D, MLA_H, SEQ]
                pool.wait_ge(ret_gate_w, l + 1)
                for n in range(3):
                    pool.wait_ge(*full(f"mla_q_swap{n}", l))
                link(nc.gpsimd.tensor_tensor(mla_qT[rows], mla_qT[rows], spread(cos, 1, shape), ALU.mult))
                for n in range(3):
                    pool.wait_ge(*read(f"mla_q_swap{n}", l))
                nc.gpsimd.tensor_tensor(mla_qT[rows], mla_qT[rows], rope_m[rows], ALU.add).then_inc(q_roped, 1)
                link(nc.gpsimd.tensor_tensor(kr_cos[rows], krT[rows], cos, ALU.mult))
                pool.wait_ge(*read("mla_kr_swap", l))
                nc.gpsimd.tensor_tensor(mla_kT[rows], spread(kr_cos[rows], 1, shape), spread(kr_sin[rows], 1, shape),
                                        ALU.add).then_inc(k_roped, 1)
                assert link.n == POOL_LINKS
            pool.wait_ge(k_roped, NL + 1)
            nc.gpsimd.memset(w_bd[:, :, :, :], 0.0).then_inc(bd_zero, 1)
            pool.wait_ge(bd_zero, 1)
            with nc.allow_non_contiguous_dma(reason="small vectors"):
                for n, name in enumerate(("w_rg_2", "w_ig_2")):
                    for half in range(2):
                        pool.dma_start(w_bd[half * HD:(half + 1) * HD, n, :, half * HD:(half + 1) * HD],
                                       a[name][0].rearrange("(c h) i o -> h i c o", h=2)[half]).then_inc(bd_in, 16)
                n_final = 0
                for dst, src in (
                    (n1g, a["norm1_g_2"].rearrange("o (p k) -> p (o k)", k=KD)),
                    (n2g, a["norm2_g_2"].rearrange("o (p k) -> p (o k)", k=KD)),
                    (qg2[0:HD], a["q_norm_g_2"].rearrange("o p -> p o")), (qg2[HD:P], a["q_norm_g_2"].rearrange("o p -> p o")),
                    (kg2[0:HD], a["k_norm_g_2"].rearrange("o p -> p o")), (kg2[HD:P], a["k_norm_g_2"].rearrange("o p -> p o")),
                    (cb, a["conv_b_2"].rearrange("o (c p) -> p (o c)", p=P)),
                    (brg, a["b_rg_2"].rearrange("o (c p) -> p (o c)", p=P)),
                    (big, a["b_ig_2"].rearrange("o (c p) -> p (o c)", p=P)),
                    (lam, a["lru_lambda_2"].rearrange("o (c p) -> p (o c)", p=P)),
                ) + tuple((cw[:, k, :], a["conv_w_2"][0, k].rearrange("(c p) -> p c", p=P)) for k in range(CONV)):
                    pool.dma_start(dst, src).then_inc(final_in, 16)
                    n_final += 1
            assert n_final == 14
            strict = tb("before")

            def mask_weights(h):
                pool.wait_ge(wexp, h + 1)
                v = stW[:, h, :].rearrange("p (b c) -> p b c", c=P)[:, 0:3:2, :]
                nc.gpsimd.tensor_tensor(v, v, spread(strict, 1, [P, 2, P]), ALU.mult).then_inc(w_masked, 1)

            for h in range(ST_H):
                pool.wait_ge(soft, h + 1)
                v = stS[:, h, :].rearrange("p (b c) -> p b c", c=P)[:, 0:3:2, :]
                nc.gpsimd.tensor_tensor(v, v, spread(strict, 1, [P, 2, P]), ALU.mult).then_inc(masked_sp, 1)
                if h >= 2:
                    mask_weights(h - 2)
            for h in range(ST_H - 2, ST_H):
                mask_weights(h)

        @block.scalar
        def _(act):
            act.wait_ge(tab_in, 16)

            def softmax_exp(name, l, p1, p0, scale):
                act.wait_ge(maxed[name], l + 1)
                for h in range(6):
                    nc.scalar.activation(p0[:, h, :], p0[:, h, :], ACT.Exp, bias=nmx[name][:, 0, h:h + 1], scale=scale,
                                         accum_out=psm[name][:, 0, h:h + 1])
                    ins = nc.scalar.activation(p1[:, h, :], p1[:, h, :], ACT.Exp, bias=nmx[name][:, 1, h:h + 1],
                                               scale=scale, accum_out=psm[name][:, 1, h:h + 1])
                if name == "swa":
                    ins = nc.scalar.activation(sk_e, sk_e, ACT.Exp)
                ins.then_inc(expd[name], 1)

            def rstd(link, dst, src, scale, eps, done):
                link(nc.scalar.activation(dst, src, ACT.Ln, bias=tb(eps), scale=scale))
                nc.scalar.activation(dst, dst, ACT.Exp, scale=-0.5).then_inc(done, 1)

            with act.Fori(0, NL) as l:
                link = Link(act, act_link, l * ACT_LINKS)
                for n in (0, 2):
                    act.wait_ge(*full(f"xT{n}", l))
                    nc.scalar.copy(XT[:, 2 * n:2 * n + 2, :], bank(f"xT{n}")[:, :]).then_inc(*took(f"xT{n}"))
                for n, w in ((0, 512), (1, 512), (2, 256)):
                    act.wait_ge(*full(f"lat{n}", l))
                    nc.scalar.activation(lat_sq[:, 2 * n:2 * n + w // SEQ, :], bank(f"lat{n}")[:, 0:w],
                                         ACT.Square).then_inc(lat_squared, 1)
                turn = slice(NOPE, DQ)
                nc.scalar.copy(krT[turn, :], bank("lat2")[turn, SEQ:2 * SEQ]).then_inc(kr_copied, 1)
                act.wait_ge(*full("ret_q", l))
                nc.scalar.copy(ret_qT, bank("ret_q")[:, :]).then_inc(*took("ret_q"))
                act.wait_ge(*full("ret_k", l))
                nc.scalar.copy(ret_kT, bank("ret_k")[:, :]).then_inc(*took("ret_k"))
                act.wait_ge(*full("lat_ssq", l))
                nc.scalar.activation(lat_rstd[:, 0, :], bank("lat_ssq")[:, 0:SEQ], ACT.Ln, bias=tb("rms_eps"), scale=1.0 / Q_RANK)
                nc.scalar.activation(lat_rstd[:, 1, :], bank("lat_ssq")[:, SEQ:2 * SEQ], ACT.Ln, bias=tb("rms_eps"),
                                     scale=1.0 / KV_RANK).then_inc(*took("lat_ssq"))
                act.wait_ge(*read("lat_ssq", l))
                nc.scalar.activation(lat_rstd, lat_rstd, ACT.Exp, scale=-0.5).then_inc(rstd_ready, 1)
                act.wait_ge(*full("swa_q01", l))
                nc.scalar.mul(swa_qT[:, 0:2, :], bank("swa_q01")[:, :], HD ** -0.5).then_inc(*took("swa_q01"))
                act.wait_ge(*full("swa_q2k", l))
                nc.scalar.mul(swa_qT[:, 2, :], bank("swa_q2k")[:, 0:SEQ], HD ** -0.5)
                nc.scalar.copy(swa_kT, bank("swa_q2k")[:, SEQ:2 * SEQ]).then_inc(*took("swa_q2k"))
                for t in range(T):
                    act.wait_ge(*full(f"ret_vg{t}", l))
                    nc.scalar.copy(ret_v[:, t, :], bank(f"ret_vg{t}")[:, 0:256])
                    nc.scalar.activation(ret_g[:, t, :], bank(f"ret_vg{t}")[:, 256:512], ACT.Silu).then_inc(*took(f"ret_vg{t}"))
                act.wait_ge(*full("swa_v", l))
                nc.scalar.copy(swa_v, bank("swa_v")[:, 0:T * P]).then_inc(*took("swa_v"))
                for n in range(3):
                    act.wait_ge(*full(f"mla_q{n}", l))
                    nc.scalar.copy(mla_qT[0:DQ, 2 * n:2 * n + 2, :], bank(f"mla_q{n}")[0:DQ, :]).then_inc(*took(f"mla_q{n}"))
                for t in range(T):
                    act.wait_ge(*full(f"mla_v{t}", l))
                    nc.scalar.copy(mla_v[:, t, :], bank(f"mla_v{t}")[:, 0:MLA_H * MLA_VD]).then_inc(*took(f"mla_v{t}"))
                softmax_exp("swa", l, swa_p1, swa_p0, 1.0)
                act.wait_ge(*read("ret_o", l))
                nc.scalar.activation(ret_sq, ret_c, ACT.Square).then_inc(gn_squared, 1)
                softmax_exp("mla", l, mla_p1, mla_p0, DQ ** -0.5)
                act.wait_ge(gn_var, l + 1)
                rstd(link, grs, gvar, 1.0 / HD, "ln_eps", gn_rstd)
                for h in range(0, 6, 2):
                    act.wait_ge(*full(f"swa_pT{h}", l))
                    nc.scalar.copy(swa_pT[:, h, :], bank(f"swa_pT{h}")[:, 0:3 * P]).then_inc(*took(f"swa_pT{h}"))
                act.wait_ge(*full("ret_oT", l))
                nc.scalar.copy(XT[:, 0:2, :], bank("ret_oT")[:, :]).then_inc(*took("ret_oT"))
                act.wait_ge(*full("swa_o0", l))
                nc.scalar.copy(XT[:, 2:4, :], bank("swa_o0")[:, :]).then_inc(*took("swa_o0"))
                act.wait_ge(*full("swa_o1", l))
                nc.scalar.copy(XT[:, 4, :], bank("swa_o1")[:, 0:SEQ]).then_inc(*took("swa_o1"))
                for h in range(0, 6, 2):
                    act.wait_ge(*full(f"mla_pT{h}", l))
                    nc.scalar.copy(mla_pT[:, h, :], bank(f"mla_pT{h}")[:, 0:3 * P]).then_inc(*took(f"mla_pT{h}"))
                act.wait_ge(*full("mla_o0", l))
                nc.scalar.copy(XT[:, 5:7, :], bank("mla_o0")[:, :]).then_inc(*took("mla_o0"))
                act.wait_ge(*full("mla_o1", l))
                nc.scalar.copy(XT[:, 7, :], bank("mla_o1")[:, 0:SEQ]).then_inc(*took("mla_o1"))
                act.wait_ge(ln_var, l * 2 + 1)
                rstd(link, lrs, mv2[:, :, 1:2], 1.0, "ln_eps", ln_rstd)
                for n in (0, 2):
                    act.wait_ge(*full(f"x1T{n}", l))
                    nc.scalar.copy(XT[:, 2 * n:2 * n + 2, :], bank(f"x1T{n}")[:, :]).then_inc(*took(f"x1T{n}"))
                act.wait_ge(*full("router", l))
                nc.scalar.activation(sc, bank("router")[:, 0:2 * N_EXP], ACT.Exp, scale=-1.0).then_inc(*took("router"))
                act.wait_ge(*full("gatesT", l))
                nc.scalar.copy(gatesT[0:N_EXP, :], bank("gatesT")[0:N_EXP, 0:SEQ]).then_inc(*took("gatesT"))
                act.wait_ge(*read("gatesT", l))
                act.dma_start(gates_dram[bass.ds(l, 1)].rearrange("o e t -> (o e) t"), gatesT[0:N_EXP, :]).then_inc(gates_out, 16)
                act.wait_ge(gates_out, (l + 1) * 16)
                act.dma_start(gates_b, gates_dram[bass.ds(l, 1)].rearrange("o e t -> (o e t)").partition_broadcast(P)
                              ).then_inc(gates_in, 16)
                with act.Fori(0, N_EXP // 2) as m:
                    for s in range(2):
                        act.wait_ge(*read(f"up{s}", l, m - 1))
                        act.wait_ge(*full(f"gate{s}", l, m))
                        nc.scalar.activation(sig[s], bank(f"gate{s}")[:, :], ACT.Silu).then_inc(*took(f"gate{s}"))
                act.wait_ge(ln_var, l * 2 + 2)
                rstd(link, lrs, mv2[:, :, 1:2], 1.0, "ln_eps", ln_rstd)
                assert link.n == ACT_LINKS, link.n

            link = Link(act, act_fin)

            def rms_rows_of(n):
                if n == 0:
                    act.wait_ge(x_ready, (NL + 1) * T)
                else:
                    for j in range(4):
                        act.wait_ge(*read(f"out{j}", NL))
                for t in range(T):
                    ins = nc.scalar.activation(xn[:, t, :], X[:, t, :], ACT.Square, accum_out=rss[:, t:t + 1])
                link(ins)
                link(nc.scalar.activation(rss, rss, ACT.Ln, bias=tb("rms_eps"), scale=1.0 / D))
                nc.scalar.activation(rss, rss, ACT.Exp, scale=-0.5).then_inc(rms_rstd, 1)

            act.wait_ge(final_in, 14 * 16)
            rms_rows_of(0)
            for n in (0, 2):
                act.wait_ge(*full(f"n1T{n}", NL))
                for k in range(2):
                    ins = nc.scalar.activation(XT[:, 2 * n + k, :], bank(f"n1T{n}")[:, k * SEQ:(k + 1) * SEQ], ACT.Copy,
                                               scale=n1g[:, 2 * n + k:2 * n + k + 1])
                ins.then_inc(*took(f"n1T{n}"))
            for n, name in enumerate(("q0", "q1", "k0", "k1")):
                act.wait_ge(*full(name, NL))
                nc.scalar.activation(qk_sq[:, n, :], bank(name)[:, :], ACT.Square).then_inc(qk_squared, 1)
            for n in range(4):
                act.wait_ge(*full(f"ssq{n}", NL))
                nc.scalar.activation(qk_rstd[:, n, :], bank(f"ssq{n}")[:, :], ACT.Ln, bias=tb("rms_eps"), scale=1.0 / HD
                                     ).then_inc(*took(f"ssq{n}"))
                act.wait_ge(*read(f"ssq{n}", NL))
                nc.scalar.activation(qk_rstd[:, n, :], qk_rstd[:, n, :], ACT.Exp, scale=-0.5).then_inc(qk_rstd_ok, 1)
                if n in (1, 3):
                    t = n // 2
                    act.wait_ge(*full(f"v{t}", NL))
                    nc.scalar.copy(st_v[:, t, :], bank(f"v{t}")[:, :]).then_inc(*took(f"v{t}"))
            act.wait_ge(pad_zero, 1)
            for n in range(2):
                act.wait_ge(*full(f"xl{n}", NL))
                nc.scalar.copy(xl_pad[:, 2 * n:2 * n + 2, CONV - 1:], bank(f"xl{n}")[:, :].rearrange("p (a b) -> p a b", b=SEQ)
                               ).then_inc(*took(f"xl{n}"))
            for n in range(2):
                act.wait_ge(*full(f"gl{n}", NL))
                nc.scalar.copy(glT[:, 2 * n:2 * n + 2, :], bank(f"gl{n}")[:, :]).then_inc(*took(f"gl{n}"))

            def soft_part(h):
                act.wait_ge(*full(f"z{h}", NL))
                link(nc.scalar.activation(stW[:, h, :], bank(f"z{h}")[:, 0:3 * P], ACT.Abs))
                link(nc.scalar.activation(stW[:, h, :], stW[:, h, :], ACT.Exp, scale=-1.0))
                nc.scalar.activation(stW[:, h, :], stW[:, h, :], ACT.Ln, bias=tb("one")).then_inc(log1pd, 1)

            def weight_part(h):
                act.wait_ge(*read(f"sfx{h}", NL))
                nc.scalar.activation(stW[:, h, :], stW[:, h, :], ACT.Exp).then_inc(wexp, 1)

            act.wait_ge(consts2, 1)
            nc.scalar.activation(sp_e, sp_e, ACT.Exp).then_inc(sp_lam, 1)
            for n, (dst, b) in enumerate(((rgT, brg), (igT, big))):
                for c in range(4):
                    name = ("rg0", "rg1", "ig0", "ig1")[2 * n + c // 2]
                    if c % 2 == 0:
                        act.wait_ge(*full(name, NL))
                    ins = nc.scalar.activation(dst[:, c, :], bank(name)[:, (c % 2) * SEQ:(c % 2 + 1) * SEQ], ACT.Exp,
                                               bias=b[:, c:c + 1], scale=-1.0)
                    if c % 2 == 1:
                        ins.then_inc(*took(name))
            for h in range(ST_H):
                soft_part(h)
                if h >= 2:
                    weight_part(h - 2)
            for h in range(ST_H - 2, ST_H):
                weight_part(h)
            act.wait_ge(lru_la, 1)
            nc.scalar.activation(lruA, rgT, ACT.Exp)
            nc.scalar.activation(lruT, rgT, ACT.Tanh, scale=-1.0).then_inc(lru_at, 1)
            act.wait_ge(gel_in, 1)
            nc.scalar.activation(gel, gel, ACT.Tanh, scale=float(np.sqrt(2.0 / np.pi))).then_inc(gel_t, 1)
            act.wait_ge(lru_m2, 1)
            nc.scalar.activation(lruT, lruT, ACT.Sqrt).then_inc(lru_sq, 1)
            for n in range(2):
                act.wait_ge(*full(f"att{n}", NL))
                nc.scalar.copy(XT[:, 2 * n:2 * n + 2, :], bank(f"att{n}")[:, :]).then_inc(*took(f"att{n}"))
            rms_rows_of(1)
            for n in (0, 2):
                act.wait_ge(*full(f"n2T{n}", NL))
                for k in range(2):
                    ins = nc.scalar.activation(XT[:, 2 * n + k, :], bank(f"n2T{n}")[:, k * SEQ:(k + 1) * SEQ], ACT.Copy,
                                               scale=n2g[:, 2 * n + k:2 * n + k + 1])
                ins.then_inc(*took(f"n2T{n}"))
            with act.Fori(0, N_CHUNK // 2) as m:
                for s in range(2):
                    act.wait_ge(*full(f"ff{s}", NL, m))
                    nc.scalar.activation(hid[s], bank(f"ff{s}")[:, :], ACT.Relu).then_inc(relu_done, 1)

        @block.tensor
        def _(pe):
            def product(dst, pairs, first=True, last=True):
                for n, (lhsT, rhs) in enumerate(pairs):
                    ins = nc.tensor.matmul(dst, lhsT, rhs, start=first and n == 0, stop=last and n == len(pairs) - 1)
                return ins

            def features(w, cols, act_T=None):
                return [(w[:, k, cols], XT[:, k, :]) for k in range(KD)]

            def rows(w, cols, t):
                return [(XT[:, k, token(t)], w[:, k, cols]) for k in range(KD)]

            def transpose_rows(prefix, src, l):
                for n in range(4):
                    name = f"{prefix}{n}"
                    pe.wait_ge(*free(name, l))
                    for k in (2 * n, 2 * n + 1):
                        for t in range(T):
                            c = (k % 2) * SEQ + t * P
                            ins = nc.tensor.transpose(bank(name)[:, c:c + P], src[:, t, k:D:KD], ident)
                    ins.then_inc(*made(name))

            def transposes_read(prefix, l):
                for n in range(4):
                    pe.wait_ge(*read(f"{prefix}{n}", l))

            def tile_of(name, n, w=SEQ):
                return bank(name)[:, n * w:(n + 1) * w]

            def probs_T(name, h, p1, p0, l):
                job = f"{name}_pT{h}"
                pe.wait_ge(*free(job, l))
                pe.wait_ge(normed[name], l * 6 + h + 1)
                nc.tensor.transpose(bank(job)[:, 0:P], p0[:, h, :], ident)
                nc.tensor.transpose(bank(job)[:, P:2 * P], p1[:, h, 0:P], ident)
                nc.tensor.transpose(bank(job)[:, 2 * P:3 * P], p1[:, h, P:2 * P], ident).then_inc(*made(job))

            def weighted_values(dst, v0, v1, pT):
                nc.tensor.matmul(dst, v0, pT[:, 0:2 * P], start=True, stop=False)
                return nc.tensor.matmul(dst[:, P:2 * P], v1, pT[:, 2 * P:3 * P], start=False, stop=True)

            def key_major_scores(dst, kT, qT):
                nc.tensor.matmul(dst[:, 0:2 * P], kT[:, 0:P], qT, start=True, stop=True)
                return nc.tensor.matmul(dst[:, 2 * P:3 * P], kT[:, P:2 * P], qT[:, P:2 * P], start=True, stop=True)

            def scores(name, kq, l):
                for n in range(3):
                    job = f"{name}_s1_{n}"
                    pe.wait_ge(*free(job, l))
                    for h in (2 * n, 2 * n + 1):
                        kT, qT = kq(h)
                        if name == "swa" and n == 1 and h == 3:
                            ins.then_inc(rows_turned, 1)
                            pe.wait_ge(rows_turned, l * 2 + 1)
                        ins = nc.tensor.matmul(tile_of(job, h % 2), qT[:, P:2 * P], kT, start=True, stop=True)
                    ins.then_inc(*made(job))
                for n, heads in enumerate((range(4), range(4, 6))):
                    job = f"{name}_s0_{n}"
                    pe.wait_ge(*free(job, l))
                    for h in heads:
                        kT, qT = kq(h)
                        if name == "swa" and h == 3:
                            ins.then_inc(rows_turned, 1)
                            pe.wait_ge(rows_turned, l * 2 + 2)
                        ins = nc.tensor.matmul(tile_of(job, h % 4, P), qT[:, 0:P], kT[:, 0:P], start=True, stop=True)
                    ins.then_inc(*made(job))

            pe.wait_ge(tab_in, 16)
            pe.wait_ge(router_in, 32)
            with pe.Fori(0, NL) as l:
                pe.wait_ge(x_ready, (l + 1) * T)
                transpose_rows("xT", X, l)
                transposes_read("xT", l)
                pe.wait_ge(wlat_in, (l + 1) * 16)
                for n in range(5):
                    job = f"lat{n // 2}"
                    if n % 2 == 0:
                        pe.wait_ge(*free(job, l))
                    ins = product(tile_of(job, n % 2), features(w_lat, slice(n * P, (n + 1) * P)))
                    if n % 2 == 1:
                        ins.then_inc(*made(job))
                product(bank("lat2")[NOPE:DQ, SEQ:2 * SEQ], features(w_lat, slice(5 * P, N_LAT))).then_inc(*made("lat2"))
                pe.wait_ge(wrqk_in, (l + 1) * 16)
                for n, job in enumerate(("ret_q", "ret_k")):
                    pe.wait_ge(*free(job, l))
                    for c in range(2):
                        ins = product(tile_of(job, c), features(w_rqk, slice((2 * n + c) * P, (2 * n + c + 1) * P)))
                    ins.then_inc(*made(job))
                pe.wait_ge(*free("lat_ssq", l))
                pe.wait_ge(lat_squared, (l + 1) * 3)
                product(tile_of("lat_ssq", 0), [(ones, lat_sq[:, c, :]) for c in range(3)])
                product(tile_of("lat_ssq", 1), [(ones, lat_sq[:, c, :]) for c in (3, 4)]).then_inc(*made("lat_ssq"))
                pe.wait_ge(wswa_in, (l + 1) * 7 * 16)
                for n in range(4):
                    job = ("swa_q01", "swa_q01", "swa_q2k", "swa_q2k")[n]
                    if n % 2 == 0:
                        pe.wait_ge(*free(job, l))
                    ins = product(tile_of(job, n % 2), features(w_swa, slice(n * P, (n + 1) * P)))
                    if n % 2 == 1:
                        ins.then_inc(*made(job))
                pe.wait_ge(wrvg_in, (l + 1) * 16)
                for t in range(T):
                    pe.wait_ge(*free(f"ret_vg{t}", l))
                    product(bank(f"ret_vg{t}")[:, :], rows(w_rvg, slice(0, 512), t)).then_inc(*made(f"ret_vg{t}"))
                pe.wait_ge(*free("swa_v", l))
                for t in range(T):
                    ins = product(tile_of("swa_v", t, P), rows(w_swa, slice(C_SV - C_SQ, C_CQ - C_SQ), t))
                ins.then_inc(*made("swa_v"))
                for job, src, name in (("ret_q_swap", ret_qT, "ret_q"), ("ret_k_swap", ret_kT, "ret_k")):
                    pe.wait_ge(*free(job, l))
                    pe.wait_ge(*read(name, l))
                    nc.tensor.matmul(bank(job)[:, :], tb("swap_r"), src, start=True, stop=True).then_inc(*made(job))
                pe.wait_ge(wup_in, (l + 1) * 32)
                for n in range(3):
                    pe.wait_ge(*free(f"mla_q{n}", l))
                    pe.wait_ge(*read("lat2", l))
                    for h in (2 * n, 2 * n + 1):
                        ins = product(tile_of(f"mla_q{n}", h % 2)[0:DQ], [
                            (w_uq[:, c, h * DQ:(h + 1) * DQ], lat_n[:, c, :]) for c in range(3)])
                    ins.then_inc(*made(f"mla_q{n}"))
                for n in range(3):
                    pe.wait_ge(*free(f"mla_k{n}", l))
                    for h in (2 * n, 2 * n + 1):
                        ins = product(tile_of(f"mla_k{n}", h % 2)[0:NOPE], [
                            (w_ukv[:, c, h * P:h * P + NOPE], lat_n[:, 3 + c, :]) for c in range(2)])
                    ins.then_inc(*made(f"mla_k{n}"))
                for t in range(T):
                    pe.wait_ge(*free(f"mla_v{t}", l))
                    product(bank(f"mla_v{t}")[:, 0:384].rearrange("p (h d) -> p h d", d=MLA_VD), [
                        (lat_n[:, 3 + c, token(t)], w_ukv[:, c, :].rearrange("p (h d) -> p h d", d=P)[:, :, NOPE:P])
                        for c in range(2)]).then_inc(*made(f"mla_v{t}"))
                turn = slice(NOPE, DQ)
                for n in range(3):
                    pe.wait_ge(*free(f"mla_q_swap{n}", l))
                    nc.tensor.matmul(bank(f"mla_q_swap{n}")[:, :], tb("swap_m")[turn, :], mla_qT[turn, 2 * n:2 * n + 2, :],
                                     start=True, stop=True).then_inc(*made(f"mla_q_swap{n}"))
                pe.wait_ge(*free("mla_kr_swap", l))
                pe.wait_ge(kr_copied, l + 1)
                nc.tensor.matmul(bank("mla_kr_swap")[:, 0:SEQ], tb("swap_m")[turn, :], krT[turn, :],
                                 start=True, stop=True).then_inc(*made("mla_kr_swap"))
                pe.wait_ge(ret_roped, (l + 1) * 2)
                for h in range(RET_H):
                    job, part = f"ret_s{h}", slice((h % 2) * HD, (h % 2 + 1) * HD)
                    pe.wait_ge(*free(job, l))
                    key_major_scores(bank(job), ret_kT[part, h // 2, :], ret_qT[part, h // 2, :]).then_inc(*made(job))
                scores("swa", lambda h: (swa_kT[(h // 3) * HD:(h // 3 + 1) * HD, :],
                                         swa_qT[(h // 3) * HD:(h // 3 + 1) * HD, h % 3, :]), l)
                for h in range(RET_H):
                    pe.wait_ge(*read(f"ret_s{h}", l))
                ro = bank("ret_o")[:, :].rearrange("p (t h d) -> p t h d", t=T, h=RET_H)
                for h in range(RET_H):
                    v = ret_v[:, :, h * HD:(h + 1) * HD]
                    nc.tensor.matmul(ro[:, 0, h, :], ret_pT[:, h, 0:P], v[:, 0, :], start=True, stop=True)
                    nc.tensor.matmul(ro[:, 1, h, :], ret_pT[:, h, P:2 * P], v[:, 0, :], start=True, stop=False)
                    ins = nc.tensor.matmul(ro[:, 1, h, :], ret_pT[:, h, 2 * P:3 * P], v[:, 1, :], start=False, stop=True)
                ins.then_inc(*made("ret_o"))
                pe.wait_ge(q_roped, l + 1)
                pe.wait_ge(k_roped, l + 2)
                scores("mla", lambda h: (mla_kT[0:DQ, h, :], mla_qT[0:DQ, h, :]), l)
                for h in range(SWA_H):
                    probs_T("swa", h, swa_p1, swa_p0, l)
                pe.wait_ge(*free("ret_oT", l))
                pe.wait_ge(ret_out, l + 1)
                rc = ret_c.rearrange("p (t h) d -> p t (h d)", t=T)
                for c in range(2):
                    for t in range(T):
                        ins = nc.tensor.transpose(bank("ret_oT")[:, c * SEQ + t * P:c * SEQ + (t + 1) * P],
                                                  rc[:, t, c * P:(c + 1) * P], ident)
                ins.then_inc(*made("ret_oT"))

                def attend(name, pT, value):
                    for h in range(6):
                        job = f"{name}_o{h // 4}"
                        if h % 4 == 0:
                            pe.wait_ge(*free(job, l))
                        pe.wait_ge(*read(f"{name}_pT{h}", l))
                        dst = tile_of(job, (h // 2) % 2)[(h % 2) * HD:(h % 2 + 1) * HD, :]
                        ins = weighted_values(dst, value(h, 0), value(h, 1), pT[:, h, :])
                        if h in (3, 5):
                            ins.then_inc(*made(job))

                attend("swa", swa_pT, lambda h, t: swa_v[:, t, (h // 3) * HD:(h // 3 + 1) * HD])
                for h in range(MLA_H):
                    probs_T("mla", h, mla_p1, mla_p0, l)
                attend("mla", mla_pT, lambda h, t: mla_v[:, t, h * MLA_VD:(h + 1) * MLA_VD])
                pe.wait_ge(wout_in, (l + 1) * 16)
                for job in ("ret_oT", "swa_o0", "swa_o1", "mla_o0", "mla_o1"):
                    pe.wait_ge(*read(job, l))
                for n in range(4):
                    pe.wait_ge(*free(f"mix{n}", l))
                    product(bank(f"mix{n}")[:, :], rows(w_out, slice((n % 2) * 512, (n % 2 + 1) * 512), n // 2)
                            ).then_inc(*made(f"mix{n}"))
                pe.wait_ge(x1_ready, (l + 1) * T)
                transpose_rows("x1T", X, l)
                transposes_read("x1T", l)
                pe.wait_ge(*free("router", l))
                for t in range(T):
                    ins = product(tile_of("router", t, N_EXP), rows(router, slice(0, N_EXP), t))
                ins.then_inc(*made("router"))

                def expert_up(m, s):
                    pe.wait_ge(gu_in[s], (l * (N_EXP // 2) + m + 1) * 16)
                    for n, job in enumerate((f"gate{s}", f"up{s}")):
                        pe.wait_ge(*free(job, l, m))
                        for c in range(2):
                            f = 2 * n + c
                            ins = product(tile_of(job, c), features(w_gu[s], slice(f * P, (f + 1) * P)))
                        ins.then_inc(*made(job))

                def expert_down(m, s, first=False, last=False):
                    pe.wait_ge(dn_in[s], (l * (N_EXP // 2) + m + 1) * 16)
                    pe.wait_ge(*read(f"up{s}", l, m))
                    for n in range(4):
                        if first:
                            pe.wait_ge(*free(f"y{n}", l))
                        for c in range(2):
                            ins = nc.tensor.matmul(bank(f"y{n}")[:, :], hid[s][:, c, token(n // 2)],
                                                   w_dn[s][:, c, (n % 2) * 512:(n % 2 + 1) * 512],
                                                   start=first and c == 0, stop=last and c == 1)
                        if last:
                            ins.then_inc(*made(f"y{n}"))
                    if not last:
                        ins.then_inc(expert_used, 1)

                expert_up(0, 0)
                pe.wait_ge(*free("gatesT", l))
                pe.wait_ge(gates_ready, l + 1)
                for t in range(T):
                    ins = nc.tensor.transpose(bank("gatesT")[0:N_EXP, token(t)], gates[:, t, :], ident)
                ins.then_inc(*made("gatesT"))
                expert_up(0, 1)
                expert_down(0, 0, first=True)
                with pe.Fori(1, N_EXP // 2) as m:
                    expert_up(m, 0)
                    expert_down(m - 1, 1)
                    expert_up(m, 1)
                    expert_down(m, 0)
                expert_down(N_EXP // 2 - 1, 1, last=True)

            l = NL
            pe.wait_ge(rms_rows, T)
            transpose_rows("n1T", xn, l)
            transposes_read("n1T", l)
            pe.wait_ge(wqk_in, 16)

            def tiles2(job, w, c0):
                pe.wait_ge(*free(job, l))
                for c in range(2):
                    ins = product(tile_of(job, c), features(w, slice(c0 + c * P, c0 + (c + 1) * P)))
                ins.then_inc(*made(job))

            for n, job in enumerate(("q0", "q1", "k0", "k1")):
                tiles2(job, w_qk2, n * 2 * P)

            def head_sums(n):
                pe.wait_ge(*free(f"ssq{n}", l))
                pe.wait_ge(qk_squared, n + 1)
                nc.tensor.matmul(bank(f"ssq{n}")[:, :], tb("half_ones"), qk_sq[:, n, :], start=True, stop=True
                                 ).then_inc(*made(f"ssq{n}"))

            def values(t):
                pe.wait_ge(*free(f"v{t}", l))
                product(bank(f"v{t}")[:, :], rows(w_vx2, slice(0, 512), t)).then_inc(*made(f"v{t}"))

            head_sums(0)
            head_sums(1)
            pe.wait_ge(wvx_in, 16)
            values(0)
            head_sums(2)
            values(1)
            head_sums(3)
            tiles2("xl0", w_vx2, 512)
            tiles2("xl1", w_vx2, 512 + 2 * P)
            pe.wait_ge(wgl_in, 16)
            tiles2("gl0", w_gl2, 0)
            tiles2("gl1", w_gl2, 2 * P)

            def z_of(h):
                job, part = f"z{h}", slice((h % 2) * HD, (h % 2 + 1) * HD)
                pe.wait_ge(*free(job, l))
                key_major_scores(bank(job), st_kT[part, h // 2, :], st_qT[part, h // 2, :]).then_inc(*made(job))

            def suffix_of(h):
                job = f"sfx{h}"
                pe.wait_ge(*free(job, l))
                pe.wait_ge(masked_sp, h + 1)
                later, s = tb("later"), stS[:, h, :]
                nc.tensor.matmul(bank(job)[:, 0:2 * P], later, s[:, 0:2 * P], start=True, stop=False)
                nc.tensor.matmul(bank(job)[:, P:2 * P], ones, s[:, 2 * P:3 * P], start=False, stop=True)
                nc.tensor.matmul(bank(job)[:, 2 * P:3 * P], later, s[:, 2 * P:3 * P], start=True, stop=True
                                 ).then_inc(*made(job))

            for name in ("q0", "q1", "k0", "k1"):
                pe.wait_ge(*read(name, l))
            z_of(0)
            z_of(1)
            pe.wait_ge(bd_in, 64)
            pe.wait_ge(conv_done, 1)
            for n, pre in enumerate(("rg", "ig")):
                for c in range(4):
                    job = f"{pre}{c // 2}"
                    if c % 2 == 0:
                        pe.wait_ge(*free(job, l))
                    ins = nc.tensor.matmul(tile_of(job, c % 2), w_bd[:, n, c, :], conv_u[:, c, :], start=True, stop=True)
                    if c % 2 == 1:
                        ins.then_inc(*made(job))
            for h in range(ST_H):
                suffix_of(h)
                if h + 2 < ST_H:
                    z_of(h + 2)
            for h in range(ST_H):
                job = f"att{h // 4}"
                if h % 4 == 0:
                    pe.wait_ge(*free(job, l))
                pe.wait_ge(w_masked, h + 1)
                dst = tile_of(job, (h // 2) % 2)[(h % 2) * HD:(h % 2 + 1) * HD, :]
                ins = weighted_values(dst, st_v[:, 0, h * HD:(h + 1) * HD], st_v[:, 1, h * HD:(h + 1) * HD], stW[:, h, :])
                if h % 4 == 3:
                    ins.then_inc(*made(job))
            pe.wait_ge(wout_in, (NL + 1) * 16)
            pe.wait_ge(*read("att0", l))
            pe.wait_ge(*read("att1", l))
            pe.wait_ge(lru_mix, 1)
            for n in range(4):
                pe.wait_ge(*free(f"out{n}", l))
                product(bank(f"out{n}")[:, :], rows(w_out, slice((n % 2) * 512, (n % 2 + 1) * 512), n // 2)
                        ).then_inc(*made(f"out{n}"))
            pe.wait_ge(rms_rows, 2 * T)
            transpose_rows("n2T", xn, l)
            transposes_read("n2T", l)

            def chunk_up(m, s):
                pe.wait_ge(up_in[s], (m + 1) * 16)
                pe.wait_ge(*free(f"ff{s}", l, m))
                for c in range(2):
                    ins = product(tile_of(f"ff{s}", c), features(w_gu[s], slice(c * P, (c + 1) * P)))
                ins.then_inc(*made(f"ff{s}"))

            def chunk_down(m, s, first=False, last=False):
                pe.wait_ge(down_in[s], (m + 1) * 16)
                pe.wait_ge(*read(f"ff{s}", l, m))
                for n in range(4):
                    if first:
                        pe.wait_ge(*free(f"m{n}", l))
                    for c in range(2):
                        ins = nc.tensor.matmul(bank(f"m{n}")[:, :], hid[s][:, c, token(n // 2)],
                                               w_dn[s][:, c, (n % 2) * 512:(n % 2 + 1) * 512],
                                               start=first and c == 0, stop=last and c == 1)
                    if last:
                        ins.then_inc(*made(f"m{n}"))
                if not last:
                    ins.then_inc(ff_used, 1)

            chunk_up(0, 0)
            chunk_up(0, 1)
            chunk_down(0, 0, first=True)
            with pe.Fori(1, N_CHUNK // 2) as m:
                chunk_up(m, 0)
                chunk_down(m - 1, 1)
                chunk_up(m, 1)
                chunk_down(m, 0)
            chunk_down(N_CHUNK // 2 - 1, 1, last=True)

        @block.vector
        def _(dve):
            v = nc.vector

            def layer_norm(l, link, which, jobs, loaded, done):
                for t in range(T):
                    for half in range(2):
                        job = jobs[2 * t + half]
                        part = X[:, t, half * 512:(half + 1) * 512]
                        dve.wait_ge(*full(job, l))
                        v.scalar_tensor_tensor(part, part, ALPHA, bank(job)[:, :], ALU.mult, ALU.add).then_inc(*took(job))
                for t in range(T):
                    for half in range(2):
                        dve.wait_ge(*read(jobs[2 * t + half], l))
                        ins = v.bn_stats(st6[:, t, half * 6:(half + 1) * 6], X[:, t, half * 512:(half + 1) * 512])
                    link(ins)
                    v.memset(lrs[:, t, :], 0.0)
                    ins = v.bn_aggr(mv2[:, t, :], st6[:, t, :])
                ins.then_inc(ln_var, 1)
                dve.wait_ge(loaded, (l + 1) * 32)
                dve.wait_ge(ln_rstd, l * 2 + which)
                for t in range(T):
                    link(v.tensor_scalar(X[:, t, :], X[:, t, :], mv2[:, t, 0:1], lrs[:, t, 0:1], ALU.subtract, ALU.mult))
                    link(v.tensor_tensor(X[:, t, :], X[:, t, :], LNB[:, 0, :], ALU.mult))
                    v.tensor_tensor(X[:, t, :], X[:, t, :], LNB[:, 1, :], ALU.add).then_inc(done, 1)

            def softmax_scores(name, l, link, p1, p0, mask, scale):
                for n in range(3):
                    job = f"{name}_s1_{n}"
                    dve.wait_ge(*full(job, l))
                    v.tensor_tensor(p1[:, 2 * n:2 * n + 2, :], bank(job)[:, :].rearrange("p (a b) -> p a b", b=SEQ),
                                    spread(mask, 1, [P, 2, SEQ]), ALU.add).then_inc(*took(job))
                for n, (h0, k) in enumerate(((0, 4), (4, 2))):
                    job = f"{name}_s0_{n}"
                    dve.wait_ge(*full(job, l))
                    v.tensor_tensor(p0[:, h0:h0 + k, :], bank(job)[:, 0:k * P].rearrange("p (a b) -> p a b", b=P),
                                    spread(mask[:, P:2 * P], 1, [P, k, P]), ALU.add).then_inc(*took(job))
                for job in (f"{name}_s1_{n}" for n in range(3)):
                    dve.wait_ge(*read(job, l))
                v.tensor_reduce(mx[name][:, 1, :], p1, AX.X, ALU.max)
                dve.wait_ge(*read(f"{name}_s0_0", l))
                dve.wait_ge(*read(f"{name}_s0_1", l))
                link(v.tensor_reduce(mx[name][:, 0, :], p0, AX.X, ALU.max))
                if name == "swa":
                    dve.wait_ge(norms_in, (l + 1) * 64)
                    sinks = spread(sink_b, 1, [P, T, SWA_H])
                    link(v.tensor_tensor(mx[name], mx[name], sinks, ALU.max))
                    v.tensor_tensor(sk_e, sinks, mx[name], ALU.subtract)
                v.tensor_scalar(nmx[name], mx[name], -scale, None, ALU.mult).then_inc(maxed[name], 1)

            def softmax_norm(name, l, link, p1, p0):
                dve.wait_ge(expd[name], l + 1)
                if name == "swa":
                    link(v.tensor_tensor(psm[name], psm[name], sk_e, ALU.add))
                link(v.reciprocal(rin[name], psm[name]))
                for h in range(6):
                    v.tensor_scalar(p0[:, h, :], p0[:, h, :], rin[name][:, 0, h:h + 1], None, ALU.mult)
                    v.tensor_scalar(p1[:, h, :], p1[:, h, :], rin[name][:, 1, h:h + 1], None, ALU.mult
                                    ).then_inc(normed[name], 1)

            def evacuate(job, dst, l, rows=slice(0, P), w=512):
                dve.wait_ge(*full(job, l))
                v.tensor_copy(dst, bank(job)[rows, 0:w]).then_inc(*took(job))

            for b in range(8):
                v.memset(marks[:, b:b + 1], 0.0).then_inc(psum_read[b], 1)
            dve.wait_ge(x_in, 16)
            for t in range(T):
                v.memset(marks[:, 8 + t:9 + t], 0.0).then_inc(x_ready, 1)
            dve.wait_ge(tab_in, 16)
            with dve.Fori(0, NL) as l:
                link = Link(dve, dve_link, l * DVE_LINKS)
                for n in (1, 3):
                    evacuate(f"xT{n}", XT[:, 2 * n:2 * n + 2, :], l)
                turn = slice(NOPE, DQ)
                dve.wait_ge(norms_in, (l + 1) * 64)
                dve.wait_ge(rstd_ready, l + 1)
                for n in range(5):
                    job, kv = f"lat{n // 2}", n >= 3
                    gain = kvn_g[:, n - 3:n - 2] if kv else qn_g[:, n:n + 1]
                    ins = v.scalar_tensor_tensor(lat_n[:, n, :], bank(job)[:, (n % 2) * SEQ:(n % 2 + 1) * SEQ], gain,
                                                 lat_rstd[:, int(kv), :], ALU.mult, ALU.mult)
                    if n in (1, 3, 4):
                        ins.then_inc(*took(job))
                for n, (dst, job) in enumerate(((ret_qT, "ret_q_swap"), (ret_kT, "ret_k_swap"))):
                    dve.wait_ge(ret_cos, l * 2 + n + 1)
                    dve.wait_ge(*full(job, l))
                    v.tensor_tensor(dst, bank(job)[:, :].rearrange("p (a b) -> p a b", b=SEQ),
                                    spread(tb("sin_r"), 1, [P, 2, SEQ]), ALU.mult).then_inc(*took(job))
                    dve.wait_ge(*read(job, l))
                    v.tensor_tensor(dst, dst, rope_r[:, 2 * n:2 * n + 2, :], ALU.add).then_inc(ret_roped, 1)
                for n in range(3):
                    evacuate(f"mla_k{n}", mla_kT[0:NOPE, 2 * n:2 * n + 2, :], l, slice(0, NOPE))
                for n in range(3):
                    job = f"mla_q_swap{n}"
                    dve.wait_ge(*full(job, l))
                    v.tensor_tensor(rope_m[turn, 2 * n:2 * n + 2, :], bank(job)[turn, :].rearrange("p (a b) -> p a b", b=SEQ),
                                    spread(tb("sin_m")[turn], 1, [ROPE_D, 2, SEQ]), ALU.mult).then_inc(*took(job))
                dve.wait_ge(*full("mla_kr_swap", l))
                v.tensor_tensor(kr_sin[turn], bank("mla_kr_swap")[turn, 0:SEQ], tb("sin_m")[turn], ALU.mult
                                ).then_inc(*took("mla_kr_swap"))
                for h in range(RET_H):
                    dve.wait_ge(*full(f"ret_s{h}", l))
                    v.tensor_tensor(ret_pT[:, h, :], bank(f"ret_s{h}")[:, 0:3 * P], decay[:, h, :], ALU.mult
                                    ).then_inc(*took(f"ret_s{h}"))
                softmax_scores("swa", l, link, swa_p1, swa_p0, tb("mask_swa"), 1.0)
                dve.wait_ge(*full("ret_o", l))
                ro = bank("ret_o")[:, :].rearrange("p (g d) -> p g d", d=HD)
                link(v.tensor_reduce(gmu, ro, AX.X, ALU.add))
                link(v.tensor_scalar(gmu, gmu, 1.0 / HD, None, ALU.mult))
                v.tensor_tensor(ret_c, ro, spread(gmu, 2, [P, 8, HD]), ALU.subtract).then_inc(*took("ret_o"))
                softmax_scores("mla", l, link, mla_p1, mla_p0, tb("mask_mla"), DQ ** -0.5)
                softmax_norm("swa", l, link, swa_p1, swa_p0)
                dve.wait_ge(gn_squared, l + 1)
                v.tensor_reduce(gvar, ret_sq, AX.X, ALU.add).then_inc(gn_var, 1)
                for h in (1, 3, 5):
                    evacuate(f"swa_pT{h}", swa_pT[:, h, :], l, w=3 * P)
                dve.wait_ge(gn_rstd, l + 1)
                dve.wait_ge(ret_gate_w, l + 1)
                link(v.tensor_tensor(ret_c, ret_c, spread(grs, 2, [P, 8, HD]), ALU.mult))
                v.tensor_tensor(ret_c, ret_c, ret_g.rearrange("p t (h d) -> p (t h) d", d=HD), ALU.mult
                                ).then_inc(ret_out, 1)
                softmax_norm("mla", l, link, mla_p1, mla_p0)
                for h in (1, 3, 5):
                    evacuate(f"mla_pT{h}", mla_pT[:, h, :], l, w=3 * P)
                layer_norm(l, link, 1, ("mix0", "mix1", "mix2", "mix3"), ln1_in, x1_ready)
                for n in (1, 3):
                    evacuate(f"x1T{n}", XT[:, 2 * n:2 * n + 2, :], l)
                dve.wait_ge(router_in, 32)
                dve.wait_ge(*read("router", l))
                link(v.tensor_scalar(sc, sc, 1.0, None, ALU.add))
                link(v.reciprocal(sc, sc))
                link(v.tensor_tensor(bi.rearrange("p (t g) e -> p t (g e)", t=T), sc.rearrange("p (t e) -> p t e", t=T),
                                     spread(rbias, 1, [P, T, N_EXP]), ALU.add))
                v.tensor_tensor(pr[:, :, 0:3], bi[:, :, 0:3], bi[:, :, 1:4], ALU.add)
                v.tensor_tensor(pr[:, :, 3:5], bi[:, :, 0:2], bi[:, :, 2:4], ALU.add)
                link(v.tensor_tensor(pr[:, :, 5:6], bi[:, :, 0:1], bi[:, :, 3:4], ALU.add))
                link(v.tensor_reduce(gs, pr, AX.X, ALU.max))

                def beaten_by(val, n, buf1, buf2, dst, limit):
                    other, own = spread(val, 2, [P, n, 4, 4]), spread(val, 3, [P, n, 4, 4])
                    v.tensor_tensor(buf1, other, own, ALU.is_gt)
                    link(v.tensor_tensor(buf2, other, own, ALU.is_equal))
                    link(v.tensor_tensor(buf2, buf2, spread(tie, 1, [P, n, 4, 4]), ALU.mult))
                    link(v.tensor_tensor(buf1, buf1, buf2, ALU.add))
                    link(v.tensor_reduce(dst, buf1, AX.X, ALU.add))
                    link(v.tensor_scalar(dst, dst, limit, None, ALU.is_lt))

                beaten_by(gs.rearrange("p (t g) -> p t g", t=T), T, g1, g2, gsel.rearrange("p (t g) -> p t g", t=T), 0.5)
                beaten_by(bi, 8, c1, c2, esel, 1.5)
                link(v.tensor_tensor(esel, esel, spread(gsel, 2, [P, 8, 4]), ALU.mult))
                link(v.tensor_tensor(esel, esel, sc.rearrange("p (g e) -> p g e", e=4), ALU.mult))
                e2 = esel.rearrange("p (t g) e -> p t (g e)", t=T)
                link(v.tensor_reduce(gden, e2, AX.X, ALU.add))
                link(v.reciprocal(gden, gden))
                v.tensor_tensor(gates, e2, spread(gden, 2, [P, T, N_EXP]), ALU.mult).then_inc(gates_ready, 1)
                dve.wait_ge(gates_in, (l + 1) * 16)
                v.memset(gden, 0.0)
                with dve.Fori(0, N_EXP // 2) as m:
                    moe = Link(dve, dve_moe, (l * (N_EXP // 2) + m) * (2 * MOE_LINKS))
                    for s in range(2):
                        dve.wait_ge(*read(f"gate{s}", l, m))
                        moe(v.tensor_tensor(gat[s].rearrange("p (a b) -> p a b", b=SEQ), sig[s].rearrange("p (a b) -> p a b", b=SEQ),
                                            gates_b[:, bass.ds(2 * m + s, 1), :].to_broadcast([P, 2, SEQ]), ALU.mult))
                        dve.wait_ge(*full(f"up{s}", l, m))
                        v.tensor_tensor(hid[s], gat[s], bank(f"up{s}")[:, :], ALU.mult).then_inc(*took(f"up{s}"))
                    assert moe.n == 2 * MOE_LINKS
                layer_norm(l, link, 2, ("y0", "y1", "y2", "y3"), ln2_in, x_ready)
                assert link.n == DVE_LINKS, link.n

            l = NL
            link = Link(dve, dve_fin)
            dve.wait_ge(final_in, 14 * 16)
            v.memset(xl_pad[:, :, 0:CONV - 1], 0.0).then_inc(pad_zero, 1)
            v.tensor_scalar(qg2, qg2, HD ** -0.5, None, ALU.mult)
            v.tensor_scalar(brg, brg, -1.0, None, ALU.mult)
            v.tensor_scalar(big, big, -1.0, None, ALU.mult)
            v.scalar_tensor_tensor(sp_e, lam, -1.0, lam, ALU.mult, ALU.min).then_inc(consts2, 1)

            def scale_rows(n):
                dve.wait_ge(rms_rstd, n + 1)
                for t in range(T):
                    v.tensor_scalar(xn[:, t, :], X[:, t, :], rss[:, t:t + 1], None, ALU.mult).then_inc(rms_rows, 1)

            def gained(prefix, gain):
                for n in (1, 3):
                    job = f"{prefix}{n}"
                    dve.wait_ge(*full(job, l))
                    for k in range(2):
                        ins = v.tensor_scalar(XT[:, 2 * n + k, :], bank(job)[:, k * SEQ:(k + 1) * SEQ],
                                              gain[:, 2 * n + k:2 * n + k + 1], None, ALU.mult)
                    ins.then_inc(*took(job))

            scale_rows(0)
            gained("n1T", n1g)
            dve.wait_ge(consts2, 1)
            for n, (dst, gain, job) in enumerate(((st_qT, qg2, "q0"), (st_qT, qg2, "q1"), (st_kT, kg2, "k0"), (st_kT, kg2, "k1"))):
                dve.wait_ge(qk_rstd_ok, n + 1)
                v.scalar_tensor_tensor(dst[:, 2 * (n % 2):2 * (n % 2) + 2, :].rearrange("p a b -> p (a b)"), bank(job)[:, :],
                                       gain[:, 0:1], qk_rstd[:, n, :], ALU.mult, ALU.mult).then_inc(*took(job))
            dve.wait_ge(*read("xl0", l))
            dve.wait_ge(*read("xl1", l))
            for k in range(CONV):
                for c in range(4):
                    src, tap = xl_pad[:, c, k:k + SEQ], cw[:, k, c:c + 1]
                    if k == 0:
                        ins = v.tensor_scalar(conv_u[:, c, :], src, tap, cb[:, c:c + 1], ALU.mult, ALU.add)
                    else:
                        ins = v.scalar_tensor_tensor(conv_u[:, c, :], src, tap, conv_u[:, c, :], ALU.mult, ALU.add)
                if k < CONV - 1:
                    link(ins)
            ins.then_inc(conv_done, 1)
            dve.wait_ge(sp_lam, 1)
            link(v.tensor_scalar(sp_s, sp_e, 2.0, None, ALU.add))
            link(v.reciprocal(sp_s, sp_s))
            link(v.tensor_tensor(sp_s, sp_s, sp_e, ALU.mult))
            link(v.tensor_tensor(sp_s2, sp_s, sp_s, ALU.mult))
            link(v.tensor_scalar(sp_p, sp_s2, 1.0 / 15, None, ALU.mult))
            for n in (13, 11, 9, 7, 5, 3):
                link(v.scalar_tensor_tensor(sp_p, sp_p, 1.0 / n, sp_s2, ALU.add, ALU.mult))
            link(v.scalar_tensor_tensor(sp_p, sp_p, 1.0, sp_s, ALU.add, ALU.mult))
            link(v.tensor_scalar(sp_s, lam, -1.0, 0.0, ALU.mult, ALU.max))
            link(v.scalar_tensor_tensor(sp_p, sp_p, 2.0, sp_s, ALU.mult, ALU.add))
            link(v.tensor_scalar(sp_p, sp_p, -LRU_C, None, ALU.mult))

            def soft_parts(h):
                z = bank(f"z{h}")[:, 0:3 * P]
                dve.wait_ge(log1pd, h + 1)
                v.scalar_tensor_tensor(stS[:, h, :], z, 0.0, stW[:, h, :], ALU.max, ALU.add).then_inc(soft, 1)
                v.scalar_tensor_tensor(stL[:, h, :], z, 0.0, stW[:, h, :], ALU.min, ALU.subtract).then_inc(*took(f"z{h}"))

            def log_weights(h):
                dve.wait_ge(*read(f"z{h}", l))
                dve.wait_ge(*full(f"sfx{h}", l))
                v.tensor_tensor(stW[:, h, :], stL[:, h, :], bank(f"sfx{h}")[:, 0:3 * P], ALU.subtract
                                ).then_inc(*took(f"sfx{h}"))

            for h in range(ST_H):
                soft_parts(h)
                if h >= 1:
                    log_weights(h - 1)
            log_weights(ST_H - 1)
            dve.wait_ge(*read("rg1", l))
            dve.wait_ge(*read("ig1", l))
            v.tensor_scalar(rgT, rgT, 1.0, None, ALU.add)
            link(v.tensor_scalar(igT, igT, 1.0, None, ALU.add))
            v.reciprocal(rgT, rgT)
            link(v.reciprocal(igT, igT))
            for c in range(4):
                ins = v.tensor_scalar(rgT[:, c, :], rgT[:, c, :], sp_p[:, c:c + 1], None, ALU.mult)
            ins.then_inc(lru_la, 1)
            v.tensor_tensor(igT, igT, conv_u, ALU.mult)
            dve.wait_ge(*read("gl0", l))
            dve.wait_ge(*read("gl1", l))
            link(v.tensor_tensor(gel, glT, glT, ALU.mult))
            link(v.tensor_scalar(gel, gel, 0.044715, 1.0, ALU.mult, ALU.add))
            v.tensor_tensor(gel, gel, glT, ALU.mult).then_inc(gel_in, 1)
            dve.wait_ge(lru_at, 1)
            link(v.tensor_tensor(rgT, lruA, lruA, ALU.mult))
            v.scalar_tensor_tensor(lruT, rgT, 1.0, lruT, ALU.add, ALU.mult).then_inc(lru_m2, 1)
            dve.wait_ge(gel_t, 1)
            link(v.tensor_scalar(gel, gel, 0.5, 0.5, ALU.mult, ALU.add))
            link(v.tensor_tensor(gel, gel, glT, ALU.mult))
            dve.wait_ge(lru_sq, 1)
            link(v.tensor_tensor(igT, igT, lruT, ALU.mult))
            for c in range(4):
                ins = v.tensor_tensor_scan(lruH[:, c, :], lruA[:, c, :], igT[:, c, :], 0.0, ALU.mult, ALU.add)
            link(ins)
            v.tensor_tensor(XT[:, 4:8, :], lruH, gel, ALU.mult).then_inc(lru_mix, 1)

            def add_rows(prefix):
                for n in range(4):
                    job, part = f"{prefix}{n}", X[:, n // 2, (n % 2) * 512:(n % 2 + 1) * 512]
                    dve.wait_ge(*full(job, l))
                    v.tensor_tensor(part, part, bank(job)[:, :], ALU.add).then_inc(*took(job))

            add_rows("out")
            scale_rows(1)
            gained("n2T", n2g)
            with dve.Fori(0, N_CHUNK // 2) as m:
                for s in range(2):
                    dve.wait_ge(relu_done, 2 * m + s + 1)
                    v.tensor_tensor(hid[s].rearrange("p a b -> p (a b)"), hid[s].rearrange("p a b -> p (a b)"),
                                    bank(f"ff{s}")[:, :], ALU.mult).then_inc(*took(f"ff{s}"))
            add_rows("m")

    return nc


INPUTS = ["x", "w_in", "ret_gn_w", "swa_sinks", "mla_q_norm_w", "mla_kv_norm_w", "mla_w_uq", "mla_w_ukv", "w_out",
          "ln1_g", "ln1_b", "router_w", "router_bias", "exp_w_gate_up", "exp_w_down", "ln2_g", "ln2_b", "norm1_g_2",
          "w_in_2", "conv_w_2", "conv_b_2", "w_rg_2", "b_rg_2", "w_ig_2", "b_ig_2", "lru_lambda_2", "q_norm_g_2",
          "k_norm_g_2", "w_out_2", "norm2_g_2", "w_up_2", "w_down_2"]


def kernel(**inputs):
    import concourse.bacc as bacc
    from concourse.bass_utils import run_bass_kernel_spmd

    nc = bacc.Bacc("TRN2", target_bir_lowering=False, num_devices=1)
    arrays = {f"in_{n}": np.ascontiguousarray(inputs[n]) for n in INPUTS}
    arrays["in_tables"] = np.ascontiguousarray(np.concatenate(list(tables().values()), axis=1).astype(np.float32))
    aps = {n[3:]: nc.dram_tensor(n, v.shape, mybir.dt.from_np(v.dtype), kind="ExternalInput").ap() for n, v in arrays.items()}
    out = nc.dram_tensor("out", (1, SEQ, D), F32, kind="ExternalOutput").ap()
    build(nc, aps, out)
    r = run_bass_kernel_spmd(nc, [arrays], core_ids=[0])
    return r.results[0]["out"]
```

```python
from contextlib import ExitStack

import numpy as np

import concourse.bass as bass
from concourse import mybir

P = 128
SEQ, D, NL = 256, 1024, 2
T = SEQ // P
KD = D // P
HD = 64
RET_H, SWA_H, SWA_KV, MLA_H = 4, 6, 2, 6
Q_RANK, KV_RANK, NOPE, ROPE_D, MLA_VD = 384, 256, 64, 32, 64
DQ = NOPE + ROPE_D
N_EXP, N_GRP, D_EXP = 16, 4, 256
PER_GRP = N_EXP // N_GRP
ST_H, CONV, D_FF, LRU_W = 8, 4, 4096, 512
FF_CHUNK = 256
N_CHUNK = D_FF // FF_CHUNK
ALPHA = float((2 * NL) ** 0.25)
LN_EPS, RMS_EPS = 1e-5, 1e-6
NEG = -1e30
LRU_C = 8.0

C_RQ, C_RV, C_SQ, C_SK, C_SV, C_CQ, C_KR = 0, 512, 1024, 1408, 1536, 1664, 2304
N_LAT = Q_RANK + KV_RANK + ROPE_D
N_SWA = C_CQ - C_SQ

F32 = mybir.dt.float32
F32R = mybir.dt.float32r
ALU = mybir.AluOpType
ACT = mybir.ActivationFunctionType
AX = mybir.AxisListType

LAYER_JOBS = [
    ("xT0", 0), ("xT1", 1), ("xT2", 2), ("xT3", 3),
    ("lat0", 4), ("lat1", 5), ("lat2", 6),
    ("ret_q", 7), ("ret_k", 0), ("lat_ssq", 1),
    ("swa_q01", 2), ("swa_q2k", 3), ("ret_vg0", 7), ("ret_vg1", 0), ("swa_v", 2),
    ("ret_q_swap", 1), ("ret_k_swap", 3),
    ("mla_q0", 4), ("mla_q1", 5), ("mla_q2", 6),
    ("mla_k0", 2), ("mla_k1", 7), ("mla_k2", 0), ("mla_v0", 1), ("mla_v1", 3),
    ("mla_q_swap0", 4), ("mla_q_swap1", 5), ("mla_q_swap2", 6), ("mla_kr_swap", 2),
    ("ret_s0", 7), ("ret_s1", 0), ("ret_s2", 1), ("ret_s3", 3),
    ("swa_s1_0", 2), ("swa_s1_1", 4), ("swa_s1_2", 5), ("swa_s0_0", 6), ("swa_s0_1", 7),
    ("ret_o", 0),
    ("mla_s1_0", 1), ("mla_s1_1", 3), ("mla_s1_2", 2), ("mla_s0_0", 4), ("mla_s0_1", 5),
    ("swa_pT0", 6), ("swa_pT1", 7), ("swa_pT2", 6), ("swa_pT3", 7), ("swa_pT4", 6), ("swa_pT5", 7),
    ("ret_oT", 0), ("swa_o0", 4), ("swa_o1", 5),
    ("mla_pT0", 1), ("mla_pT1", 3), ("mla_pT2", 2), ("mla_pT3", 1), ("mla_pT4", 3), ("mla_pT5", 2),
    ("mla_o0", 6), ("mla_o1", 7),
    ("mix0", 0), ("mix1", 4), ("mix2", 5), ("mix3", 1),
    ("x1T0", 2), ("x1T1", 3), ("x1T2", 6), ("x1T3", 7),
    ("router", 0), ("gatesT", 1),
    ("y0", 0), ("y1", 1), ("y2", 2), ("y3", 3),
    ("gate0", 4), ("up0", 5), ("gate1", 6), ("up1", 7),
]
FINAL_JOBS = [
    ("n1T0", 0), ("n1T1", 1), ("n1T2", 2), ("n1T3", 3),
    ("gl0", 6), ("gl1", 7), ("xl0", 4), ("xl1", 5), ("q0", 0),
    ("rg0", 4), ("rg1", 5), ("ig0", 6), ("ig1", 7),
    ("q1", 1), ("k0", 2), ("k1", 3),
    ("ssq0", 4), ("ssq1", 5), ("v0", 6), ("ssq2", 7), ("v1", 4), ("ssq3", 5),
    ("z0", 6), ("z1", 7),
    ("sfx0", 4), ("z2", 6), ("sfx1", 5), ("z3", 7), ("sfx2", 4), ("z4", 6), ("sfx3", 5), ("z5", 7),
    ("sfx4", 4), ("z6", 6), ("sfx5", 5), ("z7", 7), ("sfx6", 4), ("sfx7", 5),
    ("att0", 0), ("att1", 1),
    ("out0", 2), ("out1", 3), ("out2", 6), ("out3", 7),
    ("n2T0", 0), ("n2T1", 1), ("n2T2", 2), ("n2T3", 3),
    ("m0", 0), ("m1", 1), ("m2", 2), ("m3", 3),
    ("ff0", 4), ("ff1", 5),
]
REPEATED = {"gate0": N_EXP // 2, "up0": N_EXP // 2, "gate1": N_EXP // 2, "up1": N_EXP // 2,
            "ff0": N_CHUNK // 2, "ff1": N_CHUNK // 2}


def place_jobs(jobs):
    count, where = [0] * 8, {}
    for name, bank in jobs:
        where[name] = (bank, count[bank])
        count[bank] += REPEATED.get(name, 1)
    return where, count


def tables():
    pos = np.arange(SEQ, dtype=np.float32)
    row = np.arange(P)

    def rope_table(dim, first_row):
        half = dim // 2
        inv = (10000.0 ** (-np.arange(0, dim, 2, dtype=np.float32) / np.float32(dim))).astype(np.float32)
        ang = (pos[None, :] * inv[(row - first_row) % half][:, None]).astype(np.float32)
        sign = np.where((row - first_row) % dim < half, -1.0, 1.0)[:, None]
        return np.cos(ang.astype(np.float64)), np.sin(ang.astype(np.float64)) * sign

    def swap_table(dim):
        swap = np.zeros((P, P))
        swap[row, np.where(row % dim < dim // 2, row + dim // 2, row - dim // 2)] = 1.0
        return swap

    cos_r, sin_r = rope_table(HD, 0)
    cos_m, sin_m = rope_table(ROPE_D, NOPE)
    i, j = row[:, None], row[None, :]
    decay = np.zeros((P, RET_H, 3 * P))
    for h in range(RET_H):
        log_g = np.log(1.0 - 2.0 ** (-5.0 - h))
        for block, shift in ((0, 0), (1, P), (2, 0)):
            rel = (j + shift) - i
            decay[:, h, block * P:(block + 1) * P] = np.where(rel >= 0, np.exp(rel * log_g), 0.0) * HD ** -0.5
    low = (i // HD == j // HD).astype(np.float64)
    tie = np.zeros((PER_GRP, PER_GRP))
    for e in range(PER_GRP):
        tie[e, :e] = 1.0
    return {
        "ident": np.eye(P), "ones": np.ones((P, P)), "half_ones": low,
        "swap_r": swap_table(HD), "swap_m": swap_table(ROPE_D),
        "cos_r": cos_r, "sin_r": sin_r, "cos_m": cos_m, "sin_m": sin_m,
        "decay": decay.reshape(P, -1),
        "mask_swa": np.concatenate([np.where(j > i, 0.0, NEG), np.where(j <= i, 0.0, NEG)], 1),
        "mask_mla": np.concatenate([np.zeros((P, P)), np.where(j <= i, 0.0, NEG)], 1),
        "later": (i > j).astype(np.float64),
        "before": (i < j).astype(np.float64),
        "tie": np.broadcast_to(tie.reshape(1, -1), (P, PER_GRP * PER_GRP)),
        "ln_eps": np.full((P, 1), LN_EPS), "rms_eps": np.full((P, 1), RMS_EPS), "one": np.ones((P, 1)),
    }


TABLE_AT, TABLE_W = {}, 0
for _name, _t in tables().items():
    TABLE_AT[_name] = (TABLE_W, _t.shape[1])
    TABLE_W += _t.shape[1]


class Link:

    def __init__(self, eng, sem, start=0):
        self.eng, self.sem, self.start, self.n = eng, sem, start, 0

    def __call__(self, ins):
        ins.then_inc(self.sem, 1)
        self.n += 1
        self.eng.wait_ge(self.sem, self.start + self.n)


def build(nc, a, out):
    ctx = ExitStack()
    with ctx:
        def sb(name, shape):
            return ctx.enter_context(nc.sbuf_tensor(name, shape, F32))

        def sem(name):
            return ctx.enter_context(nc.semaphore(name))

        place = {}

        def region(name, shape):
            place[name] = nc.sbuf_base
            return sb(name, shape)

        def over(name, where, word, shape):
            return nc.alloc_sbuf_tensor_at(name, shape, F32R, offset=place[where] + 4 * word)

        tab = sb("tab", [P, TABLE_W])
        X = sb("X", [P, T, D])
        XT = region("XT", [P, KD, SEQ])
        LNB = sb("LNB", [P, 2, D])
        WA = region("WA", [P, 9472])
        WE = sb("WE", [P, 12480])
        WB = region("WB", [P, KD * D])
        AC = region("AC", [P, 10240])
        small = sb("small", [P, 1400])

        UNIT = 2048
        W_LAT_END = KD * N_LAT
        WH = [over("WH0", "AC", 0, [P, UNIT]), over("WH1", "AC", 2 * UNIT, [P, UNIT]), over("WH2", "AC", 4 * UNIT, [P, UNIT]),
              over("WH3", "WB", 0, [P, UNIT])]
        WL = [over("WL0", "AC", UNIT, [P, UNIT]), over("WL1", "AC", 3 * UNIT, [P, UNIT]), over("WL2", "WA", W_LAT_END, [P, UNIT]),
              over("WL3", "WB", UNIT, [P, UNIT])]
        XTH = over("XTH", "WA", W_LAT_END + UNIT, [P, KD, SEQ])
        XTL = over("XTL", "WB", 3 * UNIT, [P, KD, SEQ])
        HIDH = [over(f"HIDH{s}", "XT", s * 1024, [P, 2, SEQ]) for s in range(2)]
        HIDL = [over(f"HIDL{s}", "XT", s * 1024 + 512, [P, 2, SEQ]) for s in range(2)]
        WH_up, WL_up = ([w[:, :].rearrange("p (k n) -> p k n", k=KD) for w in part] for part in (WH, WL))
        WH_dn, WL_dn = ([w[:, :].rearrange("p (c n) -> p c n", c=2) for w in part] for part in (WH, WL))

        def tb(name):
            o, w = TABLE_AT[name]
            return tab[:, o:o + w]

        class Arena:
            def __init__(self, tensor, at=0):
                self.t, self.at, self.size = tensor, at, tensor[:, :].shape[1]

            def take(self, *shape):
                w = int(np.prod(shape))
                v = self.t[:, self.at:self.at + w]
                self.at += w
                assert self.at <= self.size, (self.at, self.size)
                if len(shape) == 2:
                    v = v.rearrange("p (a b) -> p a b", b=shape[1])
                elif len(shape) == 3:
                    v = v.rearrange("p (a b c) -> p a b c", b=shape[1], c=shape[2])
                return v

        ar = Arena(WA)
        w_lat, w_rqk = ar.take(KD, N_LAT), ar.take(KD, C_RV)
        ar = Arena(WE)
        w_rvg, w_swa = ar.take(KD, 512), ar.take(KD, N_SWA)
        w_uq, w_ukv = ar.take(Q_RANK // P, MLA_H * DQ), ar.take(KV_RANK // P, MLA_H * (NOPE + MLA_VD))
        w_gu, w_dn = [], []
        for s in range(2):
            ar = Arena(WE, s * 6240)
            w_gu.append(ar.take(KD, 2 * D_EXP))
            w_dn.append(ar.take(D_EXP // P, D))
        w_gate, w_up = ([w[:, :, n * D_EXP:(n + 1) * D_EXP] for w in w_gu] for n in range(2))
        w_out = Arena(WB).take(KD, D)
        ar = Arena(WA)
        mla_p1, mla_p0, mla_pT = ar.take(MLA_H, SEQ), ar.take(MLA_H, P), ar.take(MLA_H, 3 * P)
        swa_p1, swa_p0, swa_pT = ar.take(SWA_H, SEQ), ar.take(SWA_H, P), ar.take(SWA_H, 3 * P)
        ar = Arena(WB)
        lat_sq, lat_n, lat_rstd = ar.take(5, SEQ), ar.take(5, SEQ), ar.take(2, SEQ)
        rope_m, rope_r, kr_cos = ar.take(MLA_H, SEQ), ar.take(4, SEQ), ar.take(SEQ)
        kr_sin = ar.take(SEQ)
        ar = Arena(WB)
        gates_b = ar.take(N_EXP, SEQ)
        sig = [ar.take(512) for _ in range(2)]
        gatesT = ar.take(SEQ)
        assert ar.at <= 3 * UNIT
        ar = Arena(AC)
        ret_qT, ret_kT = ar.take(2, SEQ), ar.take(2, SEQ)
        swa_qT, swa_kT = ar.take(3, SEQ), ar.take(SEQ)
        ret_v, ret_g, swa_v = ar.take(T, 256), ar.take(T, 256), ar.take(T, P)
        mla_qT, mla_kT, mla_v = ar.take(MLA_H, SEQ), ar.take(MLA_H, SEQ), ar.take(T, MLA_H * MLA_VD)
        krT, ret_pT = ar.take(SEQ), ar.take(RET_H, 3 * P)
        ret_c, ret_sq = ar.take(T * RET_H, HD), ar.take(T * RET_H, HD)
        ar = Arena(AC)
        st_qT, st_kT, st_v = ar.take(4, SEQ), ar.take(4, SEQ), ar.take(T, 512)
        xl_pad = ar.take(4, SEQ + CONV - 1)
        conv_u, glT, rgT, igT, lruA = (ar.take(4, SEQ) for _ in range(5))
        lruT = Arena(AC, 3 * 1024).take(4, SEQ)
        xn = LNB[:, :, :]
        gel, lruH = LNB[:, 0, :].rearrange("p (a b) -> p a b", b=SEQ), LNB[:, 1, :].rearrange("p (a b) -> p a b", b=SEQ)
        ar = Arena(WB)
        qk_sq, qk_rstd = ar.take(4, 512), ar.take(4, 512)
        square_out = WB[:, 0:D], WA[:, 0:D]
        ar = Arena(WA)
        w_gl2 = ar.take(KD, 512)
        w_k2 = Arena(WA, W_LAT_END).take(KD, 512)
        ar = Arena(WA)
        stS, stL, stW = ar.take(ST_H, 3 * P), ar.take(ST_H, 3 * P), ar.take(ST_H, 3 * P)
        ar = Arena(WE)
        w_vx2, w_q2 = ar.take(KD, 1024), ar.take(KD, 512)
        w_bd = sb("w_bd", [P, 2, 4, P])
        ar = Arena(small)
        qn_g, kvn_g, gn_b, sink_b = ar.take(3), ar.take(2), ar.take(256), ar.take(SWA_H)
        router, rbias = ar.take(KD, N_EXP), ar.take(N_EXP)
        mx = {"swa": ar.take(T, 6), "mla": ar.take(T, 6)}
        nmx = {"swa": ar.take(T, 6), "mla": ar.take(T, 6)}
        psm = {"swa": ar.take(T, 6), "mla": ar.take(T, 6)}
        rin = {"swa": ar.take(T, 6), "mla": ar.take(T, 6)}
        sk_e = ar.take(T, 6)
        gmu, gvar, grs = ar.take(8), ar.take(8), ar.take(8)
        st6, mv2, lrs = ar.take(T, 2 * 6), ar.take(T, 2), ar.take(T, 1)
        sc, bi, pr, gs = ar.take(32), ar.take(8, 4), ar.take(8, 6), ar.take(8)
        c1, c2 = ar.take(8, 4, 4), ar.take(8, 4, 4)
        g1, g2 = ar.take(2, 4, 4), ar.take(2, 4, 4)
        gsel, esel, gden, gates = ar.take(8), ar.take(8, 4), ar.take(2), ar.take(2, N_EXP)
        n1g, n2g = ar.take(KD), ar.take(KD)
        qg2, kg2 = ar.take(1), ar.take(1)
        cw, cb = ar.take(CONV, 4), ar.take(4)
        brg, big, lam = ar.take(4), ar.take(4), ar.take(4)
        sp_e, sp_s, sp_s2, sp_p = ar.take(4), ar.take(4), ar.take(4), ar.take(4)
        rss, marks = ar.take(T), ar.take(8 + T + 2)
        ident, ones = tb("ident"), tb("ones")
        decay = tb("decay").rearrange("p (h c) -> p h c", h=RET_H)
        tie = tb("tie").rearrange("p (a b) -> p a b", b=PER_GRP)
        psum = [ctx.enter_context(nc.psum_tensor(f"bank{b}", [P, 512], F32)) for b in range(8)]
        gates_dram = nc.dram_tensor("gates_scratch", [NL, N_EXP, SEQ], F32, kind="Internal").ap()

        psum_full = [sem(f"psum_full{b}") for b in range(8)]
        psum_read = [sem(f"psum_read{b}") for b in range(8)]
        in_layer, per_layer = place_jobs(LAYER_JOBS)
        in_final, _ = place_jobs(FINAL_JOBS)

        def count_of(name, l):
            bank, n = (in_layer if name in in_layer else in_final)[name]
            return bank, l * per_layer[bank] + n

        def free(name, l, m=0):
            bank, n = count_of(name, l)
            return psum_read[bank], n + m + 1

        def full(name, l, m=0):
            bank, n = count_of(name, l)
            return psum_full[bank], n + m + 1

        def read(name, l, m=0):
            bank, n = count_of(name, l)
            return psum_read[bank], n + m + 2

        def bank(name):
            return psum[(in_layer if name in in_layer else in_final)[name][0]]

        def made(name):
            return psum_full[(in_layer if name in in_layer else in_final)[name][0]], 1

        def took(name):
            return psum_read[(in_layer if name in in_layer else in_final)[name][0]], 1

        ident_in, tab_in, router_in, final_in, bd_in = (sem(n) for n in ("ident_in", "tab_in", "router_in", "final_in", "bd_in"))
        x_in = [sem(f"x_in{t}") for t in range(T)]
        wlat_in, wrqk_in, wrvg_in, wswa_in, wup_in, wout_in = (
            sem(n) for n in ("wlat_in", "wrqk_in", "wrvg_in", "wswa_in", "wup_in", "wout_in"))
        norms_in, ln1_in, ln2_in, gates_in, gates_out = (sem(n) for n in ("norms_in", "ln1_in", "ln2_in", "gates_in", "gates_out"))
        gu_in, dn_in = [sem(f"gu_in{s}") for s in range(2)], [sem(f"dn_in{s}") for s in range(2)]
        x_ready = sem("x_ready")
        lat_squared, kr_copied = sem("lat_squared"), sem("kr_copied")
        rows_turned = sem("rows_turned")
        rstd_ready = sem("rstd_ready")
        ret_cos, ret_roped = sem("ret_cos"), sem("ret_roped")
        ret_gate_w, q_roped, k_roped = sem("ret_gate_w"), sem("q_roped"), sem("k_roped")
        maxed = {n: sem(f"{n}_maxed") for n in ("swa", "mla")}
        expd = {n: sem(f"{n}_expd") for n in ("swa", "mla")}
        normed = {n: sem(f"{n}_normed") for n in ("swa", "mla")}
        gn_squared, gn_var, gn_rstd, ret_out = (sem(n) for n in ("gn_squared", "gn_var", "gn_rstd", "ret_out"))
        ln_var, ln_centred, ln_rstd, x1_ready = (sem(n) for n in ("ln_var", "ln_centred", "ln_rstd", "x1_ready"))
        gates_ready, expert_used = sem("gates_ready"), sem("expert_used")
        dve_link, act_link, pool_link = sem("dve_link"), sem("act_link"), sem("pool_link")
        high_made, low_made = ([sem(f"{n}_made{s}") for s in range(4)] for n in ("high", "low"))
        xt_high, xt_low = sem("xt_high"), sem("xt_low")
        hid_ready = sem("hid_ready")
        dve_moe, dve_fin, act_fin = sem("dve_moe"), sem("dve_fin"), sem("act_fin")
        wq_in, wk_in, wvx_in, wgl_in = (sem(n) for n in ("wq_in", "wk_in", "wvx_in", "wgl_in"))
        rms_rstd, rms_rows = sem("rms_rstd"), sem("rms_rows")
        qk_squared, qk_rstd_ok = sem("qk_squared"), sem("qk_rstd_ok")
        bd_zero, pad_zero, conv_done = sem("bd_zero"), sem("pad_zero"), sem("conv_done")
        consts2 = sem("consts2")
        log1pd, soft, masked_sp = sem("log1pd"), sem("soft"), sem("masked_sp")
        wexp, w_masked = sem("wexp"), sem("w_masked")
        lru_la, lru_at, lru_m2, lru_sq, gel_in, gel_t, lru_mix, sp_lam = (
            sem(n) for n in ("lru_la", "lru_at", "lru_m2", "lru_sq", "gel_in", "gel_t", "lru_mix", "sp_lam"))
        up_in, down_in = [sem(f"up_in{s}") for s in range(2)], [sem(f"down_in{s}") for s in range(2)]
        ff_used, relu_done, stored = sem("ff_used"), sem("relu_done"), sem("stored")

        def token(t):
            return slice(t * P, (t + 1) * P)

        def spread(ap, axis, shape):
            return ap.unsqueeze(axis).to_broadcast(shape)

        DVE_LINKS, ACT_LINKS, POOL_LINKS, MOE_LINKS = 32, 5, 2, 2

        SLOT_UNITS = (N_EXP + 1, N_EXP, N_EXP - 1, 0)

        def unit(slot, l, e):
            return l * SLOT_UNITS[slot] + e + 1 if SLOT_UNITS[slot] else e + 1

        def hidden(l, e):
            return l * N_EXP + e + 2

        block = ctx.enter_context(nc.Block())

        @block.sync
        def _(sp):
            for t in range(T):
                sp.dma_start(X[:, t, :], a["x"][0, t * P:(t + 1) * P, :]).then_inc(x_in[t], 16)
            with sp.Fori(0, NL) as l:
                w = a["w_in"][bass.ds(l, 1)].rearrange("o (p k) n -> p (o k) n", k=KD)
                sp.dma_start(w_lat, w[:, :, C_CQ:C_CQ + N_LAT]).then_inc(wlat_in, 16)
                sp.wait_ge(psum_read[3], l * per_layer[3] + 1)
                for m in range(3):
                    for g in range(2):
                        sp.dma_start(w_swa[:, :, m * P + g * HD:m * P + (g + 1) * HD],
                                     w[:, :, C_SQ + (3 * g + m) * HD:C_SQ + (3 * g + m + 1) * HD]).then_inc(wswa_in, 16)
                sp.dma_start(w_rqk, w[:, :, C_RQ:C_RV]).then_inc(wrqk_in, 16)
                sp.dma_start(w_swa[:, :, C_SK - C_SQ:N_SWA], w[:, :, C_SK:C_CQ]).then_inc(wswa_in, 16)
                sp.dma_start(w_rvg, w[:, :, C_RV:C_SQ]).then_inc(wrvg_in, 16)
                sp.dma_start(w_uq, a["mla_w_uq"][bass.ds(l, 1)].rearrange("o (c p) n -> p (o c) n", p=P)).then_inc(wup_in, 16)
                sp.dma_start(w_ukv, a["mla_w_ukv"][bass.ds(l, 1)].rearrange("o (c p) n -> p (o c) n", p=P)).then_inc(wup_in, 16)
                sp.wait_ge(k_roped, l + 2)
                sp.dma_start(w_out, a["w_out"][bass.ds(l, 1)].rearrange("o (c p) n -> p (o c) n", p=P)).then_inc(wout_in, 16)

                def load_gate_up(e, s):
                    sp.dma_start(w_gu[s], a["exp_w_gate_up"][bass.ds(l, 1), bass.ds(e, 1)].rearrange(
                        "o e (p k) n -> p (o e k) n", k=KD)).then_inc(gu_in[s], 16)

                def load_down(e, s):
                    sp.dma_start(w_dn[s], a["exp_w_down"][bass.ds(l, 1), bass.ds(e, 1)].rearrange(
                        "o e (c p) n -> p (o e c) n", p=P)).then_inc(dn_in[s], 16)

                for s in range(2):
                    load_gate_up(s, s)
                    load_down(s, s)
                sp.wait_ge(x1_ready, (l + 1) * T)
                sp.dma_start(LNB[:, 0, :], a["ln2_g"][bass.ds(l, 1)].rearrange("o n -> (o n)").partition_broadcast(P)).then_inc(ln2_in, 16)
                sp.dma_start(LNB[:, 1, :], a["ln2_b"][bass.ds(l, 1)].rearrange("o n -> (o n)").partition_broadcast(P)).then_inc(ln2_in, 16)
                with sp.Fori(1, N_EXP // 2) as m:
                    for s in range(2):
                        sp.wait_ge(low_made[1], unit(1, l, 2 * m + (s - 2)))
                        load_gate_up(2 * m + s, s)
                        sp.wait_ge(low_made[2], unit(2, l, 2 * m + (s - 2)))
                        load_down(2 * m + s, s)
            w2 = a["w_in_2"][0].rearrange("(p k) n -> p k n", k=KD)
            sp.dma_start(w_gl2, w2[:, :, 2048:2560]).then_inc(wgl_in, 16)
            sp.wait_ge(psum_read[3], NL * per_layer[3] + 1)
            sp.dma_start(w_vx2, w2[:, :, 1024:2048]).then_inc(wvx_in, 16)
            sp.dma_start(w_q2, w2[:, :, 0:512]).then_inc(wq_in, 16)
            sp.dma_start(w_k2, w2[:, :, 512:1024]).then_inc(wk_in, 16)
            for n in ("q0", "q1", "k0", "k1"):
                sp.wait_ge(*read(n, NL))
            sp.dma_start(w_out, a["w_out_2"][0].rearrange("(c p) n -> p c n", p=P)).then_inc(wout_in, 16)
            sp.wait_ge(*full("v1", NL))

            def load_up(c, s):
                sp.dma_start(w_gu[s][:, :, 0:FF_CHUNK], a["w_up_2"][0].rearrange("(p k) n -> p k n", k=KD)[
                    :, :, bass.ds(c * FF_CHUNK, FF_CHUNK)]).then_inc(up_in[s], 16)

            def load_ff_down(c, s):
                sp.dma_start(w_dn[s], a["w_down_2"][0].rearrange("(g c p) n -> g p c n", c=2, p=P)[
                    bass.ds(c, 1)].rearrange("g p c n -> p (g c) n")).then_inc(down_in[s], 16)

            for s in range(2):
                load_up(s, s)
                load_ff_down(s, s)
            with sp.Fori(1, N_CHUNK // 2) as m:
                for s in range(2):
                    sp.wait_ge(low_made[s], unit(s, NL, m - 1))
                    load_up(2 * m + s, s)
                    sp.wait_ge(low_made[2 + s], unit(2 + s, NL, m - 1))
                    load_ff_down(2 * m + s, s)
            o = out.rearrange("o (t p) d -> p (o t) d", p=P)
            for t in range(T):
                sp.wait_ge(*read(f"m{2 * t}", NL))
                sp.wait_ge(*read(f"m{2 * t + 1}", NL))
                sp.dma_start(o[:, t, :], X[:, t, :]).then_inc(stored, 16)
            sp.wait_ge(stored, 16 * T)

        @block.gpsimd
        def _(pool):
            with nc.allow_non_contiguous_dma(reason="small vectors"):
                pool.dma_start(router, a["router_w"].rearrange("(p k) e -> p k e", k=KD)).then_inc(router_in, 16)
                pool.dma_start(rbias, a["router_bias"].partition_broadcast(P)).then_inc(router_in, 16)
            pool.wait_ge(tab_in, 16)
            nc.gpsimd.memset(marks[:, 8 + T:9 + T], 0.0).then_inc(k_roped, 1)

            def low_part(slot, raw, n):
                pool.wait_ge(high_made[slot], n)
                nc.gpsimd.tensor_tensor(WL_up[slot], raw, WH_up[slot].bitcast(F32), ALU.subtract).then_inc(low_made[slot], 1)

            with pool.Fori(0, NL) as l:
                link = Link(pool, pool_link, l * POOL_LINKS)
                with nc.allow_non_contiguous_dma(reason="small vectors"):
                    pool.wait_ge(x_ready, (l + 1) * T)
                    pool.dma_start(qn_g, a["mla_q_norm_w"][bass.ds(l, 1)].rearrange("o (c p) -> p (o c)", p=P)).then_inc(norms_in, 16)
                    pool.dma_start(kvn_g, a["mla_kv_norm_w"][bass.ds(l, 1)].rearrange("o (c p) -> p (o c)", p=P)).then_inc(norms_in, 16)
                    pool.dma_start(gn_b, a["ret_gn_w"][bass.ds(l, 1)].rearrange("o n -> (o n)").partition_broadcast(P)).then_inc(norms_in, 16)
                    pool.dma_start(sink_b, a["swa_sinks"][bass.ds(l, 1)].rearrange("o n -> (o n)").partition_broadcast(P)).then_inc(norms_in, 16)
                pool.dma_start(LNB[:, 0, :], a["ln1_g"][bass.ds(l, 1)].rearrange("o n -> (o n)").partition_broadcast(P)).then_inc(ln1_in, 16)
                pool.dma_start(LNB[:, 1, :], a["ln1_b"][bass.ds(l, 1)].rearrange("o n -> (o n)").partition_broadcast(P)).then_inc(ln1_in, 16)
                pool.wait_ge(k_roped, l + 1)
                for n, (src, name) in enumerate(((ret_qT, "ret_q"), (ret_kT, "ret_k"))):
                    pool.wait_ge(*read(name, l))
                    nc.gpsimd.tensor_tensor(rope_r[:, 2 * n:2 * n + 2, :], src, spread(tb("cos_r"), 1, [P, 2, SEQ]),
                                            ALU.mult).then_inc(ret_cos, 1)
                pool.wait_ge(norms_in, (l + 1) * 64)
                for t in range(T):
                    pool.wait_ge(*read(f"ret_vg{t}", l))
                nc.gpsimd.tensor_tensor(ret_g, ret_g, spread(gn_b, 1, [P, T, 256]), ALU.mult).then_inc(ret_gate_w, 1)
                rows = slice(NOPE, DQ)
                cos, shape = tb("cos_m")[rows], [ROPE_D, MLA_H, SEQ]
                pool.wait_ge(ret_gate_w, l + 1)
                for n in range(3):
                    pool.wait_ge(*full(f"mla_q_swap{n}", l))
                link(nc.gpsimd.tensor_tensor(mla_qT[rows], mla_qT[rows], spread(cos, 1, shape), ALU.mult))
                for n in range(3):
                    pool.wait_ge(*read(f"mla_q_swap{n}", l))
                nc.gpsimd.tensor_tensor(mla_qT[rows], mla_qT[rows], rope_m[rows], ALU.add).then_inc(q_roped, 1)
                link(nc.gpsimd.tensor_tensor(kr_cos[rows], krT[rows], cos, ALU.mult))
                pool.wait_ge(*read("mla_kr_swap", l))
                nc.gpsimd.tensor_tensor(mla_kT[rows], spread(kr_cos[rows], 1, shape), spread(kr_sin[rows], 1, shape),
                                        ALU.add).then_inc(k_roped, 1)
                assert link.n == POOL_LINKS

                low_part(0, w_gate[0], unit(0, l, 0))
                low_part(1, w_up[0], unit(1, l, 0))
                with pool.Fori(1, N_EXP // 2) as m:
                    for e, s in ((2 * m - 1, 1), (2 * m, 0)):
                        low_part(0, w_gate[s], unit(0, l, e))
                        low_part(1, w_up[s], unit(1, l, e))
                low_part(0, w_gate[1], unit(0, l, N_EXP - 1))
                low_part(1, w_up[1], unit(1, l, N_EXP - 1))
            pool.wait_ge(k_roped, NL + 1)
            nc.gpsimd.memset(w_bd[:, :, :, :], 0.0).then_inc(bd_zero, 1)
            pool.wait_ge(bd_zero, 1)
            with nc.allow_non_contiguous_dma(reason="small vectors"):
                for n, name in enumerate(("w_rg_2", "w_ig_2")):
                    for half in range(2):
                        pool.dma_start(w_bd[half * HD:(half + 1) * HD, n, :, half * HD:(half + 1) * HD],
                                       a[name][0].rearrange("(c h) i o -> h i c o", h=2)[half]).then_inc(bd_in, 16)
                n_final = 0
                for dst, src in (
                    (n1g, a["norm1_g_2"].rearrange("o (p k) -> p (o k)", k=KD)),
                    (n2g, a["norm2_g_2"].rearrange("o (p k) -> p (o k)", k=KD)),
                    (qg2[0:HD], a["q_norm_g_2"].rearrange("o p -> p o")), (qg2[HD:P], a["q_norm_g_2"].rearrange("o p -> p o")),
                    (kg2[0:HD], a["k_norm_g_2"].rearrange("o p -> p o")), (kg2[HD:P], a["k_norm_g_2"].rearrange("o p -> p o")),
                    (cb, a["conv_b_2"].rearrange("o (c p) -> p (o c)", p=P)),
                    (brg, a["b_rg_2"].rearrange("o (c p) -> p (o c)", p=P)),
                    (big, a["b_ig_2"].rearrange("o (c p) -> p (o c)", p=P)),
                    (lam, a["lru_lambda_2"].rearrange("o (c p) -> p (o c)", p=P)),
                ) + tuple((cw[:, k, :], a["conv_w_2"][0, k].rearrange("(c p) -> p c", p=P)) for k in range(CONV)):
                    pool.dma_start(dst, src).then_inc(final_in, 16)
                    n_final += 1
            assert n_final == 14
            strict = tb("before")

            def mask_weights(h):
                pool.wait_ge(wexp, h + 1)
                v = stW[:, h, :].rearrange("p (b c) -> p b c", c=P)[:, 0:3:2, :]
                nc.gpsimd.tensor_tensor(v, v, spread(strict, 1, [P, 2, P]), ALU.mult).then_inc(w_masked, 1)

            for h in range(ST_H):
                pool.wait_ge(soft, h + 1)
                v = stS[:, h, :].rearrange("p (b c) -> p b c", c=P)[:, 0:3:2, :]
                nc.gpsimd.tensor_tensor(v, v, spread(strict, 1, [P, 2, P]), ALU.mult).then_inc(masked_sp, 1)
                if h >= 2:
                    mask_weights(h - 2)
            for h in range(ST_H - 2, ST_H):
                mask_weights(h)
            with pool.Fori(0, N_CHUNK // 2) as m:
                for s in range(2):
                    low_part(s, w_gate[s], unit(s, NL, m))

        @block.scalar
        def _(act):
            act.dma_start(ident, a["tables"][:, 0:P]).then_inc(ident_in, 16)
            act.dma_start(tab[:, P:], a["tables"][:, P:]).then_inc(tab_in, 16)

            def softmax_exp(name, l, p1, p0, scale):
                act.wait_ge(maxed[name], l + 1)
                for h in range(6):
                    nc.scalar.activation(p0[:, h, :], p0[:, h, :], ACT.Exp, bias=nmx[name][:, 0, h:h + 1], scale=scale,
                                         accum_out=psm[name][:, 0, h:h + 1])
                    ins = nc.scalar.activation(p1[:, h, :], p1[:, h, :], ACT.Exp, bias=nmx[name][:, 1, h:h + 1],
                                               scale=scale, accum_out=psm[name][:, 1, h:h + 1])
                if name == "swa":
                    ins = nc.scalar.activation(sk_e, sk_e, ACT.Exp)
                ins.then_inc(expd[name], 1)

            def rstd(link, dst, src, scale, eps, done):
                link(nc.scalar.activation(dst, src, ACT.Ln, bias=tb(eps), scale=scale))
                nc.scalar.activation(dst, dst, ACT.Exp, scale=-0.5).then_inc(done, 1)

            def high_up(slot, raw):
                nc.scalar.copy(WH_up[slot], raw).then_inc(high_made[slot], 1)

            def high_down(slot, s, loaded, n):
                act.wait_ge(loaded[s], n * 16)
                nc.scalar.copy(WH_dn[slot], w_dn[s]).then_inc(high_made[slot], 1)

            def split_xt(prefix, l):
                for n in range(4):
                    act.wait_ge(*read(f"{prefix}{n}", l))
                    nc.scalar.copy(XTH[:, 2 * n:2 * n + 2, :], XT[:, 2 * n:2 * n + 2, :]).then_inc(xt_high, 1)

            with act.Fori(0, NL) as l:
                link = Link(act, act_link, l * ACT_LINKS)
                for n in (0, 2):
                    act.wait_ge(*full(f"xT{n}", l))
                    nc.scalar.copy(XT[:, 2 * n:2 * n + 2, :], bank(f"xT{n}")[:, :]).then_inc(*took(f"xT{n}"))
                for n, w in ((0, 512), (1, 512), (2, 256)):
                    act.wait_ge(*full(f"lat{n}", l))
                    nc.scalar.activation(lat_sq[:, 2 * n:2 * n + w // SEQ, :], bank(f"lat{n}")[:, 0:w],
                                         ACT.Square).then_inc(lat_squared, 1)
                turn = slice(NOPE, DQ)
                nc.scalar.copy(krT[turn, :], bank("lat2")[turn, SEQ:2 * SEQ]).then_inc(kr_copied, 1)
                act.wait_ge(*full("ret_q", l))
                nc.scalar.copy(ret_qT, bank("ret_q")[:, :]).then_inc(*took("ret_q"))
                act.wait_ge(*full("ret_k", l))
                nc.scalar.copy(ret_kT, bank("ret_k")[:, :]).then_inc(*took("ret_k"))
                act.wait_ge(tab_in, 16)
                act.wait_ge(*full("lat_ssq", l))
                nc.scalar.activation(lat_rstd[:, 0, :], bank("lat_ssq")[:, 0:SEQ], ACT.Ln, bias=tb("rms_eps"), scale=1.0 / Q_RANK)
                nc.scalar.activation(lat_rstd[:, 1, :], bank("lat_ssq")[:, SEQ:2 * SEQ], ACT.Ln, bias=tb("rms_eps"),
                                     scale=1.0 / KV_RANK).then_inc(*took("lat_ssq"))
                act.wait_ge(*read("lat_ssq", l))
                nc.scalar.activation(lat_rstd, lat_rstd, ACT.Exp, scale=-0.5).then_inc(rstd_ready, 1)
                act.wait_ge(*full("swa_q01", l))
                nc.scalar.mul(swa_qT[:, 0:2, :], bank("swa_q01")[:, :], HD ** -0.5).then_inc(*took("swa_q01"))
                act.wait_ge(*full("swa_q2k", l))
                nc.scalar.mul(swa_qT[:, 2, :], bank("swa_q2k")[:, 0:SEQ], HD ** -0.5)
                nc.scalar.copy(swa_kT, bank("swa_q2k")[:, SEQ:2 * SEQ]).then_inc(*took("swa_q2k"))
                for t in range(T):
                    act.wait_ge(*full(f"ret_vg{t}", l))
                    nc.scalar.copy(ret_v[:, t, :], bank(f"ret_vg{t}")[:, 0:256])
                    nc.scalar.activation(ret_g[:, t, :], bank(f"ret_vg{t}")[:, 256:512], ACT.Silu).then_inc(*took(f"ret_vg{t}"))
                act.wait_ge(*full("swa_v", l))
                nc.scalar.copy(swa_v, bank("swa_v")[:, 0:T * P]).then_inc(*took("swa_v"))
                for n in range(3):
                    act.wait_ge(*full(f"mla_q{n}", l))
                    nc.scalar.copy(mla_qT[0:DQ, 2 * n:2 * n + 2, :], bank(f"mla_q{n}")[0:DQ, :]).then_inc(*took(f"mla_q{n}"))
                for t in range(T):
                    act.wait_ge(*full(f"mla_v{t}", l))
                    nc.scalar.copy(mla_v[:, t, :], bank(f"mla_v{t}")[:, 0:MLA_H * MLA_VD]).then_inc(*took(f"mla_v{t}"))
                softmax_exp("swa", l, swa_p1, swa_p0, 1.0)
                act.wait_ge(*read("ret_o", l))
                nc.scalar.activation(ret_sq, ret_c, ACT.Square).then_inc(gn_squared, 1)
                softmax_exp("mla", l, mla_p1, mla_p0, DQ ** -0.5)
                act.wait_ge(gn_var, l + 1)
                rstd(link, grs, gvar, 1.0 / HD, "ln_eps", gn_rstd)
                for h in range(0, 6, 2):
                    act.wait_ge(*full(f"swa_pT{h}", l))
                    nc.scalar.copy(swa_pT[:, h, :], bank(f"swa_pT{h}")[:, 0:3 * P]).then_inc(*took(f"swa_pT{h}"))
                act.wait_ge(*full("ret_oT", l))
                nc.scalar.copy(XT[:, 0:2, :], bank("ret_oT")[:, :]).then_inc(*took("ret_oT"))
                act.wait_ge(*full("swa_o0", l))
                nc.scalar.copy(XT[:, 2:4, :], bank("swa_o0")[:, :]).then_inc(*took("swa_o0"))
                act.wait_ge(*full("swa_o1", l))
                nc.scalar.copy(XT[:, 4, :], bank("swa_o1")[:, 0:SEQ]).then_inc(*took("swa_o1"))
                for h in range(0, 6, 2):
                    act.wait_ge(*full(f"mla_pT{h}", l))
                    nc.scalar.copy(mla_pT[:, h, :], bank(f"mla_pT{h}")[:, 0:3 * P]).then_inc(*took(f"mla_pT{h}"))
                act.wait_ge(*full("mla_o0", l))
                nc.scalar.copy(XT[:, 5:7, :], bank("mla_o0")[:, :]).then_inc(*took("mla_o0"))
                act.wait_ge(*full("mla_o1", l))
                nc.scalar.copy(XT[:, 7, :], bank("mla_o1")[:, 0:SEQ]).then_inc(*took("mla_o1"))
                act.wait_ge(gu_in[0], (l * (N_EXP // 2) + 1) * 16)
                high_up(0, w_gate[0])
                high_up(1, w_up[0])
                high_down(2, 0, dn_in, l * (N_EXP // 2) + 1)
                for t in range(T):
                    act.wait_ge(ln_var, l * 4 + t + 1)
                    rstd(link, lrs[:, t, :], mv2[:, t, 1:2], 1.0, "ln_eps", ln_rstd)
                for n in (0, 2):
                    act.wait_ge(*full(f"x1T{n}", l))
                    nc.scalar.copy(XT[:, 2 * n:2 * n + 2, :], bank(f"x1T{n}")[:, :]).then_inc(*took(f"x1T{n}"))
                split_xt("x1T", l)
                act.wait_ge(*full("router", l))
                nc.scalar.activation(sc, bank("router")[:, 0:2 * N_EXP], ACT.Exp, scale=-1.0).then_inc(*took("router"))

                def expert_step(m, s, first=False, last=False):
                    e = 2 * m + s
                    if not first:
                        act.wait_ge(hid_ready, hidden(l, e - 2))
                    act.wait_ge(*full(f"gate{s}", l, m))
                    nc.scalar.activation(sig[s], bank(f"gate{s}")[:, :], ACT.Silu).then_inc(*took(f"gate{s}"))
                    if not last:
                        act.wait_ge(gu_in[1 - s], (l * (N_EXP // 2) + m + (s + 1)) * 16)
                        high_up(0, w_gate[1 - s])
                        act.wait_ge(*full(f"up{s}", l, m))
                        high_up(1, w_up[1 - s])
                    if last:
                        high_down(0, s, dn_in, l * (N_EXP // 2) + m + 1)
                    elif not first:
                        act.wait_ge(expert_used, l * (N_EXP - 1) + e)
                        high_down(2, s, dn_in, l * (N_EXP // 2) + m + 1)

                expert_step(0, 0, first=True)
                act.wait_ge(*full("gatesT", l))
                nc.scalar.copy(gatesT[0:N_EXP, :], bank("gatesT")[0:N_EXP, 0:SEQ]).then_inc(*took("gatesT"))
                act.wait_ge(*read("gatesT", l))
                act.dma_start(gates_dram[bass.ds(l, 1)].rearrange("o e t -> (o e) t"), gatesT[0:N_EXP, :]).then_inc(gates_out, 16)
                act.wait_ge(gates_out, (l + 1) * 16)
                act.dma_start(gates_b, gates_dram[bass.ds(l, 1)].rearrange("o e t -> (o e t)").partition_broadcast(P)
                              ).then_inc(gates_in, 16)
                with act.Fori(1, N_EXP // 2) as m:
                    expert_step(m - 1, 1)
                    expert_step(m, 0)
                expert_step(N_EXP // 2 - 1, 1, last=True)
                for t in range(T):
                    act.wait_ge(ln_var, l * 4 + T + t + 1)
                    rstd(link, lrs[:, t, :], mv2[:, t, 1:2], 1.0, "ln_eps", ln_rstd)
                assert link.n == ACT_LINKS, link.n

            link = Link(act, act_fin)

            def rms_rows_of(n):
                for t in range(T):
                    if n == 0:
                        act.wait_ge(x_ready, NL * T + t + 1)
                    else:
                        act.wait_ge(*read(f"out{2 * t}", NL))
                        act.wait_ge(*read(f"out{2 * t + 1}", NL))
                    r = rss[:, t:t + 1]
                    link(nc.scalar.activation(square_out[n], X[:, t, :], ACT.Square, accum_out=r))
                    link(nc.scalar.activation(r, r, ACT.Ln, bias=tb("rms_eps"), scale=1.0 / D))
                    nc.scalar.activation(r, r, ACT.Exp, scale=-0.5).then_inc(rms_rstd, 1)

            act.wait_ge(final_in, 14 * 16)
            rms_rows_of(0)
            for n in (0, 2):
                act.wait_ge(*full(f"n1T{n}", NL))
                for k in range(2):
                    ins = nc.scalar.activation(XT[:, 2 * n + k, :], bank(f"n1T{n}")[:, k * SEQ:(k + 1) * SEQ], ACT.Copy,
                                               scale=n1g[:, 2 * n + k:2 * n + k + 1])
                ins.then_inc(*took(f"n1T{n}"))
            for n in range(2):
                act.wait_ge(*full(f"gl{n}", NL))
                nc.scalar.copy(glT[:, 2 * n:2 * n + 2, :], bank(f"gl{n}")[:, :]).then_inc(*took(f"gl{n}"))
            act.wait_ge(pad_zero, 1)
            for n in range(2):
                act.wait_ge(*full(f"xl{n}", NL))
                nc.scalar.copy(xl_pad[:, 2 * n:2 * n + 2, CONV - 1:], bank(f"xl{n}")[:, :].rearrange("p (a b) -> p a b", b=SEQ)
                               ).then_inc(*took(f"xl{n}"))
            act.wait_ge(consts2, 1)
            nc.scalar.activation(sp_e, sp_e, ACT.Exp).then_inc(sp_lam, 1)
            act.wait_ge(gel_in, 1)
            nc.scalar.activation(gel, gel, ACT.Tanh, scale=float(np.sqrt(2.0 / np.pi))).then_inc(gel_t, 1)

            def squares(n):
                name = ("q0", "q1", "k0", "k1")[n]
                act.wait_ge(*full(name, NL))
                nc.scalar.activation(qk_sq[:, n, :], bank(name)[:, :], ACT.Square).then_inc(qk_squared, 1)

            squares(0)
            for n, (dst, b) in enumerate(((rgT, brg), (igT, big))):
                for c in range(4):
                    name = ("rg0", "rg1", "ig0", "ig1")[2 * n + c // 2]
                    if c % 2 == 0:
                        act.wait_ge(*full(name, NL))
                    ins = nc.scalar.activation(dst[:, c, :], bank(name)[:, (c % 2) * SEQ:(c % 2 + 1) * SEQ], ACT.Sigmoid,
                                               bias=b[:, c:c + 1])
                    if c % 2 == 1:
                        ins.then_inc(*took(name))
            act.wait_ge(lru_la, 1)
            nc.scalar.activation(lruA, rgT, ACT.Exp)
            nc.scalar.activation(lruT, rgT, ACT.Tanh, scale=-1.0).then_inc(lru_at, 1)
            act.wait_ge(lru_m2, 1)
            nc.scalar.activation(lruT, lruT, ACT.Sqrt).then_inc(lru_sq, 1)
            for n in range(1, 4):
                squares(n)
            for n in range(4):
                act.wait_ge(*full(f"ssq{n}", NL))
                nc.scalar.activation(qk_rstd[:, n, :], bank(f"ssq{n}")[:, :], ACT.Ln, bias=tb("rms_eps"), scale=1.0 / HD
                                     ).then_inc(*took(f"ssq{n}"))
                act.wait_ge(*read(f"ssq{n}", NL))
                nc.scalar.activation(qk_rstd[:, n, :], qk_rstd[:, n, :], ACT.Exp, scale=-0.5).then_inc(qk_rstd_ok, 1)
                if n in (1, 3):
                    t = n // 2
                    act.wait_ge(*full(f"v{t}", NL))
                    nc.scalar.copy(st_v[:, t, :], bank(f"v{t}")[:, :]).then_inc(*took(f"v{t}"))

            def soft_part(h):
                act.wait_ge(*full(f"z{h}", NL))
                link(nc.scalar.activation(stW[:, h, :], bank(f"z{h}")[:, 0:3 * P], ACT.Abs))
                link(nc.scalar.activation(stW[:, h, :], stW[:, h, :], ACT.Exp, scale=-1.0))
                nc.scalar.activation(stW[:, h, :], stW[:, h, :], ACT.Ln, bias=tb("one")).then_inc(log1pd, 1)

            def weight_part(h):
                act.wait_ge(*read(f"sfx{h}", NL))
                nc.scalar.activation(stW[:, h, :], stW[:, h, :], ACT.Exp).then_inc(wexp, 1)

            for h in range(ST_H):
                soft_part(h)
                if h >= 2:
                    weight_part(h - 2)
            for h in range(ST_H - 2, ST_H):
                weight_part(h)
            for n in range(2):
                act.wait_ge(*full(f"att{n}", NL))
                nc.scalar.copy(XT[:, 2 * n:2 * n + 2, :], bank(f"att{n}")[:, :]).then_inc(*took(f"att{n}"))

            def high_chunk(s, n):
                act.wait_ge(up_in[s], n * 16)
                high_up(s, w_gate[s])

            act.wait_ge(lru_mix, 1)
            high_down(2, 0, down_in, 1)
            high_chunk(0, 1)
            high_chunk(1, 1)
            rms_rows_of(1)
            for n in (0, 2):
                act.wait_ge(*full(f"n2T{n}", NL))
                for k in range(2):
                    ins = nc.scalar.activation(XT[:, 2 * n + k, :], bank(f"n2T{n}")[:, k * SEQ:(k + 1) * SEQ], ACT.Copy,
                                               scale=n2g[:, 2 * n + k:2 * n + k + 1])
                ins.then_inc(*took(f"n2T{n}"))
            split_xt("n2T", NL)

            def chunk_step(m, s, first=False, more_up=True, more_down=True):
                c = 2 * m + s
                act.wait_ge(hid_ready, hidden(NL, c - 2))
                act.wait_ge(*full(f"ff{s}", NL, m))
                nc.scalar.activation(sig[s], bank(f"ff{s}")[:, :], ACT.Relu).then_inc(relu_done, 1)
                if more_up:
                    high_chunk(s, m + 2)
                if more_down:
                    if not first:
                        act.wait_ge(ff_used, c)
                    high_down(3 - s, 1 - s, down_in, m + s + 1)

            chunk_step(0, 0, first=True)
            with act.Fori(1, N_CHUNK // 2 - 1) as m:
                chunk_step(m - 1, 1)
                chunk_step(m, 0)
            chunk_step(N_CHUNK // 2 - 2, 1)
            chunk_step(N_CHUNK // 2 - 1, 0, more_up=False)
            chunk_step(N_CHUNK // 2 - 1, 1, more_up=False, more_down=False)

        @block.tensor
        def _(pe):
            def product(dst, pairs, first=True, last=True):
                for n, (lhsT, rhs) in enumerate(pairs):
                    ins = nc.tensor.matmul(dst, lhsT, rhs, start=first and n == 0, stop=last and n == len(pairs) - 1)
                return ins

            def features(w, cols, act_T=None):
                return [(w[:, k, cols], XT[:, k, :]) for k in range(KD)]

            def rows(w, cols, t):
                return [(XT[:, k, token(t)], w[:, k, cols]) for k in range(KD)]

            def split_features(slot, cols):
                parts = []
                for k in range(KD):
                    high, low = WH_up[slot][:, k, cols], WL_up[slot][:, k, cols]
                    parts += [(high, XTH[:, k, :]), (high, XTL[:, k, :]), (low, XTH[:, k, :])]
                return parts

            def split_down(slot, n, s, names, l, first, last):
                if first:
                    pe.wait_ge(*free(names[n], l))
                parts, cols = [], slice((n % 2) * 512, (n % 2 + 1) * 512)
                for c in range(2):
                    high, low = HIDH[s][:, c, token(n // 2)], HIDL[s][:, c, token(n // 2)]
                    parts += [(high, WH_dn[slot][:, c, cols]), (high, WL_dn[slot][:, c, cols]), (low, WH_dn[slot][:, c, cols])]
                ins = product(bank(names[n])[:, :], parts, first, last)
                if last:
                    ins.then_inc(*made(names[n]))
                return ins

            def transpose_rows(prefix, src, l, ready, n_ready):
                for t in range(T):
                    pe.wait_ge(ready, n_ready + (t + 1))
                    for n in range(4):
                        name = f"{prefix}{n}"
                        if t == 0:
                            pe.wait_ge(*free(name, l))
                        for k in (2 * n, 2 * n + 1):
                            c = (k % 2) * SEQ + t * P
                            ins = nc.tensor.transpose(bank(name)[:, c:c + P], src[:, t, k:D:KD], ident)
                        if t == T - 1:
                            ins.then_inc(*made(name))

            def transposes_read(prefix, l):
                for n in range(4):
                    pe.wait_ge(*read(f"{prefix}{n}", l))

            def tile_of(name, n, w=SEQ):
                return bank(name)[:, n * w:(n + 1) * w]

            def probs_T(name, h, p1, p0, l):
                job = f"{name}_pT{h}"
                pe.wait_ge(*free(job, l))
                pe.wait_ge(normed[name], l * 6 + h + 1)
                nc.tensor.transpose(bank(job)[:, 0:P], p0[:, h, :], ident)
                nc.tensor.transpose(bank(job)[:, P:2 * P], p1[:, h, 0:P], ident)
                nc.tensor.transpose(bank(job)[:, 2 * P:3 * P], p1[:, h, P:2 * P], ident).then_inc(*made(job))

            def weighted_values(dst, v0, v1, pT):
                nc.tensor.matmul(dst, v0, pT[:, 0:2 * P], start=True, stop=False)
                return nc.tensor.matmul(dst[:, P:2 * P], v1, pT[:, 2 * P:3 * P], start=False, stop=True)

            def key_major_scores(dst, kT, qT):
                nc.tensor.matmul(dst[:, 0:2 * P], kT[:, 0:P], qT, start=True, stop=True)
                return nc.tensor.matmul(dst[:, 2 * P:3 * P], kT[:, P:2 * P], qT[:, P:2 * P], start=True, stop=True)

            def scores(name, kq, l):
                for n in range(3):
                    job = f"{name}_s1_{n}"
                    pe.wait_ge(*free(job, l))
                    for h in (2 * n, 2 * n + 1):
                        kT, qT = kq(h)
                        if name == "swa" and n == 1 and h == 3:
                            ins.then_inc(rows_turned, 1)
                            pe.wait_ge(rows_turned, l * 2 + 1)
                        ins = nc.tensor.matmul(tile_of(job, h % 2), qT[:, P:2 * P], kT, start=True, stop=True)
                    ins.then_inc(*made(job))
                for n, heads in enumerate((range(4), range(4, 6))):
                    job = f"{name}_s0_{n}"
                    pe.wait_ge(*free(job, l))
                    for h in heads:
                        kT, qT = kq(h)
                        if name == "swa" and h == 3:
                            ins.then_inc(rows_turned, 1)
                            pe.wait_ge(rows_turned, l * 2 + 2)
                        ins = nc.tensor.matmul(tile_of(job, h % 4, P), qT[:, 0:P], kT[:, 0:P], start=True, stop=True)
                    ins.then_inc(*made(job))

            pe.wait_ge(ident_in, 16)
            with pe.Fori(0, NL) as l:
                transpose_rows("xT", X, l, x_ready, l * T)
                transposes_read("xT", l)
                pe.wait_ge(wlat_in, (l + 1) * 16)
                for n in range(5):
                    job = f"lat{n // 2}"
                    if n % 2 == 0:
                        pe.wait_ge(*free(job, l))
                    ins = product(tile_of(job, n % 2), features(w_lat, slice(n * P, (n + 1) * P)))
                    if n % 2 == 1:
                        ins.then_inc(*made(job))
                product(bank("lat2")[NOPE:DQ, SEQ:2 * SEQ], features(w_lat, slice(5 * P, N_LAT))).then_inc(*made("lat2"))
                pe.wait_ge(wrqk_in, (l + 1) * 16)
                for n, job in enumerate(("ret_q", "ret_k")):
                    pe.wait_ge(*free(job, l))
                    for c in range(2):
                        ins = product(tile_of(job, c), features(w_rqk, slice((2 * n + c) * P, (2 * n + c + 1) * P)))
                    ins.then_inc(*made(job))
                pe.wait_ge(tab_in, 16)
                pe.wait_ge(*free("lat_ssq", l))
                pe.wait_ge(lat_squared, (l + 1) * 3)
                product(tile_of("lat_ssq", 0), [(ones, lat_sq[:, c, :]) for c in range(3)])
                product(tile_of("lat_ssq", 1), [(ones, lat_sq[:, c, :]) for c in (3, 4)]).then_inc(*made("lat_ssq"))
                pe.wait_ge(wswa_in, (l + 1) * 7 * 16)
                for n in range(4):
                    job = ("swa_q01", "swa_q01", "swa_q2k", "swa_q2k")[n]
                    if n % 2 == 0:
                        pe.wait_ge(*free(job, l))
                    ins = product(tile_of(job, n % 2), features(w_swa, slice(n * P, (n + 1) * P)))
                    if n % 2 == 1:
                        ins.then_inc(*made(job))
                pe.wait_ge(wrvg_in, (l + 1) * 16)
                for t in range(T):
                    pe.wait_ge(*free(f"ret_vg{t}", l))
                    product(bank(f"ret_vg{t}")[:, :], rows(w_rvg, slice(0, 512), t)).then_inc(*made(f"ret_vg{t}"))
                pe.wait_ge(*free("swa_v", l))
                for t in range(T):
                    ins = product(tile_of("swa_v", t, P), rows(w_swa, slice(C_SV - C_SQ, C_CQ - C_SQ), t))
                ins.then_inc(*made("swa_v"))
                for job, src, name in (("ret_q_swap", ret_qT, "ret_q"), ("ret_k_swap", ret_kT, "ret_k")):
                    pe.wait_ge(*free(job, l))
                    pe.wait_ge(*read(name, l))
                    nc.tensor.matmul(bank(job)[:, :], tb("swap_r"), src, start=True, stop=True).then_inc(*made(job))
                pe.wait_ge(wup_in, (l + 1) * 32)
                for n in range(3):
                    pe.wait_ge(*free(f"mla_q{n}", l))
                    pe.wait_ge(*read("lat2", l))
                    for h in (2 * n, 2 * n + 1):
                        ins = product(tile_of(f"mla_q{n}", h % 2)[0:DQ], [
                            (w_uq[:, c, h * DQ:(h + 1) * DQ], lat_n[:, c, :]) for c in range(3)])
                    ins.then_inc(*made(f"mla_q{n}"))
                for n in range(3):
                    pe.wait_ge(*free(f"mla_k{n}", l))
                    for h in (2 * n, 2 * n + 1):
                        ins = product(tile_of(f"mla_k{n}", h % 2)[0:NOPE], [
                            (w_ukv[:, c, h * P:h * P + NOPE], lat_n[:, 3 + c, :]) for c in range(2)])
                    ins.then_inc(*made(f"mla_k{n}"))
                for t in range(T):
                    pe.wait_ge(*free(f"mla_v{t}", l))
                    product(bank(f"mla_v{t}")[:, 0:384].rearrange("p (h d) -> p h d", d=MLA_VD), [
                        (lat_n[:, 3 + c, token(t)], w_ukv[:, c, :].rearrange("p (h d) -> p h d", d=P)[:, :, NOPE:P])
                        for c in range(2)]).then_inc(*made(f"mla_v{t}"))
                turn = slice(NOPE, DQ)
                for n in range(3):
                    pe.wait_ge(*free(f"mla_q_swap{n}", l))
                    nc.tensor.matmul(bank(f"mla_q_swap{n}")[:, :], tb("swap_m")[turn, :], mla_qT[turn, 2 * n:2 * n + 2, :],
                                     start=True, stop=True).then_inc(*made(f"mla_q_swap{n}"))
                pe.wait_ge(*free("mla_kr_swap", l))
                pe.wait_ge(kr_copied, l + 1)
                nc.tensor.matmul(bank("mla_kr_swap")[:, 0:SEQ], tb("swap_m")[turn, :], krT[turn, :],
                                 start=True, stop=True).then_inc(*made("mla_kr_swap"))
                pe.wait_ge(ret_roped, (l + 1) * 2)
                for h in range(RET_H):
                    job, part = f"ret_s{h}", slice((h % 2) * HD, (h % 2 + 1) * HD)
                    pe.wait_ge(*free(job, l))
                    key_major_scores(bank(job), ret_kT[part, h // 2, :], ret_qT[part, h // 2, :]).then_inc(*made(job))
                scores("swa", lambda h: (swa_kT[(h // 3) * HD:(h // 3 + 1) * HD, :],
                                         swa_qT[(h // 3) * HD:(h // 3 + 1) * HD, h % 3, :]), l)
                for h in range(RET_H):
                    pe.wait_ge(*read(f"ret_s{h}", l))
                ro = bank("ret_o")[:, :].rearrange("p (t h d) -> p t h d", t=T, h=RET_H)
                for h in range(RET_H):
                    v = ret_v[:, :, h * HD:(h + 1) * HD]
                    nc.tensor.matmul(ro[:, 0, h, :], ret_pT[:, h, 0:P], v[:, 0, :], start=True, stop=True)
                    nc.tensor.matmul(ro[:, 1, h, :], ret_pT[:, h, P:2 * P], v[:, 0, :], start=True, stop=False)
                    ins = nc.tensor.matmul(ro[:, 1, h, :], ret_pT[:, h, 2 * P:3 * P], v[:, 1, :], start=False, stop=True)
                ins.then_inc(*made("ret_o"))
                pe.wait_ge(q_roped, l + 1)
                pe.wait_ge(k_roped, l + 2)
                scores("mla", lambda h: (mla_kT[0:DQ, h, :], mla_qT[0:DQ, h, :]), l)
                for h in range(SWA_H):
                    probs_T("swa", h, swa_p1, swa_p0, l)
                pe.wait_ge(*free("ret_oT", l))
                pe.wait_ge(ret_out, l + 1)
                rc = ret_c.rearrange("p (t h) d -> p t (h d)", t=T)
                for c in range(2):
                    for t in range(T):
                        ins = nc.tensor.transpose(bank("ret_oT")[:, c * SEQ + t * P:c * SEQ + (t + 1) * P],
                                                  rc[:, t, c * P:(c + 1) * P], ident)
                ins.then_inc(*made("ret_oT"))

                def attend(name, pT, value):
                    for h in range(6):
                        job = f"{name}_o{h // 4}"
                        if h % 4 == 0:
                            pe.wait_ge(*free(job, l))
                        pe.wait_ge(*read(f"{name}_pT{h}", l))
                        dst = tile_of(job, (h // 2) % 2)[(h % 2) * HD:(h % 2 + 1) * HD, :]
                        ins = weighted_values(dst, value(h, 0), value(h, 1), pT[:, h, :])
                        if h in (3, 5):
                            ins.then_inc(*made(job))

                attend("swa", swa_pT, lambda h, t: swa_v[:, t, (h // 3) * HD:(h // 3 + 1) * HD])
                for h in range(MLA_H):
                    probs_T("mla", h, mla_p1, mla_p0, l)
                attend("mla", mla_pT, lambda h, t: mla_v[:, t, h * MLA_VD:(h + 1) * MLA_VD])
                pe.wait_ge(wout_in, (l + 1) * 16)
                for job in ("ret_oT", "swa_o0", "swa_o1", "mla_o0", "mla_o1"):
                    pe.wait_ge(*read(job, l))
                for n in range(4):
                    pe.wait_ge(*free(f"mix{n}", l))
                    product(bank(f"mix{n}")[:, :], rows(w_out, slice((n % 2) * 512, (n % 2 + 1) * 512), n // 2)
                            ).then_inc(*made(f"mix{n}"))
                transpose_rows("x1T", X, l, x1_ready, l * T)
                transposes_read("x1T", l)
                pe.wait_ge(router_in, 32)
                pe.wait_ge(*free("router", l))
                for t in range(T):
                    ins = product(tile_of("router", t, N_EXP), rows(router, slice(0, N_EXP), t))
                ins.then_inc(*made("router"))
                pe.wait_ge(xt_low, (l + 1) * 4)

                def expert_up(m, s):
                    for n, job in enumerate((f"gate{s}", f"up{s}")):
                        pe.wait_ge(low_made[n], unit(n, l, 2 * m + s))
                        pe.wait_ge(*free(job, l, m))
                        for c in range(2):
                            ins = product(tile_of(job, c), split_features(n, slice(c * P, (c + 1) * P)))
                        ins.then_inc(*made(job))

                def expert_down(m, s, first=False, last=False):
                    slot = 0 if last else 2
                    pe.wait_ge(low_made[slot], unit(slot, l, 2 * m + s + int(last)))
                    pe.wait_ge(hid_ready, hidden(l, 2 * m + s))
                    for n in range(4):
                        ins = split_down(slot, n, s, ("y0", "y1", "y2", "y3"), l, first, last)
                    if not last:
                        ins.then_inc(expert_used, 1)

                expert_up(0, 0)
                pe.wait_ge(*free("gatesT", l))
                pe.wait_ge(gates_ready, l + 1)
                for t in range(T):
                    ins = nc.tensor.transpose(bank("gatesT")[0:N_EXP, token(t)], gates[:, t, :], ident)
                ins.then_inc(*made("gatesT"))
                expert_up(0, 1)
                expert_down(0, 0, first=True)
                with pe.Fori(1, N_EXP // 2) as m:
                    expert_up(m, 0)
                    expert_down(m - 1, 1)
                    expert_up(m, 1)
                    expert_down(m, 0)
                expert_down(N_EXP // 2 - 1, 1, last=True)

            l = NL
            transpose_rows("n1T", xn, l, rms_rows, 0)
            transposes_read("n1T", l)
            def tiles2(job, w, c0):
                pe.wait_ge(*free(job, l))
                for c in range(2):
                    ins = product(tile_of(job, c), features(w, slice(c0 + c * P, c0 + (c + 1) * P)))
                ins.then_inc(*made(job))

            pe.wait_ge(wgl_in, 16)
            tiles2("gl0", w_gl2, 0)
            tiles2("gl1", w_gl2, 2 * P)
            pe.wait_ge(wvx_in, 16)
            tiles2("xl0", w_vx2, 512)
            tiles2("xl1", w_vx2, 512 + 2 * P)
            pe.wait_ge(wq_in, 16)
            tiles2("q0", w_q2, 0)
            pe.wait_ge(bd_in, 64)
            pe.wait_ge(conv_done, 1)
            for n, pre in enumerate(("rg", "ig")):
                for c in range(4):
                    job = f"{pre}{c // 2}"
                    if c % 2 == 0:
                        pe.wait_ge(*free(job, l))
                    ins = nc.tensor.matmul(tile_of(job, c % 2), w_bd[:, n, c, :], conv_u[:, c, :], start=True, stop=True)
                    if c % 2 == 1:
                        ins.then_inc(*made(job))
            tiles2("q1", w_q2, 2 * P)
            pe.wait_ge(wk_in, 16)
            tiles2("k0", w_k2, 0)
            tiles2("k1", w_k2, 2 * P)

            def head_sums(n):
                pe.wait_ge(*free(f"ssq{n}", l))
                pe.wait_ge(qk_squared, n + 1)
                nc.tensor.matmul(bank(f"ssq{n}")[:, :], tb("half_ones"), qk_sq[:, n, :], start=True, stop=True
                                 ).then_inc(*made(f"ssq{n}"))

            def values(t):
                pe.wait_ge(*free(f"v{t}", l))
                product(bank(f"v{t}")[:, :], rows(w_vx2, slice(0, 512), t)).then_inc(*made(f"v{t}"))

            head_sums(0)
            head_sums(1)
            values(0)
            head_sums(2)
            values(1)
            head_sums(3)
            def z_of(h):
                job, part = f"z{h}", slice((h % 2) * HD, (h % 2 + 1) * HD)
                pe.wait_ge(*free(job, l))
                key_major_scores(bank(job), st_kT[part, h // 2, :], st_qT[part, h // 2, :]).then_inc(*made(job))

            def suffix_of(h):
                job = f"sfx{h}"
                pe.wait_ge(*free(job, l))
                pe.wait_ge(masked_sp, h + 1)
                later, s = tb("later"), stS[:, h, :]
                nc.tensor.matmul(bank(job)[:, 0:2 * P], later, s[:, 0:2 * P], start=True, stop=False)
                nc.tensor.matmul(bank(job)[:, P:2 * P], ones, s[:, 2 * P:3 * P], start=False, stop=True)
                nc.tensor.matmul(bank(job)[:, 2 * P:3 * P], later, s[:, 2 * P:3 * P], start=True, stop=True
                                 ).then_inc(*made(job))

            for name in ("q0", "q1", "k0", "k1"):
                pe.wait_ge(*read(name, l))
            z_of(0)
            z_of(1)
            for h in range(ST_H):
                suffix_of(h)
                if h + 2 < ST_H:
                    z_of(h + 2)
            for h in range(ST_H):
                job = f"att{h // 4}"
                if h % 4 == 0:
                    pe.wait_ge(*free(job, l))
                pe.wait_ge(w_masked, h + 1)
                dst = tile_of(job, (h // 2) % 2)[(h % 2) * HD:(h % 2 + 1) * HD, :]
                ins = weighted_values(dst, st_v[:, 0, h * HD:(h + 1) * HD], st_v[:, 1, h * HD:(h + 1) * HD], stW[:, h, :])
                if h % 4 == 3:
                    ins.then_inc(*made(job))
            pe.wait_ge(wout_in, (NL + 1) * 16)
            pe.wait_ge(*read("att0", l))
            pe.wait_ge(*read("att1", l))
            pe.wait_ge(lru_mix, 1)
            for n in range(4):
                pe.wait_ge(*free(f"out{n}", l))
                mixed = [(XT if k < 4 else lruH)[:, k % 4, token(n // 2)] for k in range(KD)]
                product(bank(f"out{n}")[:, :], [(mixed[k], w_out[:, k, (n % 2) * 512:(n % 2 + 1) * 512]) for k in range(KD)]
                        ).then_inc(*made(f"out{n}"))
            transpose_rows("n2T", xn, l, rms_rows, T)
            transposes_read("n2T", l)

            pe.wait_ge(xt_low, (NL + 1) * 4)

            def chunk_up(m, s):
                pe.wait_ge(low_made[s], unit(s, NL, m))
                pe.wait_ge(*free(f"ff{s}", l, m))
                for c in range(2):
                    ins = product(tile_of(f"ff{s}", c), split_features(s, slice(c * P, (c + 1) * P)))
                ins.then_inc(*made(f"ff{s}"))

            def chunk_down(m, s, first=False, last=False):
                pe.wait_ge(low_made[2 + s], unit(2 + s, NL, m))
                pe.wait_ge(hid_ready, hidden(NL, 2 * m + s))
                for n in range(4):
                    ins = split_down(2 + s, n, s, ("m0", "m1", "m2", "m3"), l, first, last)
                if not last:
                    ins.then_inc(ff_used, 1)

            chunk_up(0, 0)
            chunk_up(0, 1)
            chunk_down(0, 0, first=True)
            with pe.Fori(1, N_CHUNK // 2) as m:
                chunk_up(m, 0)
                chunk_down(m - 1, 1)
                chunk_up(m, 1)
                chunk_down(m, 0)
            chunk_down(N_CHUNK // 2 - 1, 1, last=True)

        @block.vector
        def _(dve):
            v = nc.vector

            def layer_norm(l, link, which, jobs, loaded, done):
                for t in range(T):
                    for half in range(2):
                        job = jobs[2 * t + half]
                        part = X[:, t, half * 512:(half + 1) * 512]
                        dve.wait_ge(*full(job, l))
                        v.scalar_tensor_tensor(part, part, ALPHA, bank(job)[:, :], ALU.mult, ALU.add).then_inc(*took(job))
                        dve.wait_ge(*read(job, l))
                        ins = v.bn_stats(st6[:, t, half * 6:(half + 1) * 6], part)
                    link(ins)
                    v.memset(lrs[:, t, :], 0.0)
                    v.bn_aggr(mv2[:, t, :], st6[:, t, :]).then_inc(ln_var, 1)
                    n = l * 4 + (which - 1) * T + t + 1
                    dve.wait_ge(loaded, (l + 1) * 32)
                    dve.wait_ge(ln_var, n)
                    v.scalar_tensor_tensor(X[:, t, :], X[:, t, :], mv2[:, t, 0:1], LNB[:, 0, :], ALU.subtract, ALU.mult
                                           ).then_inc(ln_centred, 1)
                    dve.wait_ge(ln_centred, n)
                    dve.wait_ge(ln_rstd, n)
                    v.scalar_tensor_tensor(X[:, t, :], X[:, t, :], lrs[:, t, 0:1], LNB[:, 1, :], ALU.mult, ALU.add
                                           ).then_inc(done, 1)

            def softmax_scores(name, l, link, p1, p0, mask, scale):
                for n in range(3):
                    job = f"{name}_s1_{n}"
                    dve.wait_ge(*full(job, l))
                    v.tensor_tensor(p1[:, 2 * n:2 * n + 2, :], bank(job)[:, :].rearrange("p (a b) -> p a b", b=SEQ),
                                    spread(mask, 1, [P, 2, SEQ]), ALU.add).then_inc(*took(job))
                for n, (h0, k) in enumerate(((0, 4), (4, 2))):
                    job = f"{name}_s0_{n}"
                    dve.wait_ge(*full(job, l))
                    v.tensor_tensor(p0[:, h0:h0 + k, :], bank(job)[:, 0:k * P].rearrange("p (a b) -> p a b", b=P),
                                    spread(mask[:, P:2 * P], 1, [P, k, P]), ALU.add).then_inc(*took(job))
                for job in (f"{name}_s1_{n}" for n in range(3)):
                    dve.wait_ge(*read(job, l))
                v.tensor_reduce(mx[name][:, 1, :], p1, AX.X, ALU.max)
                dve.wait_ge(*read(f"{name}_s0_0", l))
                dve.wait_ge(*read(f"{name}_s0_1", l))
                link(v.tensor_reduce(mx[name][:, 0, :], p0, AX.X, ALU.max))
                if name == "swa":
                    dve.wait_ge(norms_in, (l + 1) * 64)
                    sinks = spread(sink_b, 1, [P, T, SWA_H])
                    link(v.tensor_tensor(mx[name], mx[name], sinks, ALU.max))
                    v.tensor_tensor(sk_e, sinks, mx[name], ALU.subtract)
                v.tensor_scalar(nmx[name], mx[name], -scale, None, ALU.mult).then_inc(maxed[name], 1)

            def softmax_norm(name, l, link, p1, p0):
                dve.wait_ge(expd[name], l + 1)
                if name == "swa":
                    link(v.tensor_tensor(psm[name], psm[name], sk_e, ALU.add))
                link(v.reciprocal(rin[name], psm[name]))
                for h in range(6):
                    v.tensor_scalar(p0[:, h, :], p0[:, h, :], rin[name][:, 0, h:h + 1], None, ALU.mult)
                    v.tensor_scalar(p1[:, h, :], p1[:, h, :], rin[name][:, 1, h:h + 1], None, ALU.mult
                                    ).then_inc(normed[name], 1)

            def evacuate(job, dst, l, rows=slice(0, P), w=512):
                dve.wait_ge(*full(job, l))
                v.tensor_copy(dst, bank(job)[rows, 0:w]).then_inc(*took(job))

            def low_of_xt(l):
                for n in range(4):
                    dve.wait_ge(xt_high, l * 4 + n + 1)
                    part = slice(2 * n, 2 * n + 2)
                    v.tensor_tensor(XTL[:, part, :], XT[:, part, :], XTH[:, part, :].bitcast(F32), ALU.subtract
                                    ).then_inc(xt_low, 1)

            def split_hidden(link, s):
                h = sig[s].rearrange("p (a b) -> p a b", b=SEQ)
                link(v.tensor_copy(HIDH[s][:, :, :], h))
                v.tensor_tensor(HIDL[s][:, :, :], h, HIDH[s][:, :, :].bitcast(F32), ALU.subtract).then_inc(hid_ready, 1)

            def low_down(slot, s, n):
                dve.wait_ge(high_made[slot], n)
                v.tensor_tensor(WL_dn[slot], w_dn[s], WH_dn[slot].bitcast(F32), ALU.subtract).then_inc(low_made[slot], 1)

            for b in range(8):
                v.memset(marks[:, b:b + 1], 0.0).then_inc(psum_read[b], 1)
            v.memset(marks[:, 9 + T:10 + T], 0.0).then_inc(hid_ready, 1)
            for t in range(T):
                dve.wait_ge(x_in[t], 16)
                v.memset(marks[:, 8 + t:9 + t], 0.0).then_inc(x_ready, 1)
            dve.wait_ge(tab_in, 16)
            with dve.Fori(0, NL) as l:
                link = Link(dve, dve_link, l * DVE_LINKS)
                for n in (1, 3):
                    evacuate(f"xT{n}", XT[:, 2 * n:2 * n + 2, :], l)
                turn = slice(NOPE, DQ)
                dve.wait_ge(norms_in, (l + 1) * 64)
                dve.wait_ge(rstd_ready, l + 1)
                for n in range(5):
                    job, kv = f"lat{n // 2}", n >= 3
                    gain = kvn_g[:, n - 3:n - 2] if kv else qn_g[:, n:n + 1]
                    ins = v.scalar_tensor_tensor(lat_n[:, n, :], bank(job)[:, (n % 2) * SEQ:(n % 2 + 1) * SEQ], gain,
                                                 lat_rstd[:, int(kv), :], ALU.mult, ALU.mult)
                    if n in (1, 3, 4):
                        ins.then_inc(*took(job))
                for n, (dst, job) in enumerate(((ret_qT, "ret_q_swap"), (ret_kT, "ret_k_swap"))):
                    dve.wait_ge(ret_cos, l * 2 + n + 1)
                    dve.wait_ge(*full(job, l))
                    v.tensor_tensor(dst, bank(job)[:, :].rearrange("p (a b) -> p a b", b=SEQ),
                                    spread(tb("sin_r"), 1, [P, 2, SEQ]), ALU.mult).then_inc(*took(job))
                    dve.wait_ge(*read(job, l))
                    v.tensor_tensor(dst, dst, rope_r[:, 2 * n:2 * n + 2, :], ALU.add).then_inc(ret_roped, 1)
                for n in range(3):
                    evacuate(f"mla_k{n}", mla_kT[0:NOPE, 2 * n:2 * n + 2, :], l, slice(0, NOPE))
                for n in range(3):
                    job = f"mla_q_swap{n}"
                    dve.wait_ge(*full(job, l))
                    v.tensor_tensor(rope_m[turn, 2 * n:2 * n + 2, :], bank(job)[turn, :].rearrange("p (a b) -> p a b", b=SEQ),
                                    spread(tb("sin_m")[turn], 1, [ROPE_D, 2, SEQ]), ALU.mult).then_inc(*took(job))
                dve.wait_ge(*full("mla_kr_swap", l))
                v.tensor_tensor(kr_sin[turn], bank("mla_kr_swap")[turn, 0:SEQ], tb("sin_m")[turn], ALU.mult
                                ).then_inc(*took("mla_kr_swap"))
                for h in range(RET_H):
                    dve.wait_ge(*full(f"ret_s{h}", l))
                    v.tensor_tensor(ret_pT[:, h, :], bank(f"ret_s{h}")[:, 0:3 * P], decay[:, h, :], ALU.mult
                                    ).then_inc(*took(f"ret_s{h}"))
                softmax_scores("swa", l, link, swa_p1, swa_p0, tb("mask_swa"), 1.0)
                dve.wait_ge(*full("ret_o", l))
                ro = bank("ret_o")[:, :].rearrange("p (g d) -> p g d", d=HD)
                link(v.tensor_reduce(gmu, ro, AX.X, ALU.add))
                link(v.tensor_scalar(gmu, gmu, 1.0 / HD, None, ALU.mult))
                v.tensor_tensor(ret_c, ro, spread(gmu, 2, [P, 8, HD]), ALU.subtract).then_inc(*took("ret_o"))
                softmax_scores("mla", l, link, mla_p1, mla_p0, tb("mask_mla"), DQ ** -0.5)
                softmax_norm("swa", l, link, swa_p1, swa_p0)
                dve.wait_ge(gn_squared, l + 1)
                v.tensor_reduce(gvar, ret_sq, AX.X, ALU.add).then_inc(gn_var, 1)
                for h in (1, 3, 5):
                    evacuate(f"swa_pT{h}", swa_pT[:, h, :], l, w=3 * P)
                dve.wait_ge(gn_rstd, l + 1)
                dve.wait_ge(ret_gate_w, l + 1)
                link(v.tensor_tensor(ret_c, ret_c, spread(grs, 2, [P, 8, HD]), ALU.mult))
                v.tensor_tensor(ret_c, ret_c, ret_g.rearrange("p t (h d) -> p (t h) d", d=HD), ALU.mult
                                ).then_inc(ret_out, 1)
                softmax_norm("mla", l, link, mla_p1, mla_p0)
                for h in (1, 3, 5):
                    evacuate(f"mla_pT{h}", mla_pT[:, h, :], l, w=3 * P)
                layer_norm(l, link, 1, ("mix0", "mix1", "mix2", "mix3"), ln1_in, x1_ready)
                for n in (1, 3):
                    evacuate(f"x1T{n}", XT[:, 2 * n:2 * n + 2, :], l)
                low_of_xt(l)
                dve.wait_ge(router_in, 32)
                dve.wait_ge(*read("router", l))
                link(v.tensor_scalar(sc, sc, 1.0, None, ALU.add))
                link(v.reciprocal(sc, sc))
                link(v.tensor_tensor(bi.rearrange("p (t g) e -> p t (g e)", t=T), sc.rearrange("p (t e) -> p t e", t=T),
                                     spread(rbias, 1, [P, T, N_EXP]), ALU.add))
                v.tensor_tensor(pr[:, :, 0:3], bi[:, :, 0:3], bi[:, :, 1:4], ALU.add)
                v.tensor_tensor(pr[:, :, 3:5], bi[:, :, 0:2], bi[:, :, 2:4], ALU.add)
                link(v.tensor_tensor(pr[:, :, 5:6], bi[:, :, 0:1], bi[:, :, 3:4], ALU.add))
                link(v.tensor_reduce(gs, pr, AX.X, ALU.max))

                def beaten_by(val, n, buf1, buf2, dst, limit):
                    other, own = spread(val, 2, [P, n, 4, 4]), spread(val, 3, [P, n, 4, 4])
                    v.tensor_tensor(buf1, other, own, ALU.is_gt)
                    link(v.tensor_tensor(buf2, other, own, ALU.is_equal))
                    link(v.tensor_tensor(buf2, buf2, spread(tie, 1, [P, n, 4, 4]), ALU.mult))
                    link(v.tensor_tensor(buf1, buf1, buf2, ALU.add))
                    link(v.tensor_reduce(dst, buf1, AX.X, ALU.add))
                    link(v.tensor_scalar(dst, dst, limit, None, ALU.is_lt))

                beaten_by(gs.rearrange("p (t g) -> p t g", t=T), T, g1, g2, gsel.rearrange("p (t g) -> p t g", t=T), 0.5)
                beaten_by(bi, 8, c1, c2, esel, 1.5)
                link(v.tensor_tensor(esel, esel, spread(gsel, 2, [P, 8, 4]), ALU.mult))
                link(v.tensor_tensor(esel, esel, sc.rearrange("p (g e) -> p g e", e=4), ALU.mult))
                e2 = esel.rearrange("p (t g) e -> p t (g e)", t=T)
                link(v.tensor_reduce(gden, e2, AX.X, ALU.add))
                link(v.reciprocal(gden, gden))
                v.tensor_tensor(gates, e2, spread(gden, 2, [P, T, N_EXP]), ALU.mult).then_inc(gates_ready, 1)
                dve.wait_ge(gates_in, (l + 1) * 16)
                v.memset(gden, 0.0)

                def expert_step(moe, m, s, last=False):
                    dve.wait_ge(*read(f"gate{s}", l, m))
                    act_s = sig[s].rearrange("p (a b) -> p a b", b=SEQ)
                    moe(v.tensor_tensor(act_s, act_s, gates_b[:, bass.ds(2 * m + s, 1), :].to_broadcast([P, 2, SEQ]), ALU.mult))
                    dve.wait_ge(*full(f"up{s}", l, m))
                    v.tensor_tensor(sig[s], sig[s], bank(f"up{s}")[:, :], ALU.mult).then_inc(*took(f"up{s}"))
                    dve.wait_ge(*read(f"up{s}", l, m))
                    split_hidden(moe, s)
                    slot = 0 if last else 2
                    low_down(slot, s, unit(slot, l, 2 * m + s + int(last)))

                def pair(m, last=False):
                    moe = Link(dve, dve_moe, (l * (N_EXP // 2) + m) * (2 * MOE_LINKS))
                    expert_step(moe, m, 0)
                    expert_step(moe, m, 1, last)
                    assert moe.n == 2 * MOE_LINKS

                with dve.Fori(0, N_EXP // 2 - 1) as m:
                    pair(m)
                pair(N_EXP // 2 - 1, last=True)
                layer_norm(l, link, 2, ("y0", "y1", "y2", "y3"), ln2_in, x_ready)
                assert link.n == DVE_LINKS, link.n

            l = NL
            link = Link(dve, dve_fin)
            dve.wait_ge(final_in, 14 * 16)
            v.memset(xl_pad[:, :, 0:CONV - 1], 0.0).then_inc(pad_zero, 1)
            v.tensor_scalar(qg2, qg2, HD ** -0.5, None, ALU.mult)
            v.scalar_tensor_tensor(sp_e, lam, -1.0, lam, ALU.mult, ALU.min).then_inc(consts2, 1)

            def scale_rows(n):
                for t in range(T):
                    dve.wait_ge(rms_rstd, n * T + t + 1)
                    v.tensor_scalar(xn[:, t, :], X[:, t, :], rss[:, t:t + 1], None, ALU.mult).then_inc(rms_rows, 1)

            def gained(prefix, gain):
                for n in (1, 3):
                    job = f"{prefix}{n}"
                    dve.wait_ge(*full(job, l))
                    for k in range(2):
                        ins = v.tensor_scalar(XT[:, 2 * n + k, :], bank(job)[:, k * SEQ:(k + 1) * SEQ],
                                              gain[:, 2 * n + k:2 * n + k + 1], None, ALU.mult)
                    ins.then_inc(*took(job))

            scale_rows(0)
            gained("n1T", n1g)
            dve.wait_ge(*read("xl0", l))
            dve.wait_ge(*read("xl1", l))
            for k in range(CONV):
                for c in range(4):
                    src, tap = xl_pad[:, c, k:k + SEQ], cw[:, k, c:c + 1]
                    if k == 0:
                        ins = v.tensor_scalar(conv_u[:, c, :], src, tap, cb[:, c:c + 1], ALU.mult, ALU.add)
                    else:
                        ins = v.scalar_tensor_tensor(conv_u[:, c, :], src, tap, conv_u[:, c, :], ALU.mult, ALU.add)
                if k < CONV - 1:
                    link(ins)
            ins.then_inc(conv_done, 1)
            dve.wait_ge(*read("gl0", l))
            dve.wait_ge(*read("gl1", l))
            link(v.tensor_tensor(gel, glT, glT, ALU.mult))
            link(v.tensor_scalar(gel, gel, 0.044715, 1.0, ALU.mult, ALU.add))
            v.tensor_tensor(gel, gel, glT, ALU.mult).then_inc(gel_in, 1)
            dve.wait_ge(sp_lam, 1)
            link(v.tensor_scalar(sp_s, sp_e, 2.0, None, ALU.add))
            link(v.reciprocal(sp_s, sp_s))
            link(v.tensor_tensor(sp_s, sp_s, sp_e, ALU.mult))
            link(v.tensor_tensor(sp_s2, sp_s, sp_s, ALU.mult))
            link(v.tensor_scalar(sp_p, sp_s2, 1.0 / 15, None, ALU.mult))
            for n in (13, 11, 9, 7, 5, 3):
                link(v.scalar_tensor_tensor(sp_p, sp_p, 1.0 / n, sp_s2, ALU.add, ALU.mult))
            link(v.scalar_tensor_tensor(sp_p, sp_p, 1.0, sp_s, ALU.add, ALU.mult))
            link(v.tensor_scalar(sp_s, lam, -1.0, 0.0, ALU.mult, ALU.max))
            link(v.scalar_tensor_tensor(sp_p, sp_p, 2.0, sp_s, ALU.mult, ALU.add))
            link(v.tensor_scalar(sp_p, sp_p, -LRU_C, None, ALU.mult))
            dve.wait_ge(*read("rg0", l))
            dve.wait_ge(*read("rg1", l))
            for c in range(4):
                ins = v.tensor_scalar(rgT[:, c, :], rgT[:, c, :], sp_p[:, c:c + 1], None, ALU.mult)
            ins.then_inc(lru_la, 1)
            dve.wait_ge(*read("ig0", l))
            dve.wait_ge(*read("ig1", l))
            v.tensor_tensor(igT, igT, conv_u, ALU.mult)
            dve.wait_ge(gel_t, 1)
            link(v.tensor_scalar(gel, gel, 0.5, 0.5, ALU.mult, ALU.add))
            link(v.tensor_tensor(gel, gel, glT, ALU.mult))
            dve.wait_ge(lru_at, 1)
            link(v.tensor_tensor(rgT, lruA, lruA, ALU.mult))
            v.scalar_tensor_tensor(lruT, rgT, 1.0, lruT, ALU.add, ALU.mult).then_inc(lru_m2, 1)
            dve.wait_ge(lru_sq, 1)
            link(v.tensor_tensor(igT, igT, lruT, ALU.mult))
            for c in range(4):
                ins = v.tensor_tensor_scan(lruH[:, c, :], lruA[:, c, :], igT[:, c, :], 0.0, ALU.mult, ALU.add)
            link(ins)
            v.tensor_tensor(lruH, lruH, gel, ALU.mult).then_inc(lru_mix, 1)
            dve.wait_ge(consts2, 1)
            for n, (dst, gain, job) in enumerate(((st_qT, qg2, "q0"), (st_qT, qg2, "q1"), (st_kT, kg2, "k0"), (st_kT, kg2, "k1"))):
                dve.wait_ge(qk_rstd_ok, n + 1)
                v.scalar_tensor_tensor(dst[:, 2 * (n % 2):2 * (n % 2) + 2, :].rearrange("p a b -> p (a b)"), bank(job)[:, :],
                                       gain[:, 0:1], qk_rstd[:, n, :], ALU.mult, ALU.mult).then_inc(*took(job))

            def soft_parts(h):
                z = bank(f"z{h}")[:, 0:3 * P]
                dve.wait_ge(log1pd, h + 1)
                v.scalar_tensor_tensor(stS[:, h, :], z, 0.0, stW[:, h, :], ALU.max, ALU.add).then_inc(soft, 1)
                v.scalar_tensor_tensor(stL[:, h, :], z, 0.0, stW[:, h, :], ALU.min, ALU.subtract).then_inc(*took(f"z{h}"))

            def log_weights(h):
                dve.wait_ge(*read(f"z{h}", l))
                dve.wait_ge(*full(f"sfx{h}", l))
                v.tensor_tensor(stW[:, h, :], stL[:, h, :], bank(f"sfx{h}")[:, 0:3 * P], ALU.subtract
                                ).then_inc(*took(f"sfx{h}"))

            for h in range(ST_H):
                soft_parts(h)
                if h >= 1:
                    log_weights(h - 1)
            log_weights(ST_H - 1)
            def add_rows(prefix):
                for n in range(4):
                    job, part = f"{prefix}{n}", X[:, n // 2, (n % 2) * 512:(n % 2 + 1) * 512]
                    dve.wait_ge(*full(job, l))
                    v.tensor_tensor(part, part, bank(job)[:, :], ALU.add).then_inc(*took(job))

            add_rows("out")
            scale_rows(1)
            gained("n2T", n2g)
            low_of_xt(NL)
            with dve.Fori(0, N_CHUNK // 2) as m:
                mlp = Link(dve, dve_moe, NL * N_EXP * MOE_LINKS + 2 * m)
                for s in range(2):
                    dve.wait_ge(relu_done, 2 * m + s + 1)
                    v.tensor_tensor(sig[s], sig[s], bank(f"ff{s}")[:, :], ALU.mult).then_inc(*took(f"ff{s}"))
                    dve.wait_ge(*read(f"ff{s}", l, m))
                    split_hidden(mlp, s)
                    low_down(2 + s, s, unit(2 + s, NL, m))
            add_rows("m")

    return nc


INPUTS = ["x", "w_in", "ret_gn_w", "swa_sinks", "mla_q_norm_w", "mla_kv_norm_w", "mla_w_uq", "mla_w_ukv", "w_out",
          "ln1_g", "ln1_b", "router_w", "router_bias", "exp_w_gate_up", "exp_w_down", "ln2_g", "ln2_b", "norm1_g_2",
          "w_in_2", "conv_w_2", "conv_b_2", "w_rg_2", "b_rg_2", "w_ig_2", "b_ig_2", "lru_lambda_2", "q_norm_g_2",
          "k_norm_g_2", "w_out_2", "norm2_g_2", "w_up_2", "w_down_2"]


def kernel(**inputs):
    import concourse.bacc as bacc
    from concourse.bass_utils import run_bass_kernel_spmd

    nc = bacc.Bacc("TRN2", target_bir_lowering=False, num_devices=1)
    arrays = {f"in_{n}": np.ascontiguousarray(inputs[n]) for n in INPUTS}
    arrays["in_tables"] = np.ascontiguousarray(np.concatenate(list(tables().values()), axis=1).astype(np.float32))
    aps = {n[3:]: nc.dram_tensor(n, v.shape, mybir.dt.from_np(v.dtype), kind="ExternalInput").ap() for n, v in arrays.items()}
    out = nc.dram_tensor("out", (1, SEQ, D), F32, kind="ExternalOutput").ap()
    build(nc, aps, out)
    r = run_bass_kernel_spmd(nc, [arrays], core_ids=[0])
    return r.results[0]["out"]
```

```python
from contextlib import ExitStack

import numpy as np

import concourse.bass as bass
from concourse import mybir

P = 128
SEQ, D, NL = 256, 1024, 2
T = SEQ // P
KD = D // P
HD = 64
RET_H, SWA_H, SWA_KV, MLA_H = 4, 6, 2, 6
Q_RANK, KV_RANK, NOPE, ROPE_D, MLA_VD = 384, 256, 64, 32, 64
DQ = NOPE + ROPE_D
N_EXP, N_GRP, D_EXP = 16, 4, 256
PER_GRP = N_EXP // N_GRP
ST_H, CONV, D_FF, LRU_W = 8, 4, 4096, 512
FF_CHUNK = 256
N_CHUNK = D_FF // FF_CHUNK
ST_GROUP = 4
C_MLA = (RET_H + SWA_H) * HD // P
ALPHA = float((2 * NL) ** 0.25)
LN_EPS, RMS_EPS = 1e-5, 1e-6
NEG = -1e30
LRU_C = 8.0

C_RQ, C_RV, C_SQ, C_SK, C_SV, C_CQ, C_KR = 0, 512, 1024, 1408, 1536, 1664, 2304
N_LAT = Q_RANK + KV_RANK + ROPE_D
N_SWA = C_CQ - C_SQ

F32 = mybir.dt.float32
F32R = mybir.dt.float32r
ALU = mybir.AluOpType
ACT = mybir.ActivationFunctionType
AX = mybir.AxisListType

LAYER_JOBS = [
    ("xT0", 0), ("xT1", 1), ("xT2", 2), ("xT3", 3),
    ("lat0", 4), ("lat1", 5), ("lat2", 6),
    ("ret_q", 7), ("ret_k", 0), ("lat_ssq", 1),
    ("swa_q01", 2), ("swa_q2k", 3), ("ret_vg0", 7), ("ret_vg1", 0), ("swa_v", 2),
    ("ret_q_swap", 1), ("ret_k_swap", 3),
    ("swa_s1_0", 4), ("swa_s1_1", 5), ("swa_s1_2", 6), ("swa_s0_0", 7), ("swa_s0_1", 0),
    ("mla_q0", 2), ("mla_q1", 1), ("mla_q2", 3),
    ("mla_k0", 4), ("mla_k1", 5), ("mla_k2", 6), ("mla_v0", 7), ("mla_v1", 0),
    ("mla_q_swap0", 2), ("mla_q_swap1", 1), ("mla_q_swap2", 3), ("mla_kr_swap", 4),
    ("ret_s0", 5), ("ret_s1", 6), ("ret_s2", 7), ("ret_s3", 0), ("ret_o", 4),
    ("swa_pT0", 7), ("swa_pT1", 0), ("swa_pT2", 7), ("swa_pT3", 0), ("swa_pT4", 7), ("swa_pT5", 0),
    ("mla_s1_0", 1), ("mla_s1_1", 3), ("mla_s1_2", 2), ("mla_s0_0", 5), ("mla_s0_1", 6),
    ("swa_o0", 5), ("swa_o1", 6), ("ret_oT", 4),
    ("mix0", 0), ("mix1", 1), ("mix2", 2), ("mix3", 3),
    ("mla_pT0", 7), ("mla_pT1", 4), ("mla_pT2", 7), ("mla_pT3", 4), ("mla_pT4", 7), ("mla_pT5", 4),
    ("mla_o0", 5), ("mla_o1", 6),
    ("x1T0", 4), ("x1T1", 5), ("x1T2", 6), ("x1T3", 7),
    ("router", 0), ("gatesT", 1),
    ("y0", 0), ("y1", 1), ("y2", 2), ("y3", 3),
    ("gate0", 4), ("up0", 5), ("gate1", 6), ("up1", 7),
]
FINAL_JOBS = [
    ("n1T0", 0), ("n1T1", 1), ("n1T2", 2), ("n1T3", 3),
    ("gl0", 6), ("gl1", 7), ("xl0", 4), ("xl1", 5), ("q0", 0),
    ("rg0", 4), ("rg1", 5), ("ig0", 6), ("ig1", 7),
    ("q1", 1), ("k0", 2), ("k1", 3),
    ("ssq0", 4), ("ssq1", 5), ("ssq2", 6), ("ssq3", 7), ("v0", 4),
    ("z0", 6), ("z1", 7), ("z2", 2), ("z3", 3), ("v1", 0),
    ("sfx0", 4), ("z4", 6), ("sfx1", 5), ("z5", 7), ("sfx2", 4), ("z6", 2), ("sfx3", 5), ("z7", 3),
    ("out0", 0), ("out1", 1),
    ("sfx4", 4), ("sfx5", 5), ("sfx6", 4), ("sfx7", 5),
    ("att0", 6), ("att1", 7), ("out2", 2), ("out3", 3),
    ("n2T0", 0), ("n2T1", 1), ("n2T2", 2), ("n2T3", 3),
    ("m0", 0), ("m1", 1), ("m2", 2), ("m3", 3),
    ("ff0", 4), ("ff1", 5),
]
PROJ_PAIRS = (2048, 1536, 0, 512, 1024)
PROJ_JOBS = ("gl0", "gl1", "xl0", "xl1", "q0", "q1", "k0", "k1")
REPEATED = {"gate0": N_EXP // 2, "up0": N_EXP // 2, "gate1": N_EXP // 2, "up1": N_EXP // 2,
            "ff0": N_CHUNK // 2, "ff1": N_CHUNK // 2}


def place_jobs(jobs):
    count, where = [0] * 8, {}
    for name, bank in jobs:
        where[name] = (bank, count[bank])
        count[bank] += REPEATED.get(name, 1)
    return where, count


def tables():
    pos = np.arange(SEQ, dtype=np.float32)
    row = np.arange(P)

    def rope_table(dim, first_row):
        half = dim // 2
        inv = (10000.0 ** (-np.arange(0, dim, 2, dtype=np.float32) / np.float32(dim))).astype(np.float32)
        ang = (pos[None, :] * inv[(row - first_row) % half][:, None]).astype(np.float32)
        sign = np.where((row - first_row) % dim < half, -1.0, 1.0)[:, None]
        return np.cos(ang.astype(np.float64)), np.sin(ang.astype(np.float64)) * sign

    def swap_table(dim):
        swap = np.zeros((P, P))
        swap[row, np.where(row % dim < dim // 2, row + dim // 2, row - dim // 2)] = 1.0
        return swap

    cos_r, sin_r = rope_table(HD, 0)
    cos_m, sin_m = rope_table(ROPE_D, NOPE)
    i, j = row[:, None], row[None, :]
    decay = np.zeros((P, RET_H, 3 * P))
    for h in range(RET_H):
        log_g = np.log(1.0 - 2.0 ** (-5.0 - h))
        for block, shift in ((0, 0), (1, P), (2, 0)):
            rel = (j + shift) - i
            decay[:, h, block * P:(block + 1) * P] = np.where(rel >= 0, np.exp(rel * log_g), 0.0) * HD ** -0.5
    low = (i // HD == j // HD).astype(np.float64)
    tie = np.zeros((PER_GRP, PER_GRP))
    for e in range(PER_GRP):
        tie[e, :e] = 1.0
    return {
        "ident": np.eye(P), "ones": np.ones((P, P)), "half_ones": low,
        "swap_r": swap_table(HD), "swap_m": swap_table(ROPE_D),
        "cos_r": cos_r, "sin_r": sin_r, "cos_m": cos_m, "sin_m": sin_m,
        "decay": decay.reshape(P, -1),
        "mask_swa": np.concatenate([np.where(j > i, 0.0, NEG), np.where(j <= i, 0.0, NEG)], 1),
        "mask_mla": np.concatenate([np.zeros((P, P)), np.where(j <= i, 0.0, NEG)], 1),
        "later": (i > j).astype(np.float64),
        "before": (i < j).astype(np.float64),
        "tie": np.broadcast_to(tie.reshape(1, -1), (P, PER_GRP * PER_GRP)),
        "ln_eps": np.full((P, 1), LN_EPS), "rms_eps": np.full((P, 1), RMS_EPS), "one": np.ones((P, 1)),
    }


TABLE_AT, TABLE_W = {}, 0
for _name, _t in tables().items():
    TABLE_AT[_name] = (TABLE_W, _t.shape[1])
    TABLE_W += _t.shape[1]


class Link:

    def __init__(self, eng, sem, start=0):
        self.eng, self.sem, self.start, self.n = eng, sem, start, 0

    def __call__(self, ins):
        ins.then_inc(self.sem, 1)
        self.n += 1
        self.eng.wait_ge(self.sem, self.start + self.n)


def build(nc, a, out):
    ctx = ExitStack()
    with ctx:
        def sb(name, shape):
            return ctx.enter_context(nc.sbuf_tensor(name, shape, F32))

        def sem(name):
            return ctx.enter_context(nc.semaphore(name))

        place = {}

        def region(name, shape):
            place[name] = nc.sbuf_base
            return sb(name, shape)

        def over(name, where, word, shape):
            return nc.alloc_sbuf_tensor_at(name, shape, F32R, offset=place[where] + 4 * word)

        tab = sb("tab", [P, TABLE_W])
        X = sb("X", [P, T, D])
        XT = region("XT", [P, KD, SEQ])
        LNB = sb("LNB", [P, 2, D])
        WA = region("WA", [P, 9472])
        WE = region("WE", [P, 12480])
        WB = region("WB", [P, KD * D])
        AC = region("AC", [P, 10240])
        small = sb("small", [P, 1400])

        UNIT = 2048
        W_LAT_END = KD * N_LAT
        E_SLOT = 6240
        WH = [over("WH0", "AC", 0, [P, UNIT]), over("WH1", "AC", 2 * UNIT, [P, UNIT]), over("WH2", "AC", 4 * UNIT, [P, UNIT]),
              over("WH3", "WB", 0, [P, UNIT])]
        WL = [over("WL0", "AC", UNIT, [P, UNIT]), over("WL1", "AC", 3 * UNIT, [P, UNIT]), over("WL2", "WA", W_LAT_END, [P, UNIT]),
              over("WL3", "WB", UNIT, [P, UNIT])]
        XTH = over("XTH", "WA", W_LAT_END + UNIT, [P, KD, SEQ])
        XTL = over("XTL", "WB", 3 * UNIT, [P, KD, SEQ])
        E_DN = [KD * 2 * D_EXP, E_SLOT + KD * 2 * D_EXP]
        PH = [over("PH0", "WA", 0, [P, KD, 256]), over("PH1", "WB", 2 * UNIT, [P, KD, 256]), over("PH2", "WE", E_DN[1], [P, KD, 256])]
        PL = [over("PL0", "WA", UNIT, [P, KD, 256]), over("PL1", "WE", E_DN[0], [P, KD, 256]), over("PL2", "XT", 0, [P, KD, 256])]
        HIDH = [over(f"HIDH{s}", "XT", s * 1024, [P, 2, SEQ]) for s in range(2)]
        HIDL = [over(f"HIDL{s}", "XT", s * 1024 + 512, [P, 2, SEQ]) for s in range(2)]
        WH_up, WL_up = ([w[:, :].rearrange("p (k n) -> p k n", k=KD) for w in part] for part in (WH, WL))
        WH_dn, WL_dn = ([w[:, :].rearrange("p (c n) -> p c n", c=2) for w in part] for part in (WH, WL))

        def tb(name):
            o, w = TABLE_AT[name]
            return tab[:, o:o + w]

        class Arena:
            def __init__(self, tensor, at=0):
                self.t, self.at, self.size = tensor, at, tensor[:, :].shape[1]

            def take(self, *shape):
                w = int(np.prod(shape))
                v = self.t[:, self.at:self.at + w]
                self.at += w
                assert self.at <= self.size, (self.at, self.size)
                if len(shape) == 2:
                    v = v.rearrange("p (a b) -> p a b", b=shape[1])
                elif len(shape) == 3:
                    v = v.rearrange("p (a b c) -> p a b c", b=shape[1], c=shape[2])
                return v

        ar = Arena(WA)
        w_lat, w_rqk = ar.take(KD, N_LAT), ar.take(KD, C_RV)
        ar = Arena(WE)
        w_rvg, w_swa = ar.take(KD, 512), ar.take(KD, N_SWA)
        w_uq, w_ukv = ar.take(Q_RANK // P, MLA_H * DQ), ar.take(KV_RANK // P, MLA_H * (NOPE + MLA_VD))
        w_gu, w_dn = [], []
        for s in range(2):
            ar = Arena(WE, s * E_SLOT)
            w_gu.append(ar.take(KD, 2 * D_EXP))
            w_dn.append(ar.take(D_EXP // P, D))
        w_gate, w_up = ([w[:, :, n * D_EXP:(n + 1) * D_EXP] for w in w_gu] for n in range(2))
        w_out = Arena(WB).take(KD, D)
        ar = Arena(WA)
        mla_p1, mla_p0, mla_pT = ar.take(MLA_H, SEQ), ar.take(MLA_H, P), ar.take(MLA_H, 3 * P)
        swa_p1, swa_p0, swa_pT = ar.take(SWA_H, SEQ), ar.take(SWA_H, P), ar.take(SWA_H, 3 * P)
        ar = Arena(WB)
        lat_sq, lat_n, lat_rstd = ar.take(5, SEQ), ar.take(5, SEQ), ar.take(2, SEQ)
        rope_m, rope_r, kr_cos = ar.take(MLA_H, SEQ), ar.take(4, SEQ), ar.take(SEQ)
        kr_sin = ar.take(SEQ)
        ar = Arena(WB)
        gates_b = ar.take(N_EXP, SEQ)
        sig = [ar.take(512) for _ in range(2)]
        gatesT = ar.take(SEQ)
        assert ar.at <= 3 * UNIT
        ar = Arena(AC)
        ret_qT, ret_kT = ar.take(2, SEQ), ar.take(2, SEQ)
        swa_qT, swa_kT = ar.take(3, SEQ), ar.take(SEQ)
        ret_v, ret_g, swa_v = ar.take(T, 256), ar.take(T, 256), ar.take(T, P)
        mla_qT, mla_kT, mla_v = ar.take(MLA_H, SEQ), ar.take(MLA_H, SEQ), ar.take(T, MLA_H * MLA_VD)
        krT, ret_pT = ar.take(SEQ), ar.take(RET_H, 3 * P)
        ret_c, ret_sq = ar.take(T * RET_H, HD), ar.take(T * RET_H, HD)
        ar = Arena(AC)
        st_qT, st_kT, st_v = ar.take(4, SEQ), ar.take(4, SEQ), ar.take(T, 512)
        xl_pad = ar.take(4, SEQ + CONV - 1)
        conv_u, glT, rgT, igT, lruA = (ar.take(4, SEQ) for _ in range(5))
        lruT = Arena(AC, 3 * 1024).take(4, SEQ)
        xn = LNB[:, :, :]
        gel, lruH = LNB[:, 0, :].rearrange("p (a b) -> p a b", b=SEQ), LNB[:, 1, :].rearrange("p (a b) -> p a b", b=SEQ)
        ar = Arena(WB)
        qk_sq, qk_rstd = ar.take(4, 512), ar.take(4, 512)
        square_out = WB[:, 0:D], WA[:, 0:D]
        stS, stL, stW = (Arena(t, at).take(ST_H, 3 * P) for t, at in ((WE, 0), (WE, E_SLOT), (WA, 2 * UNIT)))
        w_bd = sb("w_bd", [P, 2, 4, P])
        ar = Arena(small)
        qn_g, kvn_g, gn_b, sink_b = ar.take(3), ar.take(2), ar.take(256), ar.take(SWA_H)
        router, rbias = ar.take(KD, N_EXP), ar.take(N_EXP)
        mx = {"swa": ar.take(T, 6), "mla": ar.take(T, 6)}
        nmx = {"swa": ar.take(T, 6), "mla": ar.take(T, 6)}
        psm = {"swa": ar.take(T, 6), "mla": ar.take(T, 6)}
        rin = {"swa": ar.take(T, 6), "mla": ar.take(T, 6)}
        sk_e = ar.take(T, 6)
        gmu, gvar, grs = ar.take(8), ar.take(8), ar.take(8)
        st6, mv2, lrs = ar.take(T, 2 * 6), ar.take(T, 2), ar.take(T, 1)
        sc, bi, pr, gs = ar.take(32), ar.take(8, 4), ar.take(8, 6), ar.take(8)
        c1, c2 = ar.take(8, 4, 4), ar.take(8, 4, 4)
        g1, g2 = ar.take(2, 4, 4), ar.take(2, 4, 4)
        gsel, esel, gden, gates = ar.take(8), ar.take(8, 4), ar.take(2), ar.take(2, N_EXP)
        n1g, n2g = ar.take(KD), ar.take(KD)
        qg2, kg2 = ar.take(1), ar.take(1)
        cw, cb = ar.take(CONV, 4), ar.take(4)
        brg, big, lam = ar.take(4), ar.take(4), ar.take(4)
        sp_e, sp_s, sp_s2, sp_p = ar.take(4), ar.take(4), ar.take(4), ar.take(4)
        rss, marks = ar.take(T), ar.take(8 + T + 2)
        ident, ones = tb("ident"), tb("ones")
        decay = tb("decay").rearrange("p (h c) -> p h c", h=RET_H)
        tie = tb("tie").rearrange("p (a b) -> p a b", b=PER_GRP)
        psum = [ctx.enter_context(nc.psum_tensor(f"bank{b}", [P, 512], F32)) for b in range(8)]
        gates_dram = nc.dram_tensor("gates_scratch", [NL, N_EXP, SEQ], F32, kind="Internal").ap()

        psum_full = [sem(f"psum_full{b}") for b in range(8)]
        psum_read = [sem(f"psum_read{b}") for b in range(8)]
        in_layer, per_layer = place_jobs(LAYER_JOBS)
        in_final, _ = place_jobs(FINAL_JOBS)

        def count_of(name, l):
            bank, n = (in_layer if name in in_layer else in_final)[name]
            return bank, l * per_layer[bank] + n

        def free(name, l, m=0):
            bank, n = count_of(name, l)
            return psum_read[bank], n + m + 1

        def full(name, l, m=0):
            bank, n = count_of(name, l)
            return psum_full[bank], n + m + 1

        def read(name, l, m=0):
            bank, n = count_of(name, l)
            return psum_read[bank], n + m + 2

        def bank(name):
            return psum[(in_layer if name in in_layer else in_final)[name][0]]

        def made(name):
            return psum_full[(in_layer if name in in_layer else in_final)[name][0]], 1

        def took(name):
            return psum_read[(in_layer if name in in_layer else in_final)[name][0]], 1

        ident_in, tab_in, router_in, final_in, bd_in = (sem(n) for n in ("ident_in", "tab_in", "router_in", "final_in", "bd_in"))
        wlat2_in, wout2_in = sem("wlat2_in"), sem("wout2_in")
        x_in = [sem(f"x_in{t}") for t in range(T)]
        wlat_in, wrqk_in, wrvg_in, wswa_in, wup_in, wout_in = (
            sem(n) for n in ("wlat_in", "wrqk_in", "wrvg_in", "wswa_in", "wup_in", "wout_in"))
        norms_in, ln1_in, ln2_in, gates_in, gates_out = (sem(n) for n in ("norms_in", "ln1_in", "ln2_in", "gates_in", "gates_out"))
        gu_in, dn_in = [sem(f"gu_in{s}") for s in range(2)], [sem(f"dn_in{s}") for s in range(2)]
        x_ready = sem("x_ready")
        lat_squared, kr_copied = sem("lat_squared"), sem("kr_copied")
        rows_turned = sem("rows_turned")
        rstd_ready = sem("rstd_ready")
        ret_cos, ret_roped = sem("ret_cos"), sem("ret_roped")
        ret_gate_w, q_roped, k_roped = sem("ret_gate_w"), sem("q_roped"), sem("k_roped")
        maxed = {n: sem(f"{n}_maxed") for n in ("swa", "mla")}
        expd = {n: sem(f"{n}_expd") for n in ("swa", "mla")}
        normed = {n: sem(f"{n}_normed") for n in ("swa", "mla")}
        gn_squared, gn_var, gn_rooted, ret_out = (sem(n) for n in ("gn_squared", "gn_var", "gn_rooted", "ret_out"))
        ln_var, ln_centred, ln_rooted, ln_rstd, x1_ready = (sem(n) for n in ("ln_var", "ln_centred", "ln_rooted", "ln_rstd", "x1_ready"))
        gates_ready, expert_used = sem("gates_ready"), sem("expert_used")
        dve_link, pool_link = sem("dve_link"), sem("pool_link")
        high_made, low_made = ([sem(f"{n}_made{s}") for s in range(4)] for n in ("high", "low"))
        xt_high, xt_low = sem("xt_high"), sem("xt_low")
        hid_ready = sem("hid_ready")
        dve_moe, dve_fin, act_fin = sem("dve_moe"), sem("dve_fin"), sem("act_fin")
        proj_in = [sem(f"proj_in{s}") for s in range(2)]
        proj_high, proj_low = ([sem(f"proj_{n}{s}") for s in range(3)] for n in ("high", "low"))
        rms_rooted, rms_rstd, rms_rows = (sem(n) for n in ("rms_rooted", "rms_rstd", "rms_rows"))
        qk_squared, qk_rstd_ok = sem("qk_squared"), sem("qk_rstd_ok")
        bd_zero, pad_zero, conv_done = sem("bd_zero"), sem("pad_zero"), sem("conv_done")
        consts2 = sem("consts2")
        log1pd, soft, masked_sp = sem("log1pd"), sem("soft"), sem("masked_sp")
        wexp, w_masked = sem("wexp"), sem("w_masked")
        lru_la, lru_at, lru_m2, lru_sq, gel_in, gel_t, lru_mix, sp_lam = (
            sem(n) for n in ("lru_la", "lru_at", "lru_m2", "lru_sq", "gel_in", "gel_t", "lru_mix", "sp_lam"))
        up_in, down_in = [sem(f"up_in{s}") for s in range(2)], [sem(f"down_in{s}") for s in range(2)]
        ff_used, relu_done, stored = sem("ff_used"), sem("relu_done"), sem("stored")

        def token(t):
            return slice(t * P, (t + 1) * P)

        def spread(ap, axis, shape):
            return ap.unsqueeze(axis).to_broadcast(shape)

        DVE_LINKS, POOL_LINKS, MOE_LINKS = 33, 2, 2

        SLOT_UNITS = (N_EXP + 1, N_EXP, N_EXP - 1, 0)

        def unit(slot, l, e):
            return l * SLOT_UNITS[slot] + e + 1 if SLOT_UNITS[slot] else e + 1

        def hidden(l, e):
            return l * N_EXP + e + 2

        block = ctx.enter_context(nc.Block())

        @block.sync
        def _(sp):
            for t in range(T):
                sp.dma_start(X[:, t, :], a["x"][0, t * P:(t + 1) * P, :]).then_inc(x_in[t], 16)
            with sp.Fori(0, NL) as l:
                w = a["w_in"][bass.ds(l, 1)].rearrange("o (p k) n -> p (o k) n", k=KD)
                sp.dma_start(w_lat[:, :, 0:2 * P], w[:, :, C_CQ:C_CQ + 2 * P]).then_inc(wlat_in, 16)
                sp.dma_start(w_lat[:, :, 2 * P:N_LAT], w[:, :, C_CQ + 2 * P:C_CQ + N_LAT]).then_inc(wlat2_in, 16)
                sp.wait_ge(psum_read[3], l * per_layer[3] + 1)
                for m in range(3):
                    for g in range(2):
                        sp.dma_start(w_swa[:, :, m * P + g * HD:m * P + (g + 1) * HD],
                                     w[:, :, C_SQ + (3 * g + m) * HD:C_SQ + (3 * g + m + 1) * HD]).then_inc(wswa_in, 16)
                sp.dma_start(w_rqk, w[:, :, C_RQ:C_RV]).then_inc(wrqk_in, 16)
                sp.dma_start(w_swa[:, :, C_SK - C_SQ:N_SWA], w[:, :, C_SK:C_CQ]).then_inc(wswa_in, 16)
                sp.dma_start(w_rvg, w[:, :, C_RV:C_SQ]).then_inc(wrvg_in, 16)
                sp.dma_start(w_uq, a["mla_w_uq"][bass.ds(l, 1)].rearrange("o (c p) n -> p (o c) n", p=P)).then_inc(wup_in, 16)
                sp.dma_start(w_ukv, a["mla_w_ukv"][bass.ds(l, 1)].rearrange("o (c p) n -> p (o c) n", p=P)).then_inc(wup_in, 16)
                sp.wait_ge(k_roped, l + 2)
                wo = a["w_out"][bass.ds(l, 1)].rearrange("o (c p) n -> p (o c) n", p=P)
                sp.dma_start(w_out[:, 0:C_MLA, :], wo[:, 0:C_MLA, :]).then_inc(wout_in, 16)
                sp.dma_start(w_out[:, C_MLA:KD, :], wo[:, C_MLA:KD, :]).then_inc(wout2_in, 16)

                def load_gate_up(e, s):
                    sp.dma_start(w_gu[s], a["exp_w_gate_up"][bass.ds(l, 1), bass.ds(e, 1)].rearrange(
                        "o e (p k) n -> p (o e k) n", k=KD)).then_inc(gu_in[s], 16)

                def load_down(e, s):
                    sp.dma_start(w_dn[s], a["exp_w_down"][bass.ds(l, 1), bass.ds(e, 1)].rearrange(
                        "o e (c p) n -> p (o e c) n", p=P)).then_inc(dn_in[s], 16)

                for s in range(2):
                    load_gate_up(s, s)
                    load_down(s, s)
                sp.wait_ge(x1_ready, (l + 1) * T)
                sp.dma_start(LNB[:, 0, :], a["ln2_g"][bass.ds(l, 1)].rearrange("o n -> (o n)").partition_broadcast(P)).then_inc(ln2_in, 16)
                sp.dma_start(LNB[:, 1, :], a["ln2_b"][bass.ds(l, 1)].rearrange("o n -> (o n)").partition_broadcast(P)).then_inc(ln2_in, 16)
                with sp.Fori(1, N_EXP // 2) as m:
                    for s in range(2):
                        sp.wait_ge(low_made[1], unit(1, l, 2 * m + (s - 2)))
                        load_gate_up(2 * m + s, s)
                        sp.wait_ge(low_made[2], unit(2, l, 2 * m + (s - 2)))
                        load_down(2 * m + s, s)
            w2 = a["w_in_2"][0].rearrange("(p k) n -> p k n", k=KD)
            for p, col in enumerate(PROJ_PAIRS):
                if p < 2:
                    sp.wait_ge(low_made[1], unit(1, NL - 1, N_EXP - 2 + p))
                else:
                    u = 2 * p - 3
                    sp.wait_ge(proj_low[u % 3], u // 3 + 1)
                sp.dma_start(w_gu[p % 2], w2[:, :, col:col + 512]).then_inc(proj_in[p % 2], 16)
            for n in ("q0", "q1", "k0", "k1"):
                sp.wait_ge(*read(n, NL))
            wo = a["w_out_2"][0].rearrange("(c p) n -> p c n", p=P)
            sp.dma_start(w_out[:, 0:6, :], wo[:, 0:6, :]).then_inc(wout_in, 16)
            sp.wait_ge(*full("v1", NL))
            sp.dma_start(w_out[:, 6:KD, :], wo[:, 6:KD, :]).then_inc(wout2_in, 16)
            sp.wait_ge(*full("att1", NL))

            def load_up(c, s):
                sp.dma_start(w_gu[s][:, :, 0:FF_CHUNK], a["w_up_2"][0].rearrange("(p k) n -> p k n", k=KD)[
                    :, :, bass.ds(c * FF_CHUNK, FF_CHUNK)]).then_inc(up_in[s], 16)

            def load_ff_down(c, s):
                sp.dma_start(w_dn[s], a["w_down_2"][0].rearrange("(g c p) n -> g p c n", c=2, p=P)[
                    bass.ds(c, 1)].rearrange("g p c n -> p (g c) n")).then_inc(down_in[s], 16)

            for s in range(2):
                load_up(s, s)
                load_ff_down(s, s)
            with sp.Fori(1, N_CHUNK // 2) as m:
                for s in range(2):
                    sp.wait_ge(low_made[s], unit(s, NL, m - 1))
                    load_up(2 * m + s, s)
                    sp.wait_ge(low_made[2 + s], unit(2 + s, NL, m - 1))
                    load_ff_down(2 * m + s, s)
            o = out.rearrange("o (t p) d -> p (o t) d", p=P)
            for t in range(T):
                sp.wait_ge(*read(f"m{2 * t}", NL))
                sp.wait_ge(*read(f"m{2 * t + 1}", NL))
                sp.dma_start(o[:, t, :], X[:, t, :]).then_inc(stored, 16)
            sp.wait_ge(stored, 16 * T)

        @block.gpsimd
        def _(pool):
            with nc.allow_non_contiguous_dma(reason="small vectors"):
                pool.dma_start(router, a["router_w"].rearrange("(p k) e -> p k e", k=KD)).then_inc(router_in, 16)
                pool.dma_start(rbias, a["router_bias"].partition_broadcast(P)).then_inc(router_in, 16)
            nc.gpsimd.memset(marks[:, 8 + T:9 + T], 0.0).then_inc(k_roped, 1)

            def low_part(slot, raw, n):
                pool.wait_ge(high_made[slot], n)
                nc.gpsimd.tensor_tensor(WL_up[slot], raw, WH_up[slot].bitcast(F32), ALU.subtract).then_inc(low_made[slot], 1)

            with pool.Fori(0, NL) as l:
                link = Link(pool, pool_link, l * POOL_LINKS)
                with nc.allow_non_contiguous_dma(reason="small vectors"):
                    pool.wait_ge(x_ready, (l + 1) * T)
                    pool.dma_start(qn_g, a["mla_q_norm_w"][bass.ds(l, 1)].rearrange("o (c p) -> p (o c)", p=P)).then_inc(norms_in, 16)
                    pool.dma_start(kvn_g, a["mla_kv_norm_w"][bass.ds(l, 1)].rearrange("o (c p) -> p (o c)", p=P)).then_inc(norms_in, 16)
                    pool.dma_start(gn_b, a["ret_gn_w"][bass.ds(l, 1)].rearrange("o n -> (o n)").partition_broadcast(P)).then_inc(norms_in, 16)
                    pool.dma_start(sink_b, a["swa_sinks"][bass.ds(l, 1)].rearrange("o n -> (o n)").partition_broadcast(P)).then_inc(norms_in, 16)
                pool.dma_start(LNB[:, 0, :], a["ln1_g"][bass.ds(l, 1)].rearrange("o n -> (o n)").partition_broadcast(P)).then_inc(ln1_in, 16)
                pool.dma_start(LNB[:, 1, :], a["ln1_b"][bass.ds(l, 1)].rearrange("o n -> (o n)").partition_broadcast(P)).then_inc(ln1_in, 16)
                pool.wait_ge(k_roped, l + 1)
                pool.wait_ge(tab_in, 16)
                for n, (src, name) in enumerate(((ret_qT, "ret_q"), (ret_kT, "ret_k"))):
                    pool.wait_ge(*read(name, l))
                    nc.gpsimd.tensor_tensor(rope_r[:, 2 * n:2 * n + 2, :], src, spread(tb("cos_r"), 1, [P, 2, SEQ]),
                                            ALU.mult).then_inc(ret_cos, 1)
                pool.wait_ge(norms_in, (l + 1) * 64)
                for t in range(T):
                    pool.wait_ge(*read(f"ret_vg{t}", l))
                nc.gpsimd.tensor_tensor(ret_g, ret_g, spread(gn_b, 1, [P, T, 256]), ALU.mult).then_inc(ret_gate_w, 1)
                rows = slice(NOPE, DQ)
                cos, shape = tb("cos_m")[rows], [ROPE_D, MLA_H, SEQ]
                pool.wait_ge(ret_gate_w, l + 1)
                for n in range(3):
                    pool.wait_ge(*full(f"mla_q_swap{n}", l))
                link(nc.gpsimd.tensor_tensor(mla_qT[rows], mla_qT[rows], spread(cos, 1, shape), ALU.mult))
                for n in range(3):
                    pool.wait_ge(*read(f"mla_q_swap{n}", l))
                nc.gpsimd.tensor_tensor(mla_qT[rows], mla_qT[rows], rope_m[rows], ALU.add).then_inc(q_roped, 1)
                link(nc.gpsimd.tensor_tensor(kr_cos[rows], krT[rows], cos, ALU.mult))
                pool.wait_ge(*read("mla_kr_swap", l))
                nc.gpsimd.tensor_tensor(mla_kT[rows], spread(kr_cos[rows], 1, shape), spread(kr_sin[rows], 1, shape),
                                        ALU.add).then_inc(k_roped, 1)
                assert link.n == POOL_LINKS

                low_part(0, w_gate[0], unit(0, l, 0))
                low_part(1, w_up[0], unit(1, l, 0))
                with pool.Fori(1, N_EXP // 2) as m:
                    for e, s in ((2 * m - 1, 1), (2 * m, 0)):
                        low_part(0, w_gate[s], unit(0, l, e))
                        low_part(1, w_up[s], unit(1, l, e))
                low_part(0, w_gate[1], unit(0, l, N_EXP - 1))
                low_part(1, w_up[1], unit(1, l, N_EXP - 1))
            pool.wait_ge(k_roped, NL + 1)
            nc.gpsimd.memset(w_bd[:, :, :, :], 0.0).then_inc(bd_zero, 1)
            pool.wait_ge(bd_zero, 1)
            with nc.allow_non_contiguous_dma(reason="small vectors"):
                for n, name in enumerate(("w_rg_2", "w_ig_2")):
                    for half in range(2):
                        pool.dma_start(w_bd[half * HD:(half + 1) * HD, n, :, half * HD:(half + 1) * HD],
                                       a[name][0].rearrange("(c h) i o -> h i c o", h=2)[half]).then_inc(bd_in, 16)
                n_final = 0
                for dst, src in (
                    (n1g, a["norm1_g_2"].rearrange("o (p k) -> p (o k)", k=KD)),
                    (n2g, a["norm2_g_2"].rearrange("o (p k) -> p (o k)", k=KD)),
                    (qg2[0:HD], a["q_norm_g_2"].rearrange("o p -> p o")), (qg2[HD:P], a["q_norm_g_2"].rearrange("o p -> p o")),
                    (kg2[0:HD], a["k_norm_g_2"].rearrange("o p -> p o")), (kg2[HD:P], a["k_norm_g_2"].rearrange("o p -> p o")),
                    (cb, a["conv_b_2"].rearrange("o (c p) -> p (o c)", p=P)),
                    (brg, a["b_rg_2"].rearrange("o (c p) -> p (o c)", p=P)),
                    (big, a["b_ig_2"].rearrange("o (c p) -> p (o c)", p=P)),
                    (lam, a["lru_lambda_2"].rearrange("o (c p) -> p (o c)", p=P)),
                ) + tuple((cw[:, k, :], a["conv_w_2"][0, k].rearrange("(c p) -> p c", p=P)) for k in range(CONV)):
                    pool.dma_start(dst, src).then_inc(final_in, 16)
                    n_final += 1
            assert n_final == 14
            for u in range(2 * len(PROJ_PAIRS)):
                pool.wait_ge(proj_high[u % 3], u // 3 + 1)
                raw = (w_gate, w_up)[u % 2][u // 2 % 2]
                nc.gpsimd.tensor_tensor(PL[u % 3][:, :, :], raw, PH[u % 3][:, :, :].bitcast(F32), ALU.subtract
                                        ).then_inc(proj_low[u % 3], 1)
            strict = tb("before")

            def mask_weights(h):
                pool.wait_ge(wexp, h + 1)
                v = stW[:, h, :].rearrange("p (b c) -> p b c", c=P)[:, 0:3:2, :]
                nc.gpsimd.tensor_tensor(v, v, spread(strict, 1, [P, 2, P]), ALU.mult).then_inc(w_masked, 1)

            for h in range(ST_H):
                pool.wait_ge(soft, h + 1)
                v = stS[:, h, :].rearrange("p (b c) -> p b c", c=P)[:, 0:3:2, :]
                nc.gpsimd.tensor_tensor(v, v, spread(strict, 1, [P, 2, P]), ALU.mult).then_inc(masked_sp, 1)
                if h % ST_GROUP == ST_GROUP - 1:
                    for g in range(h + 1 - ST_GROUP, h + 1):
                        mask_weights(g)
            with pool.Fori(0, N_CHUNK // 2) as m:
                for s in range(2):
                    low_part(s, w_gate[s], unit(s, NL, m))

        @block.scalar
        def _(act):
            act.dma_start(ident, a["tables"][:, 0:P]).then_inc(ident_in, 16)

            def softmax_exp(name, l, p1, p0, scale):
                act.wait_ge(maxed[name], l + 1)
                for h in range(6):
                    nc.scalar.activation(p0[:, h, :], p0[:, h, :], ACT.Exp, bias=nmx[name][:, 0, h:h + 1], scale=scale,
                                         accum_out=psm[name][:, 0, h:h + 1])
                    ins = nc.scalar.activation(p1[:, h, :], p1[:, h, :], ACT.Exp, bias=nmx[name][:, 1, h:h + 1],
                                               scale=scale, accum_out=psm[name][:, 1, h:h + 1])
                if name == "swa":
                    ins = nc.scalar.activation(sk_e, sk_e, ACT.Exp)
                ins.then_inc(expd[name], 1)

            def high_up(slot, raw):
                nc.scalar.copy(WH_up[slot], raw).then_inc(high_made[slot], 1)

            def high_down(slot, s, loaded, n):
                act.wait_ge(loaded[s], n * 16)
                nc.scalar.copy(WH_dn[slot], w_dn[s]).then_inc(high_made[slot], 1)

            def split_xt(prefix, l):
                for n in range(4):
                    act.wait_ge(*read(f"{prefix}{n}", l))
                    nc.scalar.copy(XTH[:, 2 * n:2 * n + 2, :], XT[:, 2 * n:2 * n + 2, :]).then_inc(xt_high, 1)

            act.wait_ge(wlat_in, 16)
            act.dma_start(tab[:, P:], a["tables"][:, P:]).then_inc(tab_in, 16)
            def deviations(l, which):
                for t in range(T):
                    act.wait_ge(ln_var, l * 2 * T + which * T + (t + 1))
                    nc.scalar.activation(lrs[:, t, :], mv2[:, t, 1:2], ACT.Sqrt, bias=tb("ln_eps")).then_inc(ln_rooted, 1)

            with act.Fori(0, NL) as l:
                for n in (0, 2):
                    act.wait_ge(*full(f"xT{n}", l))
                    nc.scalar.copy(XT[:, 2 * n:2 * n + 2, :], bank(f"xT{n}")[:, :]).then_inc(*took(f"xT{n}"))
                for n, w in ((0, 512), (1, 512), (2, 256)):
                    act.wait_ge(*full(f"lat{n}", l))
                    nc.scalar.activation(lat_sq[:, 2 * n:2 * n + w // SEQ, :], bank(f"lat{n}")[:, 0:w],
                                         ACT.Square).then_inc(lat_squared, 1)
                turn = slice(NOPE, DQ)
                nc.scalar.copy(krT[turn, :], bank("lat2")[turn, SEQ:2 * SEQ]).then_inc(kr_copied, 1)
                act.wait_ge(*full("ret_q", l))
                nc.scalar.copy(ret_qT, bank("ret_q")[:, :]).then_inc(*took("ret_q"))
                act.wait_ge(*full("ret_k", l))
                nc.scalar.copy(ret_kT, bank("ret_k")[:, :]).then_inc(*took("ret_k"))
                act.wait_ge(tab_in, 16)
                act.wait_ge(*full("lat_ssq", l))
                nc.scalar.activation(lat_rstd[:, 0, :], bank("lat_ssq")[:, 0:SEQ], ACT.Ln, bias=tb("rms_eps"), scale=1.0 / Q_RANK)
                nc.scalar.activation(lat_rstd[:, 1, :], bank("lat_ssq")[:, SEQ:2 * SEQ], ACT.Ln, bias=tb("rms_eps"),
                                     scale=1.0 / KV_RANK).then_inc(*took("lat_ssq"))
                act.wait_ge(*read("lat_ssq", l))
                nc.scalar.activation(lat_rstd, lat_rstd, ACT.Exp, scale=-0.5).then_inc(rstd_ready, 1)
                act.wait_ge(*full("swa_q01", l))
                nc.scalar.mul(swa_qT[:, 0:2, :], bank("swa_q01")[:, :], HD ** -0.5).then_inc(*took("swa_q01"))
                act.wait_ge(*full("swa_q2k", l))
                nc.scalar.mul(swa_qT[:, 2, :], bank("swa_q2k")[:, 0:SEQ], HD ** -0.5)
                nc.scalar.copy(swa_kT, bank("swa_q2k")[:, SEQ:2 * SEQ]).then_inc(*took("swa_q2k"))
                for t in range(T):
                    act.wait_ge(*full(f"ret_vg{t}", l))
                    nc.scalar.copy(ret_v[:, t, :], bank(f"ret_vg{t}")[:, 0:256])
                    nc.scalar.activation(ret_g[:, t, :], bank(f"ret_vg{t}")[:, 256:512], ACT.Silu).then_inc(*took(f"ret_vg{t}"))
                act.wait_ge(*full("swa_v", l))
                nc.scalar.copy(swa_v, bank("swa_v")[:, 0:T * P]).then_inc(*took("swa_v"))
                for n in range(3):
                    act.wait_ge(*full(f"mla_q{n}", l))
                    nc.scalar.copy(mla_qT[0:DQ, 2 * n:2 * n + 2, :], bank(f"mla_q{n}")[0:DQ, :]).then_inc(*took(f"mla_q{n}"))
                softmax_exp("swa", l, swa_p1, swa_p0, 1.0)
                for t in range(T):
                    act.wait_ge(*full(f"mla_v{t}", l))
                    nc.scalar.copy(mla_v[:, t, :], bank(f"mla_v{t}")[:, 0:MLA_H * MLA_VD]).then_inc(*took(f"mla_v{t}"))
                act.wait_ge(*read("ret_o", l))
                nc.scalar.activation(ret_sq, ret_c, ACT.Square).then_inc(gn_squared, 1)
                for h in range(0, 6, 2):
                    act.wait_ge(*full(f"swa_pT{h}", l))
                    nc.scalar.copy(swa_pT[:, h, :], bank(f"swa_pT{h}")[:, 0:3 * P]).then_inc(*took(f"swa_pT{h}"))
                act.wait_ge(gn_var, l + 1)
                nc.scalar.activation(grs, gvar, ACT.Sqrt, bias=tb("ln_eps"), scale=1.0 / HD).then_inc(gn_rooted, 1)
                act.wait_ge(*full("swa_o0", l))
                nc.scalar.copy(XT[:, 2:4, :], bank("swa_o0")[:, :]).then_inc(*took("swa_o0"))
                act.wait_ge(*full("swa_o1", l))
                nc.scalar.copy(XT[:, 4, :], bank("swa_o1")[:, 0:SEQ]).then_inc(*took("swa_o1"))
                act.wait_ge(*full("ret_oT", l))
                nc.scalar.copy(XT[:, 0:2, :], bank("ret_oT")[:, :]).then_inc(*took("ret_oT"))
                softmax_exp("mla", l, mla_p1, mla_p0, DQ ** -0.5)
                for h in range(0, 6, 2):
                    act.wait_ge(*full(f"mla_pT{h}", l))
                    nc.scalar.copy(mla_pT[:, h, :], bank(f"mla_pT{h}")[:, 0:3 * P]).then_inc(*took(f"mla_pT{h}"))
                act.wait_ge(*full("mla_o0", l))
                nc.scalar.copy(XT[:, 5:7, :], bank("mla_o0")[:, :]).then_inc(*took("mla_o0"))
                act.wait_ge(*full("mla_o1", l))
                nc.scalar.copy(XT[:, 7, :], bank("mla_o1")[:, 0:SEQ]).then_inc(*took("mla_o1"))
                act.wait_ge(gu_in[0], (l * (N_EXP // 2) + 1) * 16)
                high_up(0, w_gate[0])
                high_up(1, w_up[0])
                high_down(2, 0, dn_in, l * (N_EXP // 2) + 1)
                deviations(l, 0)
                for n in (0, 2):
                    act.wait_ge(*full(f"x1T{n}", l))
                    nc.scalar.copy(XT[:, 2 * n:2 * n + 2, :], bank(f"x1T{n}")[:, :]).then_inc(*took(f"x1T{n}"))
                split_xt("x1T", l)
                act.wait_ge(*full("router", l))
                nc.scalar.activation(sc, bank("router")[:, 0:2 * N_EXP], ACT.Exp, scale=-1.0).then_inc(*took("router"))

                def gates_to_dram():
                    act.wait_ge(*full("gatesT", l))
                    nc.scalar.copy(gatesT[0:N_EXP, :], bank("gatesT")[0:N_EXP, 0:SEQ]).then_inc(*took("gatesT"))
                    act.wait_ge(*read("gatesT", l))
                    act.dma_start(gates_dram[bass.ds(l, 1)].rearrange("o e t -> (o e) t"), gatesT[0:N_EXP, :]).then_inc(gates_out, 16)

                def gates_from_dram():
                    act.wait_ge(gates_out, (l + 1) * 16)
                    act.dma_start(gates_b, gates_dram[bass.ds(l, 1)].rearrange("o e t -> (o e t)").partition_broadcast(P)
                                  ).then_inc(gates_in, 16)

                def expert_step(m, s, first=False, last=False):
                    e = 2 * m + s
                    if not first:
                        act.wait_ge(hid_ready, hidden(l, e - 2))
                    act.wait_ge(*full(f"gate{s}", l, m))
                    nc.scalar.activation(sig[s], bank(f"gate{s}")[:, :], ACT.Silu).then_inc(*took(f"gate{s}"))
                    if not last:
                        act.wait_ge(gu_in[1 - s], (l * (N_EXP // 2) + m + (s + 1)) * 16)
                        high_up(0, w_gate[1 - s])
                        if first:
                            gates_to_dram()
                            gates_from_dram()
                        act.wait_ge(*full(f"up{s}", l, m))
                        high_up(1, w_up[1 - s])
                    if last:
                        high_down(0, s, dn_in, l * (N_EXP // 2) + m + 1)
                    elif not first:
                        act.wait_ge(expert_used, l * (N_EXP - 1) + e)
                        high_down(2, s, dn_in, l * (N_EXP // 2) + m + 1)

                expert_step(0, 0, first=True)
                with act.Fori(1, N_EXP // 2) as m:
                    expert_step(m - 1, 1)
                    expert_step(m, 0)
                expert_step(N_EXP // 2 - 1, 1, last=True)
                deviations(l, 1)

            link = Link(act, act_fin)

            def high_unit(u):
                if u % 2 == 0:
                    act.wait_ge(proj_in[u // 2 % 2], (u // 4 + 1) * 16)
                if u >= 3:
                    act.wait_ge(*full(PROJ_JOBS[u - 3], NL))
                nc.scalar.copy(PH[u % 3][:, :, :], (w_gate, w_up)[u % 2][u // 2 % 2]).then_inc(proj_high[u % 3], 1)

            def rms_rows_of(n):
                for t in range(T):
                    if n == 0:
                        act.wait_ge(x_ready, NL * T + t + 1)
                    else:
                        act.wait_ge(*read(f"out{2 * t}", NL))
                        act.wait_ge(*read(f"out{2 * t + 1}", NL))
                    r = rss[:, t:t + 1]
                    link(nc.scalar.activation(square_out[n], X[:, t, :], ACT.Square, accum_out=r))
                    nc.scalar.activation(r, r, ACT.Sqrt, bias=tb("rms_eps"), scale=1.0 / D).then_inc(rms_rooted, 1)
                    if n == 0:
                        high_unit(t)

            act.wait_ge(final_in, 14 * 16)
            rms_rows_of(0)
            def high_features(prefix, gain):
                for n in range(4):
                    act.wait_ge(*full(f"{prefix}{n}", NL))
                    for k in (2 * n, 2 * n + 1):
                        ins = nc.scalar.activation(XTH[:, k, :], bank(f"{prefix}{n}")[:, (k % 2) * SEQ:(k % 2 + 1) * SEQ], ACT.Copy,
                                                   scale=gain[:, k:k + 1])
                    ins.then_inc(xt_high, 1)

            high_features("n1T", n1g)
            high_unit(2)
            for n in range(2):
                act.wait_ge(*full(f"gl{n}", NL))
                nc.scalar.copy(glT[:, 2 * n:2 * n + 2, :], bank(f"gl{n}")[:, :]).then_inc(*took(f"gl{n}"))
                high_unit(3 + n)
            act.wait_ge(pad_zero, 1)
            for n in range(2):
                act.wait_ge(*full(f"xl{n}", NL))
                nc.scalar.copy(xl_pad[:, 2 * n:2 * n + 2, CONV - 1:], bank(f"xl{n}")[:, :].rearrange("p (a b) -> p a b", b=SEQ)
                               ).then_inc(*took(f"xl{n}"))
                high_unit(5 + n)
            act.wait_ge(consts2, 1)
            nc.scalar.activation(sp_e, sp_e, ACT.Exp).then_inc(sp_lam, 1)
            act.wait_ge(gel_in, 1)
            nc.scalar.activation(gel, gel, ACT.Tanh, scale=float(np.sqrt(2.0 / np.pi))).then_inc(gel_t, 1)

            def squares(n):
                name = ("q0", "q1", "k0", "k1")[n]
                act.wait_ge(*full(name, NL))
                nc.scalar.activation(qk_sq[:, n, :], bank(name)[:, :], ACT.Square).then_inc(qk_squared, 1)

            squares(0)
            high_unit(7)
            for n, (dst, b) in enumerate(((rgT, brg), (igT, big))):
                for c in range(4):
                    name = ("rg0", "rg1", "ig0", "ig1")[2 * n + c // 2]
                    if c % 2 == 0:
                        act.wait_ge(*full(name, NL))
                    ins = nc.scalar.activation(dst[:, c, :], bank(name)[:, (c % 2) * SEQ:(c % 2 + 1) * SEQ], ACT.Sigmoid,
                                               bias=b[:, c:c + 1])
                    if c % 2 == 1:
                        ins.then_inc(*took(name))
            act.wait_ge(lru_la, 1)
            nc.scalar.activation(lruA, rgT, ACT.Exp)
            nc.scalar.activation(lruT, rgT, ACT.Tanh, scale=-1.0).then_inc(lru_at, 1)
            act.wait_ge(lru_m2, 1)
            nc.scalar.activation(lruT, lruT, ACT.Sqrt).then_inc(lru_sq, 1)
            for n in range(1, 4):
                squares(n)
                if n < 3:
                    high_unit(7 + n)
            for n in range(4):
                act.wait_ge(*full(f"ssq{n}", NL))
                nc.scalar.activation(qk_rstd[:, n, :], bank(f"ssq{n}")[:, :], ACT.Ln, bias=tb("rms_eps"), scale=1.0 / HD
                                     ).then_inc(*took(f"ssq{n}"))
            for n in range(4):
                act.wait_ge(*read(f"ssq{n}", NL))
                nc.scalar.activation(qk_rstd[:, n, :], qk_rstd[:, n, :], ACT.Exp, scale=-0.5).then_inc(qk_rstd_ok, 1)

            def copy_values(t):
                act.wait_ge(*full(f"v{t}", NL))
                nc.scalar.copy(st_v[:, t, :], bank(f"v{t}")[:, :]).then_inc(*took(f"v{t}"))

            copy_values(0)

            def soft_exps(heads):
                for h in heads:
                    act.wait_ge(*full(f"z{h}", NL))
                    ins = nc.scalar.activation(stW[:, h, :], bank(f"z{h}")[:, 0:3 * P], ACT.Abs)
                link(ins)
                for h in heads:
                    ins = nc.scalar.activation(stW[:, h, :], stW[:, h, :], ACT.Exp, scale=-1.0)
                link(ins)

            def soft_logs(heads):
                for h in heads:
                    nc.scalar.activation(stW[:, h, :], stW[:, h, :], ACT.Ln, bias=tb("one")).then_inc(log1pd, 1)

            def weight_part(h):
                act.wait_ge(*read(f"sfx{h}", NL))
                nc.scalar.activation(stW[:, h, :], stW[:, h, :], ACT.Exp).then_inc(wexp, 1)

            for h0 in range(0, ST_H, ST_GROUP):
                soft_exps(range(h0, h0 + ST_GROUP))
                for h in range(max(h0 - ST_GROUP, 0), h0):
                    weight_part(h)
                soft_logs(range(h0, h0 + ST_GROUP))
                if h0 == 0:
                    copy_values(1)
            for h in range(ST_H - ST_GROUP, ST_H):
                weight_part(h)
            for n in range(2):
                act.wait_ge(*full(f"att{n}", NL))
                nc.scalar.copy(XT[:, 2 * n:2 * n + 2, :], bank(f"att{n}")[:, :]).then_inc(*took(f"att{n}"))

            def high_chunk(s, n):
                act.wait_ge(up_in[s], n * 16)
                high_up(s, w_gate[s])

            act.wait_ge(lru_mix, 1)
            high_down(2, 0, down_in, 1)
            high_chunk(0, 1)
            high_chunk(1, 1)
            rms_rows_of(1)
            high_features("n2T", n2g)

            def chunk_step(m, s, first=False, more_up=True, more_down=True):
                c = 2 * m + s
                act.wait_ge(hid_ready, hidden(NL, c - 2))
                act.wait_ge(*full(f"ff{s}", NL, m))
                nc.scalar.activation(sig[s], bank(f"ff{s}")[:, :], ACT.Relu).then_inc(relu_done, 1)
                if more_up:
                    high_chunk(s, m + 2)
                if more_down:
                    if not first:
                        act.wait_ge(ff_used, c)
                    high_down(3 - s, 1 - s, down_in, m + s + 1)

            chunk_step(0, 0, first=True)
            with act.Fori(1, N_CHUNK // 2 - 1) as m:
                chunk_step(m - 1, 1)
                chunk_step(m, 0)
            chunk_step(N_CHUNK // 2 - 2, 1)
            chunk_step(N_CHUNK // 2 - 1, 0, more_up=False)
            chunk_step(N_CHUNK // 2 - 1, 1, more_up=False, more_down=False)

        @block.tensor
        def _(pe):
            def product(dst, pairs, first=True, last=True):
                for n, (lhsT, rhs) in enumerate(pairs):
                    ins = nc.tensor.matmul(dst, lhsT, rhs, start=first and n == 0, stop=last and n == len(pairs) - 1)
                return ins

            def features(w, cols, act_T=None):
                return [(w[:, k, cols], XT[:, k, :]) for k in range(KD)]

            def rows(w, cols, t):
                return [(XT[:, k, token(t)], w[:, k, cols]) for k in range(KD)]

            def split_features(slot, cols):
                parts = []
                for k in range(KD):
                    high, low = WH_up[slot][:, k, cols], WL_up[slot][:, k, cols]
                    parts += [(high, XTH[:, k, :]), (high, XTL[:, k, :]), (low, XTH[:, k, :])]
                return parts

            def split_product(dst, slot, cols, ready=None):
                parts = split_features(slot, cols)
                for k in range(KD):
                    if ready and k % 2 == 0:
                        ready(k // 2)
                    ins = product(dst, parts[3 * k:3 * k + 3], k == 0, k == KD - 1)
                return ins

            def split_down(slot, n, s, names, l, first, last):
                if first:
                    pe.wait_ge(*free(names[n], l))
                parts, cols = [], slice((n % 2) * 512, (n % 2 + 1) * 512)
                for c in range(2):
                    high, low = HIDH[s][:, c, token(n // 2)], HIDL[s][:, c, token(n // 2)]
                    parts += [(high, WH_dn[slot][:, c, cols]), (high, WL_dn[slot][:, c, cols]), (low, WH_dn[slot][:, c, cols])]
                ins = product(bank(names[n])[:, :], parts, first, last)
                if last:
                    ins.then_inc(*made(names[n]))
                return ins

            def transpose_rows(prefix, src, l, ready, n_ready):
                for t in range(T):
                    pe.wait_ge(ready, n_ready + (t + 1))
                    for n in range(4):
                        name = f"{prefix}{n}"
                        if t == 0:
                            pe.wait_ge(*free(name, l))
                        for k in (2 * n, 2 * n + 1):
                            c = (k % 2) * SEQ + t * P
                            ins = nc.tensor.transpose(bank(name)[:, c:c + P], src[:, t, k:D:KD], ident)
                        if t == T - 1:
                            ins.then_inc(*made(name))

            def transposes_read(prefix, l):
                for n in range(4):
                    pe.wait_ge(*read(f"{prefix}{n}", l))

            def tile_of(name, n, w=SEQ):
                return bank(name)[:, n * w:(n + 1) * w]

            def probs_T(name, h, p1, p0, l):
                job = f"{name}_pT{h}"
                pe.wait_ge(*free(job, l))
                pe.wait_ge(normed[name], l * 6 + h + 1)
                nc.tensor.transpose(bank(job)[:, 0:P], p0[:, h, :], ident)
                nc.tensor.transpose(bank(job)[:, P:2 * P], p1[:, h, 0:P], ident)
                nc.tensor.transpose(bank(job)[:, 2 * P:3 * P], p1[:, h, P:2 * P], ident).then_inc(*made(job))

            def weighted_values(dst, v0, v1, pT):
                nc.tensor.matmul(dst, v0, pT[:, 0:2 * P], start=True, stop=False)
                return nc.tensor.matmul(dst[:, P:2 * P], v1, pT[:, 2 * P:3 * P], start=False, stop=True)

            def key_major_scores(dst, kT, qT):
                nc.tensor.matmul(dst[:, 0:2 * P], kT[:, 0:P], qT, start=True, stop=True)
                return nc.tensor.matmul(dst[:, 2 * P:3 * P], kT[:, P:2 * P], qT[:, P:2 * P], start=True, stop=True)

            def scores(name, kq, l):
                for n in range(3):
                    job = f"{name}_s1_{n}"
                    pe.wait_ge(*free(job, l))
                    for h in (2 * n, 2 * n + 1):
                        kT, qT = kq(h)
                        if name == "swa" and n == 1 and h == 3:
                            ins.then_inc(rows_turned, 1)
                            pe.wait_ge(rows_turned, l * 2 + 1)
                        ins = nc.tensor.matmul(tile_of(job, h % 2), qT[:, P:2 * P], kT, start=True, stop=True)
                    ins.then_inc(*made(job))
                for n, heads in enumerate((range(4), range(4, 6))):
                    job = f"{name}_s0_{n}"
                    pe.wait_ge(*free(job, l))
                    for h in heads:
                        kT, qT = kq(h)
                        if name == "swa" and h == 3:
                            ins.then_inc(rows_turned, 1)
                            pe.wait_ge(rows_turned, l * 2 + 2)
                        ins = nc.tensor.matmul(tile_of(job, h % 4, P), qT[:, 0:P], kT[:, 0:P], start=True, stop=True)
                    ins.then_inc(*made(job))

            pe.wait_ge(ident_in, 16)
            with pe.Fori(0, NL) as l:
                transpose_rows("xT", X, l, x_ready, l * T)
                transposes_read("xT", l)
                pe.wait_ge(wlat_in, (l + 1) * 16)
                for n in range(5):
                    if n == 2:
                        pe.wait_ge(wlat2_in, (l + 1) * 16)
                    job = f"lat{n // 2}"
                    if n % 2 == 0:
                        pe.wait_ge(*free(job, l))
                    ins = product(tile_of(job, n % 2), features(w_lat, slice(n * P, (n + 1) * P)))
                    if n % 2 == 1:
                        ins.then_inc(*made(job))
                product(bank("lat2")[NOPE:DQ, SEQ:2 * SEQ], features(w_lat, slice(5 * P, N_LAT))).then_inc(*made("lat2"))
                pe.wait_ge(wrqk_in, (l + 1) * 16)
                for n, job in enumerate(("ret_q", "ret_k")):
                    pe.wait_ge(*free(job, l))
                    for c in range(2):
                        ins = product(tile_of(job, c), features(w_rqk, slice((2 * n + c) * P, (2 * n + c + 1) * P)))
                    ins.then_inc(*made(job))
                pe.wait_ge(tab_in, 16)
                pe.wait_ge(*free("lat_ssq", l))
                pe.wait_ge(lat_squared, (l + 1) * 3)
                product(tile_of("lat_ssq", 0), [(ones, lat_sq[:, c, :]) for c in range(3)])
                product(tile_of("lat_ssq", 1), [(ones, lat_sq[:, c, :]) for c in (3, 4)]).then_inc(*made("lat_ssq"))
                pe.wait_ge(wswa_in, (l + 1) * 7 * 16)
                for n in range(4):
                    job = ("swa_q01", "swa_q01", "swa_q2k", "swa_q2k")[n]
                    if n % 2 == 0:
                        pe.wait_ge(*free(job, l))
                    ins = product(tile_of(job, n % 2), features(w_swa, slice(n * P, (n + 1) * P)))
                    if n % 2 == 1:
                        ins.then_inc(*made(job))
                pe.wait_ge(wrvg_in, (l + 1) * 16)
                for t in range(T):
                    pe.wait_ge(*free(f"ret_vg{t}", l))
                    product(bank(f"ret_vg{t}")[:, :], rows(w_rvg, slice(0, 512), t)).then_inc(*made(f"ret_vg{t}"))
                pe.wait_ge(*free("swa_v", l))
                for t in range(T):
                    ins = product(tile_of("swa_v", t, P), rows(w_swa, slice(C_SV - C_SQ, C_CQ - C_SQ), t))
                ins.then_inc(*made("swa_v"))
                for job, src, name in (("ret_q_swap", ret_qT, "ret_q"), ("ret_k_swap", ret_kT, "ret_k")):
                    pe.wait_ge(*free(job, l))
                    pe.wait_ge(*read(name, l))
                    nc.tensor.matmul(bank(job)[:, :], tb("swap_r"), src, start=True, stop=True).then_inc(*made(job))
                scores("swa", lambda h: (swa_kT[(h // 3) * HD:(h // 3 + 1) * HD, :],
                                         swa_qT[(h // 3) * HD:(h // 3 + 1) * HD, h % 3, :]), l)
                pe.wait_ge(wup_in, (l + 1) * 32)
                for n in range(3):
                    pe.wait_ge(*free(f"mla_q{n}", l))
                    pe.wait_ge(*read("lat2", l))
                    for h in (2 * n, 2 * n + 1):
                        ins = product(tile_of(f"mla_q{n}", h % 2)[0:DQ], [
                            (w_uq[:, c, h * DQ:(h + 1) * DQ], lat_n[:, c, :]) for c in range(3)])
                    ins.then_inc(*made(f"mla_q{n}"))
                for n in range(3):
                    pe.wait_ge(*free(f"mla_k{n}", l))
                    for h in (2 * n, 2 * n + 1):
                        ins = product(tile_of(f"mla_k{n}", h % 2)[0:NOPE], [
                            (w_ukv[:, c, h * P:h * P + NOPE], lat_n[:, 3 + c, :]) for c in range(2)])
                    ins.then_inc(*made(f"mla_k{n}"))
                for t in range(T):
                    pe.wait_ge(*free(f"mla_v{t}", l))
                    product(bank(f"mla_v{t}")[:, 0:384].rearrange("p (h d) -> p h d", d=MLA_VD), [
                        (lat_n[:, 3 + c, token(t)], w_ukv[:, c, :].rearrange("p (h d) -> p h d", d=P)[:, :, NOPE:P])
                        for c in range(2)]).then_inc(*made(f"mla_v{t}"))
                turn = slice(NOPE, DQ)
                for n in range(3):
                    pe.wait_ge(*free(f"mla_q_swap{n}", l))
                    nc.tensor.matmul(bank(f"mla_q_swap{n}")[:, :], tb("swap_m")[turn, :], mla_qT[turn, 2 * n:2 * n + 2, :],
                                     start=True, stop=True).then_inc(*made(f"mla_q_swap{n}"))
                pe.wait_ge(*free("mla_kr_swap", l))
                pe.wait_ge(kr_copied, l + 1)
                nc.tensor.matmul(bank("mla_kr_swap")[:, 0:SEQ], tb("swap_m")[turn, :], krT[turn, :],
                                 start=True, stop=True).then_inc(*made("mla_kr_swap"))
                pe.wait_ge(ret_roped, (l + 1) * 2)
                for h in range(RET_H):
                    job, part = f"ret_s{h}", slice((h % 2) * HD, (h % 2 + 1) * HD)
                    pe.wait_ge(*free(job, l))
                    key_major_scores(bank(job), ret_kT[part, h // 2, :], ret_qT[part, h // 2, :]).then_inc(*made(job))
                for h in range(RET_H):
                    pe.wait_ge(*read(f"ret_s{h}", l))
                ro = bank("ret_o")[:, :].rearrange("p (t h d) -> p t h d", t=T, h=RET_H)
                for h in range(RET_H):
                    v = ret_v[:, :, h * HD:(h + 1) * HD]
                    nc.tensor.matmul(ro[:, 0, h, :], ret_pT[:, h, 0:P], v[:, 0, :], start=True, stop=True)
                    nc.tensor.matmul(ro[:, 1, h, :], ret_pT[:, h, P:2 * P], v[:, 0, :], start=True, stop=False)
                    ins = nc.tensor.matmul(ro[:, 1, h, :], ret_pT[:, h, 2 * P:3 * P], v[:, 1, :], start=False, stop=True)
                ins.then_inc(*made("ret_o"))
                def attend(name, pT, value):
                    for h in range(6):
                        job = f"{name}_o{h // 4}"
                        if h % 4 == 0:
                            pe.wait_ge(*free(job, l))
                        pe.wait_ge(*read(f"{name}_pT{h}", l))
                        dst = tile_of(job, (h // 2) % 2)[(h % 2) * HD:(h % 2 + 1) * HD, :]
                        ins = weighted_values(dst, value(h, 0), value(h, 1), pT[:, h, :])
                        if h in (3, 5):
                            ins.then_inc(*made(job))

                for h in range(SWA_H):
                    probs_T("swa", h, swa_p1, swa_p0, l)
                pe.wait_ge(q_roped, l + 1)
                pe.wait_ge(k_roped, l + 2)
                scores("mla", lambda h: (mla_kT[0:DQ, h, :], mla_qT[0:DQ, h, :]), l)
                attend("swa", swa_pT, lambda h, t: swa_v[:, t, (h // 3) * HD:(h // 3 + 1) * HD])
                pe.wait_ge(*free("ret_oT", l))
                pe.wait_ge(ret_out, l + 1)
                rc = ret_c.rearrange("p (t h) d -> p t (h d)", t=T)
                for c in range(2):
                    for t in range(T):
                        ins = nc.tensor.transpose(bank("ret_oT")[:, c * SEQ + t * P:c * SEQ + (t + 1) * P],
                                                  rc[:, t, c * P:(c + 1) * P], ident)
                ins.then_inc(*made("ret_oT"))

                pe.wait_ge(wout_in, (l + 1) * 16)
                for job in ("ret_oT", "swa_o0", "swa_o1"):
                    pe.wait_ge(*read(job, l))

                def mix_part(n, chunks):
                    cols = slice((n % 2) * 512, (n % 2 + 1) * 512)
                    return product(bank(f"mix{n}")[:, :], [(XT[:, k, token(n // 2)], w_out[:, k, cols]) for k in chunks],
                                   chunks[0] == 0, chunks[-1] == KD - 1)

                for n in range(4):
                    pe.wait_ge(*free(f"mix{n}", l))
                    mix_part(n, range(C_MLA))
                for h in range(MLA_H):
                    probs_T("mla", h, mla_p1, mla_p0, l)
                attend("mla", mla_pT, lambda h, t: mla_v[:, t, h * MLA_VD:(h + 1) * MLA_VD])
                pe.wait_ge(wout2_in, (l + 1) * 16)
                for job in ("mla_o0", "mla_o1"):
                    pe.wait_ge(*read(job, l))
                for n in range(4):
                    mix_part(n, range(C_MLA, KD)).then_inc(*made(f"mix{n}"))
                transpose_rows("x1T", X, l, x1_ready, l * T)
                transposes_read("x1T", l)
                pe.wait_ge(router_in, 32)
                pe.wait_ge(*free("router", l))
                for t in range(T):
                    ins = product(tile_of("router", t, N_EXP), rows(router, slice(0, N_EXP), t))
                ins.then_inc(*made("router"))

                def ready(n):
                    pe.wait_ge(xt_low, l * 4 + n + 1)

                def expert_up(m, s, between=None):
                    for n, job in enumerate((f"gate{s}", f"up{s}")):
                        pe.wait_ge(low_made[n], unit(n, l, 2 * m + s))
                        pe.wait_ge(*free(job, l, m))
                        for c in range(2):
                            ins = split_product(tile_of(job, c), n, slice(c * P, (c + 1) * P),
                                                ready if between and n == 0 and c == 0 else None)
                        ins.then_inc(*made(job))
                        if between and n == 0:
                            between()

                def expert_down(m, s, first=False, last=False):
                    slot = 0 if last else 2
                    pe.wait_ge(low_made[slot], unit(slot, l, 2 * m + s + int(last)))
                    pe.wait_ge(hid_ready, hidden(l, 2 * m + s))
                    for n in range(4):
                        ins = split_down(slot, n, s, ("y0", "y1", "y2", "y3"), l, first, last)
                    if not last:
                        ins.then_inc(expert_used, 1)

                def gates_transposed():
                    pe.wait_ge(*free("gatesT", l))
                    pe.wait_ge(gates_ready, l + 1)
                    for t in range(T):
                        ins = nc.tensor.transpose(bank("gatesT")[0:N_EXP, token(t)], gates[:, t, :], ident)
                    ins.then_inc(*made("gatesT"))

                expert_up(0, 0, gates_transposed)
                expert_up(0, 1)
                expert_down(0, 0, first=True)
                with pe.Fori(1, N_EXP // 2) as m:
                    expert_up(m, 0)
                    expert_down(m - 1, 1)
                    expert_up(m, 1)
                    expert_down(m, 0)
                expert_down(N_EXP // 2 - 1, 1, last=True)

            l = NL
            transpose_rows("n1T", xn, l, rms_rows, 0)
            def unit_ready(u):
                pe.wait_ge(proj_low[u % 3], u // 3 + 1)

            def project(u, ready=None):
                job = PROJ_JOBS[u]
                unit_ready(u)
                pe.wait_ge(*free(job, l))
                for c in range(2):
                    for k in range(KD):
                        if ready and c == 0 and k % 2 == 0:
                            ready(k // 2)
                        high, low = (w[u % 3][:, k, c * P:(c + 1) * P] for w in (PH, PL))
                        ins = product(tile_of(job, c), [(high, XTH[:, k, :]), (high, XTL[:, k, :]), (low, XTH[:, k, :])],
                                      k == 0, k == KD - 1)
                ins.then_inc(*made(job))

            project(0, lambda n: pe.wait_ge(*read(f"n1T{n}", l)))
            for u in range(1, 5):
                project(u)
            pe.wait_ge(bd_in, 64)
            pe.wait_ge(conv_done, 1)
            for n, pre in enumerate(("rg", "ig")):
                for c in range(4):
                    job = f"{pre}{c // 2}"
                    if c % 2 == 0:
                        pe.wait_ge(*free(job, l))
                    ins = nc.tensor.matmul(tile_of(job, c % 2), w_bd[:, n, c, :], conv_u[:, c, :], start=True, stop=True)
                    if c % 2 == 1:
                        ins.then_inc(*made(job))
            for u in range(5, 8):
                project(u)

            def head_sums(n):
                pe.wait_ge(*free(f"ssq{n}", l))
                pe.wait_ge(qk_squared, n + 1)
                nc.tensor.matmul(bank(f"ssq{n}")[:, :], tb("half_ones"), qk_sq[:, n, :], start=True, stop=True
                                 ).then_inc(*made(f"ssq{n}"))

            def values(t):
                pe.wait_ge(*free(f"v{t}", l))
                for u in (8, 9):
                    unit_ready(u)
                    ins = product(tile_of(f"v{t}", u - 8), [pair for k in range(KD) for pair in (
                        (XTH[:, k, token(t)], PH[u % 3][:, k, :]), (XTH[:, k, token(t)], PL[u % 3][:, k, :]),
                        (XTL[:, k, token(t)], PH[u % 3][:, k, :]))])
                ins.then_inc(*made(f"v{t}"))

            for n in range(4):
                head_sums(n)
            values(0)

            def z_of(h):
                job, part = f"z{h}", slice((h % 2) * HD, (h % 2 + 1) * HD)
                pe.wait_ge(*free(job, l))
                key_major_scores(bank(job), st_kT[part, h // 2, :], st_qT[part, h // 2, :]).then_inc(*made(job))

            def suffix_of(h):
                job = f"sfx{h}"
                pe.wait_ge(*free(job, l))
                pe.wait_ge(masked_sp, h + 1)
                later, s = tb("later"), stS[:, h, :]
                nc.tensor.matmul(bank(job)[:, 0:2 * P], later, s[:, 0:2 * P], start=True, stop=False)
                nc.tensor.matmul(bank(job)[:, P:2 * P], ones, s[:, 2 * P:3 * P], start=False, stop=True)
                nc.tensor.matmul(bank(job)[:, 2 * P:3 * P], later, s[:, 2 * P:3 * P], start=True, stop=True
                                 ).then_inc(*made(job))

            for name in ("q0", "q1", "k0", "k1"):
                pe.wait_ge(*read(name, l))
            def out_part(n, chunks, first, last):
                ins = product(bank(f"out{n}")[:, :], [
                    ((XT if k < 4 else lruH)[:, k % 4, token(n // 2)], w_out[:, k, (n % 2) * 512:(n % 2 + 1) * 512])
                    for k in chunks], first, last)
                if last:
                    ins.then_inc(*made(f"out{n}"))

            for h in range(ST_GROUP):
                z_of(h)
            values(1)
            for h in range(ST_GROUP):
                suffix_of(h)
                z_of(h + ST_GROUP)
            pe.wait_ge(wout_in, (NL + 1) * 16)
            pe.wait_ge(wout2_in, (NL + 1) * 16)
            pe.wait_ge(lru_mix, 1)
            for n in range(2):
                pe.wait_ge(*free(f"out{n}", l))
                out_part(n, range(4, KD), True, False)
            for h in range(ST_GROUP, ST_H):
                suffix_of(h)
            for h in range(ST_H):
                job = f"att{h // 4}"
                if h % 4 == 0:
                    pe.wait_ge(*free(job, l))
                pe.wait_ge(w_masked, h + 1)
                dst = tile_of(job, (h // 2) % 2)[(h % 2) * HD:(h % 2 + 1) * HD, :]
                ins = weighted_values(dst, st_v[:, 0, h * HD:(h + 1) * HD], st_v[:, 1, h * HD:(h + 1) * HD], stW[:, h, :])
                if h % 4 == 3:
                    ins.then_inc(*made(job))
            pe.wait_ge(*read("att0", l))
            pe.wait_ge(*read("att1", l))
            for n in range(2):
                out_part(n, range(4), False, True)
            for n in range(2, 4):
                pe.wait_ge(*free(f"out{n}", l))
                out_part(n, range(KD), True, True)
            transpose_rows("n2T", xn, l, rms_rows, T)

            def chunk_up(m, s, ready=None):
                pe.wait_ge(low_made[s], unit(s, NL, m))
                pe.wait_ge(*free(f"ff{s}", l, m))
                for c in range(2):
                    ins = split_product(tile_of(f"ff{s}", c), s, slice(c * P, (c + 1) * P), ready if c == 0 else None)
                ins.then_inc(*made(f"ff{s}"))

            def chunk_down(m, s, first=False, last=False):
                pe.wait_ge(low_made[2 + s], unit(2 + s, NL, m))
                pe.wait_ge(hid_ready, hidden(NL, 2 * m + s))
                for n in range(4):
                    ins = split_down(2 + s, n, s, ("m0", "m1", "m2", "m3"), l, first, last)
                if not last:
                    ins.then_inc(ff_used, 1)

            chunk_up(0, 0, lambda n: pe.wait_ge(*read(f"n2T{n}", l)))
            chunk_up(0, 1)
            chunk_down(0, 0, first=True)
            with pe.Fori(1, N_CHUNK // 2) as m:
                chunk_up(m, 0)
                chunk_down(m - 1, 1)
                chunk_up(m, 1)
                chunk_down(m, 0)
            chunk_down(N_CHUNK // 2 - 1, 1, last=True)

        @block.vector
        def _(dve):
            v = nc.vector

            def layer_norm(l, link, which, jobs, loaded, done):
                for t in range(T):
                    for half in range(2):
                        job = jobs[2 * t + half]
                        part = X[:, t, half * 512:(half + 1) * 512]
                        dve.wait_ge(*full(job, l))
                        v.scalar_tensor_tensor(part, part, ALPHA, bank(job)[:, :], ALU.mult, ALU.add).then_inc(*took(job))
                        dve.wait_ge(*read(job, l))
                        ins = v.bn_stats(st6[:, t, half * 6:(half + 1) * 6], part)
                    link(ins)
                    v.memset(lrs[:, t, :], 0.0)
                    v.bn_aggr(mv2[:, t, :], st6[:, t, :]).then_inc(ln_var, 1)
                    n = l * 4 + (which - 1) * T + t + 1
                    dve.wait_ge(loaded, (l + 1) * 32)
                    dve.wait_ge(ln_var, n)
                    v.scalar_tensor_tensor(X[:, t, :], X[:, t, :], mv2[:, t, 0:1], LNB[:, 0, :], ALU.subtract, ALU.mult
                                           ).then_inc(ln_centred, 1)
                    dve.wait_ge(ln_rooted, n)
                    v.reciprocal(lrs[:, t, :], lrs[:, t, :]).then_inc(ln_rstd, 1)
                    dve.wait_ge(ln_centred, n)
                    dve.wait_ge(ln_rstd, n)
                    v.scalar_tensor_tensor(X[:, t, :], X[:, t, :], lrs[:, t, 0:1], LNB[:, 1, :], ALU.mult, ALU.add
                                           ).then_inc(done, 1)

            def softmax_scores(name, l, link, p1, p0, mask, scale):
                for n in range(3):
                    job = f"{name}_s1_{n}"
                    dve.wait_ge(*full(job, l))
                    v.tensor_tensor(p1[:, 2 * n:2 * n + 2, :], bank(job)[:, :].rearrange("p (a b) -> p a b", b=SEQ),
                                    spread(mask, 1, [P, 2, SEQ]), ALU.add).then_inc(*took(job))
                for n, (h0, k) in enumerate(((0, 4), (4, 2))):
                    job = f"{name}_s0_{n}"
                    dve.wait_ge(*full(job, l))
                    v.tensor_tensor(p0[:, h0:h0 + k, :], bank(job)[:, 0:k * P].rearrange("p (a b) -> p a b", b=P),
                                    spread(mask[:, P:2 * P], 1, [P, k, P]), ALU.add).then_inc(*took(job))
                for job in (f"{name}_s1_{n}" for n in range(3)):
                    dve.wait_ge(*read(job, l))
                v.tensor_reduce(mx[name][:, 1, :], p1, AX.X, ALU.max)
                dve.wait_ge(*read(f"{name}_s0_0", l))
                dve.wait_ge(*read(f"{name}_s0_1", l))
                link(v.tensor_reduce(mx[name][:, 0, :], p0, AX.X, ALU.max))
                if name == "swa":
                    dve.wait_ge(norms_in, (l + 1) * 64)
                    sinks = spread(sink_b, 1, [P, T, SWA_H])
                    link(v.tensor_tensor(mx[name], mx[name], sinks, ALU.max))
                    v.tensor_tensor(sk_e, sinks, mx[name], ALU.subtract)
                v.tensor_scalar(nmx[name], mx[name], -scale, None, ALU.mult).then_inc(maxed[name], 1)

            def softmax_norm(name, l, link, p1, p0):
                dve.wait_ge(expd[name], l + 1)
                if name == "swa":
                    link(v.tensor_tensor(psm[name], psm[name], sk_e, ALU.add))
                link(v.reciprocal(rin[name], psm[name]))
                for h in range(6):
                    v.tensor_scalar(p0[:, h, :], p0[:, h, :], rin[name][:, 0, h:h + 1], None, ALU.mult)
                    v.tensor_scalar(p1[:, h, :], p1[:, h, :], rin[name][:, 1, h:h + 1], None, ALU.mult
                                    ).then_inc(normed[name], 1)

            def evacuate(job, dst, l, rows=slice(0, P), w=512):
                dve.wait_ge(*full(job, l))
                v.tensor_copy(dst, bank(job)[rows, 0:w]).then_inc(*took(job))

            def low_of_xt(l):
                for n in range(4):
                    dve.wait_ge(xt_high, l * 4 + n + 1)
                    part = slice(2 * n, 2 * n + 2)
                    v.tensor_tensor(XTL[:, part, :], XT[:, part, :], XTH[:, part, :].bitcast(F32), ALU.subtract
                                    ).then_inc(xt_low, 1)

            def split_hidden(link, s):
                h = sig[s].rearrange("p (a b) -> p a b", b=SEQ)
                link(v.tensor_copy(HIDH[s][:, :, :], h))
                v.tensor_tensor(HIDL[s][:, :, :], h, HIDH[s][:, :, :].bitcast(F32), ALU.subtract).then_inc(hid_ready, 1)

            def low_down(slot, s, n):
                dve.wait_ge(high_made[slot], n)
                v.tensor_tensor(WL_dn[slot], w_dn[s], WH_dn[slot].bitcast(F32), ALU.subtract).then_inc(low_made[slot], 1)

            for b in range(8):
                v.memset(marks[:, b:b + 1], 0.0).then_inc(psum_read[b], 1)
            v.memset(marks[:, 9 + T:10 + T], 0.0).then_inc(hid_ready, 1)
            for t in range(T):
                dve.wait_ge(x_in[t], 16)
                v.memset(marks[:, 8 + t:9 + t], 0.0).then_inc(x_ready, 1)
            with dve.Fori(0, NL) as l:
                link = Link(dve, dve_link, l * DVE_LINKS)
                for n in (1, 3):
                    evacuate(f"xT{n}", XT[:, 2 * n:2 * n + 2, :], l)
                turn = slice(NOPE, DQ)
                dve.wait_ge(tab_in, 16)
                dve.wait_ge(norms_in, (l + 1) * 64)
                dve.wait_ge(rstd_ready, l + 1)
                for n in range(5):
                    job, kv = f"lat{n // 2}", n >= 3
                    gain = kvn_g[:, n - 3:n - 2] if kv else qn_g[:, n:n + 1]
                    ins = v.scalar_tensor_tensor(lat_n[:, n, :], bank(job)[:, (n % 2) * SEQ:(n % 2 + 1) * SEQ], gain,
                                                 lat_rstd[:, int(kv), :], ALU.mult, ALU.mult)
                    if n in (1, 3, 4):
                        ins.then_inc(*took(job))
                for n, (dst, job) in enumerate(((ret_qT, "ret_q_swap"), (ret_kT, "ret_k_swap"))):
                    dve.wait_ge(ret_cos, l * 2 + n + 1)
                    dve.wait_ge(*full(job, l))
                    v.tensor_tensor(dst, bank(job)[:, :].rearrange("p (a b) -> p a b", b=SEQ),
                                    spread(tb("sin_r"), 1, [P, 2, SEQ]), ALU.mult).then_inc(*took(job))
                    dve.wait_ge(*read(job, l))
                    v.tensor_tensor(dst, dst, rope_r[:, 2 * n:2 * n + 2, :], ALU.add).then_inc(ret_roped, 1)
                softmax_scores("swa", l, link, swa_p1, swa_p0, tb("mask_swa"), 1.0)
                for n in range(3):
                    evacuate(f"mla_k{n}", mla_kT[0:NOPE, 2 * n:2 * n + 2, :], l, slice(0, NOPE))
                for n in range(3):
                    job = f"mla_q_swap{n}"
                    dve.wait_ge(*full(job, l))
                    v.tensor_tensor(rope_m[turn, 2 * n:2 * n + 2, :], bank(job)[turn, :].rearrange("p (a b) -> p a b", b=SEQ),
                                    spread(tb("sin_m")[turn], 1, [ROPE_D, 2, SEQ]), ALU.mult).then_inc(*took(job))
                dve.wait_ge(*full("mla_kr_swap", l))
                v.tensor_tensor(kr_sin[turn], bank("mla_kr_swap")[turn, 0:SEQ], tb("sin_m")[turn], ALU.mult
                                ).then_inc(*took("mla_kr_swap"))
                for h in range(RET_H):
                    dve.wait_ge(*full(f"ret_s{h}", l))
                    v.tensor_tensor(ret_pT[:, h, :], bank(f"ret_s{h}")[:, 0:3 * P], decay[:, h, :], ALU.mult
                                    ).then_inc(*took(f"ret_s{h}"))
                softmax_norm("swa", l, link, swa_p1, swa_p0)
                dve.wait_ge(*full("ret_o", l))
                ro = bank("ret_o")[:, :].rearrange("p (g d) -> p g d", d=HD)
                link(v.tensor_reduce(gmu, ro, AX.X, ALU.add))
                link(v.tensor_scalar(gmu, gmu, 1.0 / HD, None, ALU.mult))
                v.tensor_tensor(ret_c, ro, spread(gmu, 2, [P, 8, HD]), ALU.subtract).then_inc(*took("ret_o"))
                for h in (1, 3, 5):
                    evacuate(f"swa_pT{h}", swa_pT[:, h, :], l, w=3 * P)
                dve.wait_ge(gn_squared, l + 1)
                v.tensor_reduce(gvar, ret_sq, AX.X, ALU.add).then_inc(gn_var, 1)
                dve.wait_ge(gn_rooted, l + 1)
                link(v.reciprocal(grs, grs))
                dve.wait_ge(ret_gate_w, l + 1)
                link(v.tensor_tensor(ret_c, ret_c, spread(grs, 2, [P, 8, HD]), ALU.mult))
                v.tensor_tensor(ret_c, ret_c, ret_g.rearrange("p t (h d) -> p (t h) d", d=HD), ALU.mult
                                ).then_inc(ret_out, 1)
                softmax_scores("mla", l, link, mla_p1, mla_p0, tb("mask_mla"), DQ ** -0.5)
                softmax_norm("mla", l, link, mla_p1, mla_p0)
                for h in (1, 3, 5):
                    evacuate(f"mla_pT{h}", mla_pT[:, h, :], l, w=3 * P)
                layer_norm(l, link, 1, ("mix0", "mix1", "mix2", "mix3"), ln1_in, x1_ready)
                for n in (1, 3):
                    evacuate(f"x1T{n}", XT[:, 2 * n:2 * n + 2, :], l)
                low_of_xt(l)
                dve.wait_ge(router_in, 32)
                dve.wait_ge(*read("router", l))
                link(v.tensor_scalar(sc, sc, 1.0, None, ALU.add))
                link(v.reciprocal(sc, sc))
                link(v.tensor_tensor(bi.rearrange("p (t g) e -> p t (g e)", t=T), sc.rearrange("p (t e) -> p t e", t=T),
                                     spread(rbias, 1, [P, T, N_EXP]), ALU.add))
                v.tensor_tensor(pr[:, :, 0:3], bi[:, :, 0:3], bi[:, :, 1:4], ALU.add)
                v.tensor_tensor(pr[:, :, 3:5], bi[:, :, 0:2], bi[:, :, 2:4], ALU.add)
                link(v.tensor_tensor(pr[:, :, 5:6], bi[:, :, 0:1], bi[:, :, 3:4], ALU.add))
                link(v.tensor_reduce(gs, pr, AX.X, ALU.max))

                def beaten_by(val, n, buf1, buf2, dst, limit):
                    other, own = spread(val, 2, [P, n, 4, 4]), spread(val, 3, [P, n, 4, 4])
                    v.tensor_tensor(buf1, other, own, ALU.is_gt)
                    link(v.tensor_tensor(buf2, other, own, ALU.is_equal))
                    link(v.tensor_tensor(buf2, buf2, spread(tie, 1, [P, n, 4, 4]), ALU.mult))
                    link(v.tensor_tensor(buf1, buf1, buf2, ALU.add))
                    link(v.tensor_reduce(dst, buf1, AX.X, ALU.add))
                    link(v.tensor_scalar(dst, dst, limit, None, ALU.is_lt))

                beaten_by(gs.rearrange("p (t g) -> p t g", t=T), T, g1, g2, gsel.rearrange("p (t g) -> p t g", t=T), 0.5)
                beaten_by(bi, 8, c1, c2, esel, 1.5)
                link(v.tensor_tensor(esel, esel, spread(gsel, 2, [P, 8, 4]), ALU.mult))
                link(v.tensor_tensor(esel, esel, sc.rearrange("p (g e) -> p g e", e=4), ALU.mult))
                e2 = esel.rearrange("p (t g) e -> p t (g e)", t=T)
                link(v.tensor_reduce(gden, e2, AX.X, ALU.add))
                link(v.reciprocal(gden, gden))
                v.tensor_tensor(gates, e2, spread(gden, 2, [P, T, N_EXP]), ALU.mult).then_inc(gates_ready, 1)
                dve.wait_ge(gates_in, (l + 1) * 16)
                v.memset(gden, 0.0)

                def expert_step(moe, m, s, last=False):
                    dve.wait_ge(*read(f"gate{s}", l, m))
                    act_s = sig[s].rearrange("p (a b) -> p a b", b=SEQ)
                    moe(v.tensor_tensor(act_s, act_s, gates_b[:, bass.ds(2 * m + s, 1), :].to_broadcast([P, 2, SEQ]), ALU.mult))
                    dve.wait_ge(*full(f"up{s}", l, m))
                    v.tensor_tensor(sig[s], sig[s], bank(f"up{s}")[:, :], ALU.mult).then_inc(*took(f"up{s}"))
                    dve.wait_ge(*read(f"up{s}", l, m))
                    split_hidden(moe, s)
                    slot = 0 if last else 2
                    low_down(slot, s, unit(slot, l, 2 * m + s + int(last)))

                def pair(m, last=False):
                    moe = Link(dve, dve_moe, (l * (N_EXP // 2) + m) * (2 * MOE_LINKS))
                    expert_step(moe, m, 0)
                    expert_step(moe, m, 1, last)
                    assert moe.n == 2 * MOE_LINKS

                with dve.Fori(0, N_EXP // 2 - 1) as m:
                    pair(m)
                pair(N_EXP // 2 - 1, last=True)
                layer_norm(l, link, 2, ("y0", "y1", "y2", "y3"), ln2_in, x_ready)
                assert link.n == DVE_LINKS, link.n

            l = NL
            link = Link(dve, dve_fin)
            dve.wait_ge(final_in, 14 * 16)
            v.memset(xl_pad[:, :, 0:CONV - 1], 0.0).then_inc(pad_zero, 1)
            v.tensor_scalar(qg2, qg2, HD ** -0.5, None, ALU.mult)
            v.scalar_tensor_tensor(sp_e, lam, -1.0, lam, ALU.mult, ALU.min).then_inc(consts2, 1)

            def scale_rows(n):
                for t in range(T):
                    dve.wait_ge(rms_rooted, n * T + t + 1)
                    r = rss[:, t:t + 1]
                    v.reciprocal(r, r).then_inc(rms_rstd, 1)
                    dve.wait_ge(rms_rstd, n * T + t + 1)
                    v.tensor_scalar(xn[:, t, :], X[:, t, :], rss[:, t:t + 1], None, ALU.mult).then_inc(rms_rows, 1)

            def low_features(prefix, gain, which):
                for n in range(4):
                    dve.wait_ge(xt_high, (NL + which) * 4 + n + 1)
                    for k in (2 * n, 2 * n + 1):
                        ins = v.scalar_tensor_tensor(XTL[:, k, :], bank(f"{prefix}{n}")[:, (k % 2) * SEQ:(k % 2 + 1) * SEQ],
                                                     gain[:, k:k + 1], XTH[:, k, :].bitcast(F32), ALU.mult, ALU.subtract)
                    ins.then_inc(*took(f"{prefix}{n}"))

            scale_rows(0)
            low_features("n1T", n1g, 0)
            dve.wait_ge(*read("xl0", l))
            dve.wait_ge(*read("xl1", l))
            for k in range(CONV):
                for c in range(4):
                    src, tap = xl_pad[:, c, k:k + SEQ], cw[:, k, c:c + 1]
                    if k == 0:
                        ins = v.tensor_scalar(conv_u[:, c, :], src, tap, cb[:, c:c + 1], ALU.mult, ALU.add)
                    else:
                        ins = v.scalar_tensor_tensor(conv_u[:, c, :], src, tap, conv_u[:, c, :], ALU.mult, ALU.add)
                if k < CONV - 1:
                    link(ins)
            ins.then_inc(conv_done, 1)
            dve.wait_ge(*read("gl0", l))
            dve.wait_ge(*read("gl1", l))
            link(v.tensor_tensor(gel, glT, glT, ALU.mult))
            link(v.tensor_scalar(gel, gel, 0.044715, 1.0, ALU.mult, ALU.add))
            v.tensor_tensor(gel, gel, glT, ALU.mult).then_inc(gel_in, 1)
            dve.wait_ge(sp_lam, 1)
            link(v.tensor_scalar(sp_s, sp_e, 2.0, None, ALU.add))
            link(v.reciprocal(sp_s, sp_s))
            link(v.tensor_tensor(sp_s, sp_s, sp_e, ALU.mult))
            link(v.tensor_tensor(sp_s2, sp_s, sp_s, ALU.mult))
            link(v.tensor_scalar(sp_p, sp_s2, 1.0 / 15, None, ALU.mult))
            for n in (13, 11, 9, 7, 5, 3):
                link(v.scalar_tensor_tensor(sp_p, sp_p, 1.0 / n, sp_s2, ALU.add, ALU.mult))
            link(v.scalar_tensor_tensor(sp_p, sp_p, 1.0, sp_s, ALU.add, ALU.mult))
            link(v.tensor_scalar(sp_s, lam, -1.0, 0.0, ALU.mult, ALU.max))
            link(v.scalar_tensor_tensor(sp_p, sp_p, 2.0, sp_s, ALU.mult, ALU.add))
            link(v.tensor_scalar(sp_p, sp_p, -LRU_C, None, ALU.mult))
            dve.wait_ge(*read("rg0", l))
            dve.wait_ge(*read("rg1", l))
            for c in range(4):
                ins = v.tensor_scalar(rgT[:, c, :], rgT[:, c, :], sp_p[:, c:c + 1], None, ALU.mult)
            ins.then_inc(lru_la, 1)
            dve.wait_ge(*read("ig0", l))
            dve.wait_ge(*read("ig1", l))
            v.tensor_tensor(igT, igT, conv_u, ALU.mult)
            dve.wait_ge(gel_t, 1)
            link(v.tensor_scalar(gel, gel, 0.5, 0.5, ALU.mult, ALU.add))
            link(v.tensor_tensor(gel, gel, glT, ALU.mult))
            dve.wait_ge(lru_at, 1)
            link(v.tensor_tensor(rgT, lruA, lruA, ALU.mult))
            v.scalar_tensor_tensor(lruT, rgT, 1.0, lruT, ALU.add, ALU.mult).then_inc(lru_m2, 1)
            dve.wait_ge(lru_sq, 1)
            link(v.tensor_tensor(igT, igT, lruT, ALU.mult))
            for c in range(4):
                ins = v.tensor_tensor_scan(lruH[:, c, :], lruA[:, c, :], igT[:, c, :], 0.0, ALU.mult, ALU.add)
            link(ins)
            v.tensor_tensor(lruH, lruH, gel, ALU.mult).then_inc(lru_mix, 1)
            dve.wait_ge(consts2, 1)
            for n, (dst, gain, job) in enumerate(((st_qT, qg2, "q0"), (st_qT, qg2, "q1"), (st_kT, kg2, "k0"), (st_kT, kg2, "k1"))):
                dve.wait_ge(qk_rstd_ok, n + 1)
                v.scalar_tensor_tensor(dst[:, 2 * (n % 2):2 * (n % 2) + 2, :].rearrange("p a b -> p (a b)"), bank(job)[:, :],
                                       gain[:, 0:1], qk_rstd[:, n, :], ALU.mult, ALU.mult).then_inc(*took(job))

            def soft_parts(h):
                z = bank(f"z{h}")[:, 0:3 * P]
                dve.wait_ge(log1pd, h + 1)
                v.scalar_tensor_tensor(stS[:, h, :], z, 0.0, stW[:, h, :], ALU.max, ALU.add).then_inc(soft, 1)
                v.scalar_tensor_tensor(stL[:, h, :], z, 0.0, stW[:, h, :], ALU.min, ALU.subtract).then_inc(*took(f"z{h}"))

            def log_weights(h):
                dve.wait_ge(*read(f"z{h}", l))
                dve.wait_ge(*full(f"sfx{h}", l))
                v.tensor_tensor(stW[:, h, :], stL[:, h, :], bank(f"sfx{h}")[:, 0:3 * P], ALU.subtract
                                ).then_inc(*took(f"sfx{h}"))

            dve.wait_ge(proj_low[0], 4)
            for h in range(ST_H):
                soft_parts(h)
                if h % ST_GROUP > 0:
                    log_weights(h - 1)
                if h % ST_GROUP == ST_GROUP - 1:
                    log_weights(h)
            def add_rows(prefix):
                for n in range(4):
                    job, part = f"{prefix}{n}", X[:, n // 2, (n % 2) * 512:(n % 2 + 1) * 512]
                    dve.wait_ge(*full(job, l))
                    v.tensor_tensor(part, part, bank(job)[:, :], ALU.add).then_inc(*took(job))

            add_rows("out")
            scale_rows(1)
            low_features("n2T", n2g, 1)
            with dve.Fori(0, N_CHUNK // 2) as m:
                mlp = Link(dve, dve_moe, NL * N_EXP * MOE_LINKS + 2 * m)
                for s in range(2):
                    dve.wait_ge(relu_done, 2 * m + s + 1)
                    v.tensor_tensor(sig[s], sig[s], bank(f"ff{s}")[:, :], ALU.mult).then_inc(*took(f"ff{s}"))
                    dve.wait_ge(*read(f"ff{s}", l, m))
                    split_hidden(mlp, s)
                    low_down(2 + s, s, unit(2 + s, NL, m))
            add_rows("m")

    return nc


INPUTS = ["x", "w_in", "ret_gn_w", "swa_sinks", "mla_q_norm_w", "mla_kv_norm_w", "mla_w_uq", "mla_w_ukv", "w_out",
          "ln1_g", "ln1_b", "router_w", "router_bias", "exp_w_gate_up", "exp_w_down", "ln2_g", "ln2_b", "norm1_g_2",
          "w_in_2", "conv_w_2", "conv_b_2", "w_rg_2", "b_rg_2", "w_ig_2", "b_ig_2", "lru_lambda_2", "q_norm_g_2",
          "k_norm_g_2", "w_out_2", "norm2_g_2", "w_up_2", "w_down_2"]


def kernel(**inputs):
    import concourse.bacc as bacc
    from concourse.bass_utils import run_bass_kernel_spmd

    nc = bacc.Bacc("TRN2", target_bir_lowering=False, num_devices=1)
    arrays = {f"in_{n}": np.ascontiguousarray(inputs[n]) for n in INPUTS}
    arrays["in_tables"] = np.ascontiguousarray(np.concatenate(list(tables().values()), axis=1).astype(np.float32))
    aps = {n[3:]: nc.dram_tensor(n, v.shape, mybir.dt.from_np(v.dtype), kind="ExternalInput").ap() for n, v in arrays.items()}
    out = nc.dram_tensor("out", (1, SEQ, D), F32, kind="ExternalOutput").ap()
    build(nc, aps, out)
    r = run_bass_kernel_spmd(nc, [arrays], core_ids=[0])
    return r.results[0]["out"]
```
